# Optimizing a Trainium2 kernel written in Bass

```python
import math
import jax, jax.numpy as jnp
from jax import lax
import numpy as np

D_MODEL = 1024
BATCH = 1
SEQ = 256
DEPTH = 2

N_META = 16
CHUNK = 128
PAD = CHUNK
ROPE_THETA = 10000.0
EPS = 1e-6
LB_FLOOR = 1e-30
RET_HEADS = 4
RET_DK = 128
RET_DV = 256
HG_HEADS = 8
HG_DK = 128
HG_DV = 128
DA_HEADS = 8
DA_DH = 64
DA_DV = 2 * DA_DH
N_BRANCH = 3
BRANCH_WIDTH = 1024
D_FF = 2816
CONV_W = 3
Q_BLOCK = 128
MASK_VALUE = -1e30
RET_QK_W = RET_HEADS * RET_DK
RET_V_W = RET_HEADS * RET_DV
HG_K_W = HG_HEADS * HG_DK
HG_V_W = HG_HEADS * HG_DV
DA_QK_W = DA_HEADS * 2 * DA_DH
DA_V_W = DA_HEADS * DA_DV
IN_SPLITS = (RET_QK_W, RET_QK_W, RET_V_W, RET_V_W, HG_K_W, HG_K_W, HG_V_W, HG_V_W, DA_QK_W, DA_QK_W, DA_V_W, N_BRANCH * D_MODEL)
IN_WIDTH = sum(IN_SPLITS)
F32 = jnp.float32


def _rms(x):
    xf = x.astype(F32)
    return xf * lax.rsqrt(jnp.mean(xf * xf, axis=-1, keepdims=True) + EPS)

def rms_norm(x, g):
    return (_rms(x) * g.astype(F32)).astype(x.dtype)

def rope(x, pos):
    d = x.shape[-1]
    inv = ROPE_THETA ** (-jnp.arange(0, d, 2, dtype=F32) / d)
    ang = pos.astype(F32)[:, None] * inv[None, :]
    cos = jnp.cos(ang)[None, :, None, :]
    sin = jnp.sin(ang)[None, :, None, :]
    x1, x2 = jnp.split(x, 2, axis=-1)
    return jnp.concatenate([x1 * cos - x2 * sin, x2 * cos + x1 * sin], axis=-1)

def to_chunks(x):
    b, l = x.shape[:2]
    return jnp.swapaxes(x.reshape((b, l // CHUNK, CHUNK) + x.shape[2:]), 0, 1)

def from_chunks(x):
    n, b = x.shape[:2]
    return jnp.swapaxes(x, 0, 1).reshape((b, n * CHUNK) + x.shape[3:])

def retention(q, k, v, gate, valid, pos):
    b = q.shape[0]
    q = rope(q, pos)
    k = jnp.where(valid[None, :, None, None], rope(k, pos) * RET_DK ** -0.5, 0.0)
    log_g = jnp.log1p(-jnp.exp2(-5.0 - jnp.arange(RET_HEADS, dtype=F32)))
    idx = jnp.arange(CHUNK, dtype=F32)
    gap = idx[:, None] - idx[None, :]
    intra = jnp.where(gap >= 0, jnp.exp(log_g[:, None, None] * jnp.maximum(gap, 0.0)), 0.0)
    q_dec = jnp.exp(log_g[:, None] * (idx[None, :] + 1.0))
    k_dec = jnp.exp(log_g[:, None] * (CHUNK - 1.0 - idx[None, :]))
    c_dec = jnp.exp(log_g * CHUNK)[None, :, None, None]

    def step(state, xs):
        qc, kc, vc = xs
        s = jnp.einsum('bqhd,bkhd->bhqk', qc, kc) * intra[None]
        o = jnp.einsum('bhqk,bkhe->bqhe', s, vc) + jnp.einsum('bqhd,hq,bhde->bqhe', qc, q_dec, state)
        state = c_dec * state + jnp.einsum('bkhd,hk,bkhe->bhde', kc, k_dec, vc)
        return state, o

    s0 = jnp.zeros((b, RET_HEADS, RET_DK, RET_DV), F32)
    _, o = lax.scan(step, s0, (to_chunks(q), to_chunks(k), to_chunks(v)))
    o = _rms(from_chunks(o)) * jax.nn.silu(gate)
    return o.reshape(b, -1, RET_V_W)

def hgrn2(q, f_logit, inp, gate, lb, valid):
    b = q.shape[0]
    lbh = lb.reshape(HG_HEADS, HG_DK)
    log_f = jnp.logaddexp(jnp.log(jnp.maximum(lbh, LB_FLOOR)), jnp.log1p(-lbh) + jax.nn.log_sigmoid(f_logit))
    k = (1.0 - lbh) * jax.nn.sigmoid(-f_logit)
    v = jnp.where(valid[None, :, None, None], inp, 0.0)
    causal = jnp.tril(jnp.ones((CHUNK, CHUNK), bool))[None, :, :, None, None]

    def step(state, xs):
        qc, kc, vc, lfc = xs
        cb = jnp.cumsum(lfc, axis=1)
        rel = cb[:, :, None] - cb[:, None, :]
        dec = jnp.where(causal, jnp.exp(jnp.where(causal, rel, 0.0)), 0.0)
        a = jnp.einsum('bqhd,bkhd,bqkhd->bhqk', qc, kc, dec)
        o = jnp.einsum('bhqk,bkhe->bqhe', a, vc) + jnp.einsum('bqhd,bhde->bqhe', qc * jnp.exp(cb), state)
        c_end = cb[:, -1]
        state = jnp.exp(c_end)[..., None] * state + jnp.einsum('bkhd,bkhe->bhde', kc * jnp.exp(c_end[:, None] - cb), vc)
        return state, o

    s0 = jnp.zeros((b, HG_HEADS, HG_DK, HG_DV), F32)
    _, o = lax.scan(step, s0, (to_chunks(q), to_chunks(k), to_chunks(v), to_chunks(log_f)))
    o = _rms(from_chunks(o)) * jax.nn.silu(gate)
    return o.reshape(b, -1, HG_V_W)

def diff_attention(q, k, v, lam_p, subln_g, lambda_init, valid, pos):
    b, l = q.shape[:2]
    lp = lam_p.astype(F32)
    lam = jnp.exp(jnp.sum(lp[0] * lp[1])) - jnp.exp(jnp.sum(lp[2] * lp[3])) + lambda_init
    q = rope(q.reshape(b, l, 2 * DA_HEADS, DA_DH), pos).reshape(b, l, DA_HEADS, 2, DA_DH) * DA_DH ** -0.5
    k = rope(k.reshape(b, l, 2 * DA_HEADS, DA_DH), pos).reshape(b, l, DA_HEADS, 2, DA_DH)
    n_blk = l // Q_BLOCK
    q_blocks = jnp.swapaxes(q.reshape(b, n_blk, Q_BLOCK, DA_HEADS, 2, DA_DH), 0, 1)
    key_pos = jnp.arange(l)

    def block(args):
        qb, bi = args
        s = jnp.einsum('bqhmd,bkhmd->bhmqk', qb, k)
        q_pos = bi * Q_BLOCK + jnp.arange(Q_BLOCK)
        allowed = (key_pos[None, :] <= q_pos[:, None]) & valid[None, :]
        p = jax.nn.softmax(jnp.where(allowed, s, MASK_VALUE), axis=-1)
        w = p[:, :, 0] - lam * p[:, :, 1]
        return jnp.einsum('bhqk,bkhe->bqhe', w, v)

    o = lax.map(block, (q_blocks, jnp.arange(n_blk)))
    o = jnp.swapaxes(o, 0, 1).reshape(b, l, DA_HEADS, DA_DV)
    o = _rms(o) * subln_g.astype(F32) * (1.0 - lambda_init)
    return o.reshape(b, l, DA_V_W)

def mixer(hn, w_in, w_branch, w_out, lb, lam_p, subln_g, lambda_init, valid, pos):
    b, l, _ = hn.shape
    proj = (hn @ w_in).astype(F32)
    offs = [int(o) for o in np.cumsum(IN_SPLITS)[:-1]]
    rq, rk, rv, rg, hq, hf, hi, hg, dq, dk, dv, mg = jnp.split(proj, offs, axis=-1)
    o_ret = retention(rq.reshape(b, l, RET_HEADS, RET_DK), rk.reshape(b, l, RET_HEADS, RET_DK),
                      rv.reshape(b, l, RET_HEADS, RET_DV), rg.reshape(b, l, RET_HEADS, RET_DV), valid, pos)
    o_hg = hgrn2(hq.reshape(b, l, HG_HEADS, HG_DK), hf.reshape(b, l, HG_HEADS, HG_DK),
                 hi.reshape(b, l, HG_HEADS, HG_DV), hg.reshape(b, l, HG_HEADS, HG_DV), lb, valid)
    o_da = diff_attention(dq.reshape(b, l, DA_HEADS, 2, DA_DH), dk.reshape(b, l, DA_HEADS, 2, DA_DH),
                          dv.reshape(b, l, DA_HEADS, DA_DV), lam_p, subln_g, lambda_init, valid, pos)
    branches = jnp.stack([o_ret, o_hg, o_da], axis=2)
    y_b = jnp.einsum('blnc,ncd->blnd', branches, w_branch.astype(F32))
    gates = jax.nn.sigmoid(mg.reshape(b, l, N_BRANCH, D_MODEL))
    y = jnp.sum(gates * y_b, axis=2)
    return y.astype(hn.dtype) @ w_out

def conv_ffn(hn, w_ffn_in, conv_w, conv_b, w_ffn_out, valid):
    l = hn.shape[1]
    u = jnp.where(valid[None, :, None], hn @ w_ffn_in, 0.0)
    up = jnp.pad(u, ((0, 0), (CONV_W - 1, 0), (0, 0)))
    c = conv_b + sum(conv_w[j] * up[:, j:j + l] for j in range(CONV_W))
    gate, val = jnp.split(c, 2, axis=-1)
    return (jax.nn.silu(gate) * val) @ w_ffn_out

def first_inputs(seed: int = 0) -> dict:
    key = jax.random.key(seed)
    ks = jax.random.split(key, 16)

    def nrm(k, shape, scale):
        return jax.random.normal(k, shape, F32) * scale

    return {
        'x': nrm(ks[0], (BATCH, SEQ, D_MODEL), 1.0),
        'meta': nrm(ks[1], (N_META, D_MODEL), 1.0),
        'norm_mix_g': 1.0 + nrm(ks[2], (DEPTH, D_MODEL), 0.02),
        'w_in': nrm(ks[3], (DEPTH, D_MODEL, IN_WIDTH), D_MODEL ** -0.5),
        'w_branch': nrm(ks[4], (DEPTH, N_BRANCH, BRANCH_WIDTH, D_MODEL), BRANCH_WIDTH ** -0.5),
        'w_out': nrm(ks[5], (DEPTH, D_MODEL, D_MODEL), D_MODEL ** -0.5),
        'hg_lb': nrm(ks[6], (DEPTH, HG_K_W), 0.1),
        'da_lambda': nrm(ks[7], (DEPTH, 4, DA_DH), 0.1),
        'da_subln_g': 1.0 + nrm(ks[8], (DEPTH, DA_DV), 0.02),
        'norm_ffn_g': 1.0 + nrm(ks[9], (DEPTH, D_MODEL), 0.02),
        'w_ffn_in': nrm(ks[10], (DEPTH, D_MODEL, 2 * D_FF), D_MODEL ** -0.5),
        'ffn_conv_w': nrm(ks[11], (DEPTH, CONV_W, 2 * D_FF), CONV_W ** -0.5),
        'ffn_conv_b': nrm(ks[12], (DEPTH, 2 * D_FF), 0.01),
        'w_ffn_out': nrm(ks[13], (DEPTH, D_FF, D_MODEL), D_FF ** -0.5),
        'norm_final_g': 1.0 + nrm(ks[14], (D_MODEL,), 0.02),
    }

def first_block(x, meta, norm_mix_g, w_in, w_branch, w_out, hg_lb, da_lambda, da_subln_g,
              norm_ffn_g, w_ffn_in, ffn_conv_w, ffn_conv_b, w_ffn_out, norm_final_g):
    b, s, d = x.shape
    l = PAD + s
    h = jnp.concatenate([jnp.zeros((b, PAD - N_META, d), x.dtype),
                         jnp.broadcast_to(meta[None].astype(x.dtype), (b, N_META, d)), x], axis=1)
    t = jnp.arange(l)
    valid = t >= PAD - N_META
    pos = t - (PAD - N_META)
    lb_soft = jax.nn.softmax(hg_lb.astype(F32), axis=0)
    lbs = jnp.cumsum(lb_soft, axis=0) - lb_soft[0]
    for li in range(DEPTH):
        lambda_init = 0.8 - 0.6 * math.exp(-0.3 * li)
        h = h + mixer(rms_norm(h, norm_mix_g[li]), w_in[li], w_branch[li], w_out[li], lbs[li],
                      da_lambda[li], da_subln_g[li], lambda_init, valid, pos)
        h = h + conv_ffn(rms_norm(h, norm_ffn_g[li]), w_ffn_in[li], ffn_conv_w[li], ffn_conv_b[li],
                         w_ffn_out[li], valid)
    h = rms_norm(h, norm_final_g)
    return h[:, PAD:]


MLA_HEADS = 4
MLA_Q_RANK = 256
MLA_KV_RANK = 128
MLA_NOPE = 64
MLA_ROPE = 32
MLA_V = 64
CONV_WIDTH = 256
CONV_K = 3
DSA_HEADS = 4
DSA_HEAD_DIM = 64
IDX_HEADS = 8
IDX_DIM = 32
DSA_TOPK_MAX = 256
GLA_HEADS = 4
GLA_DK = 32
GLA_DV = 64
GLA_GATE_RANK = 16
GLA_TAU = 16.0
GLA_CHUNK = 64
N_BRANCH_2 = 4
BRANCH_WIDTH_2 = 256
D_FF_2 = ((8 * D_MODEL + 3 * 256 - 1) // (3 * 256)) * 256
NEG = -1e30

IN_SIZES = (
    MLA_Q_RANK, MLA_KV_RANK, MLA_ROPE,
    CONV_WIDTH, CONV_WIDTH, CONV_WIDTH,
    DSA_HEADS * DSA_HEAD_DIM, DSA_HEAD_DIM, DSA_HEAD_DIM,
    IDX_HEADS * IDX_DIM, IDX_DIM, IDX_HEADS,
    GLA_HEADS * GLA_DK, GLA_HEADS * GLA_DK, GLA_HEADS * GLA_DV,
    GLA_GATE_RANK, GLA_HEADS * GLA_DV,
    N_BRANCH_2 * D_MODEL,
)
IN_TOTAL = sum(IN_SIZES)


def rmsnorm(x, g):
    x32 = x.astype(jnp.float32)
    y = x32 * lax.rsqrt(jnp.mean(x32 * x32, axis=-1, keepdims=True) + EPS)
    return (y * g.astype(jnp.float32)).astype(x.dtype)

def apply_rope(x, positions):
    half = x.shape[-1] // 2
    inv_freq = ROPE_THETA ** (-jnp.arange(half, dtype=jnp.float32) / half)
    ang = positions.astype(jnp.float32)[:, :, None, None] * inv_freq
    cos, sin = jnp.cos(ang), jnp.sin(ang)
    x32 = x.astype(jnp.float32)
    x1, x2 = x32[..., :half], x32[..., half:]
    return jnp.concatenate([x1 * cos - x2 * sin, x1 * sin + x2 * cos], axis=-1).astype(x.dtype)

def to_blocks(a):
    b, s = a.shape[:2]
    return jnp.moveaxis(a.reshape((b, s // Q_BLOCK, Q_BLOCK) + a.shape[2:]), 1, 0)

def from_blocks(a):
    nb, b, qb = a.shape[:3]
    return jnp.moveaxis(a, 0, 1).reshape((b, nb * qb) + a.shape[3:])

def causal_block_attention(q, k, v, scale):
    s_len = k.shape[1]
    key_pos = jnp.arange(s_len)

    def one_block(args):
        qb, start = args
        qpos = start + jnp.arange(Q_BLOCK)
        s = jnp.einsum('bqhd,bkhd->bhqk', qb, k).astype(jnp.float32) * scale
        s = jnp.where(key_pos[None, :] <= qpos[:, None], s, NEG)
        p = jax.nn.softmax(s, axis=-1).astype(v.dtype)
        return jnp.einsum('bhqk,bkhd->bqhd', p, v)

    o = lax.map(one_block, (to_blocks(q), jnp.arange(s_len // Q_BLOCK) * Q_BLOCK))
    return from_blocks(o)

def mla_branch(cq, ckv, krope, positions, q_norm_g, w_q_up, kv_norm_g, w_kv_up):
    b, s, _ = cq.shape
    q = (rmsnorm(cq, q_norm_g) @ w_q_up).reshape(b, s, MLA_HEADS, MLA_NOPE + MLA_ROPE)
    q = jnp.concatenate([q[..., :MLA_NOPE], apply_rope(q[..., MLA_NOPE:], positions)], axis=-1)
    kv = (rmsnorm(ckv, kv_norm_g) @ w_kv_up).reshape(b, s, MLA_HEADS, MLA_NOPE + MLA_V)
    k_rope = apply_rope(krope[:, :, None, :], positions)
    k = jnp.concatenate([kv[..., :MLA_NOPE], jnp.broadcast_to(k_rope, (b, s, MLA_HEADS, MLA_ROPE))], axis=-1)
    v = kv[..., MLA_NOPE:]
    o = causal_block_attention(q, k, v, (MLA_NOPE + MLA_ROPE) ** -0.5)
    return o.reshape(b, s, MLA_HEADS * MLA_V)

def shortconv_branch(cb, cc, cx, conv_w):
    u = cc * cx
    y = lax.conv_general_dilated(
        u, conv_w[:, None, :], window_strides=(1,), padding=[(CONV_K - 1, 0)],
        dimension_numbers=('NWC', 'WIO', 'NWC'), feature_group_count=CONV_WIDTH)
    return cb * y

def dsa_branch(dq, dk, dv, iq, ik, iw):
    b, s, _ = dq.shape
    topk = min(DSA_TOPK_MAX, s // 4)
    q = dq.reshape(b, s, DSA_HEADS, DSA_HEAD_DIM)
    q_idx = iq.reshape(b, s, IDX_HEADS, IDX_DIM)
    key_pos = jnp.arange(s)
    gather = jax.vmap(lambda a, i: a[i])

    def one_block(args):
        qb, qib, wb, start = args
        qpos = start + jnp.arange(Q_BLOCK)
        rel = jax.nn.relu(jnp.einsum('bqhd,bsd->bqhs', qib, ik).astype(jnp.float32) * IDX_DIM ** -0.5)
        score = jnp.einsum('bqh,bqhs->bqs', wb.astype(jnp.float32) * IDX_HEADS ** -0.5, rel)
        score = jnp.where(key_pos[None, None, :] <= qpos[None, :, None], score, NEG)
        _, idx = lax.top_k(score, topk)
        valid = idx <= qpos[None, :, None]
        k_sel = gather(dk, idx)
        v_sel = gather(dv, idx)
        att = jnp.einsum('bqhd,bqkd->bqhk', qb, k_sel).astype(jnp.float32) * DSA_HEAD_DIM ** -0.5
        att = jnp.where(valid[:, :, None, :], att, NEG)
        p = jax.nn.softmax(att, axis=-1).astype(dv.dtype)
        return jnp.einsum('bqhk,bqkd->bqhd', p, v_sel)

    o = lax.map(one_block, (to_blocks(q), to_blocks(q_idx), to_blocks(iw), jnp.arange(s // Q_BLOCK) * Q_BLOCK))
    return from_blocks(o).reshape(b, s, DSA_HEADS * DSA_HEAD_DIM)

def gla_branch(gq, gk, gv, glr, gr, w_gate_up, b_gate, norm_g):
    b, s, _ = gq.shape
    nc = s // GLA_CHUNK
    f32 = jnp.float32

    def chunks(a, d):
        return a.astype(f32).reshape(b, nc, GLA_CHUNK, GLA_HEADS, d).transpose(1, 0, 3, 2, 4)

    q = chunks(gq, GLA_DK) * GLA_DK ** -0.5
    k = chunks(gk, GLA_DK)
    v = chunks(gv, GLA_DV)
    log_alpha = jax.nn.log_sigmoid((glr @ w_gate_up + b_gate).astype(f32)) / GLA_TAU
    g = chunks(log_alpha, GLA_DK)
    causal = jnp.tril(jnp.ones((GLA_CHUNK, GLA_CHUNK), dtype=bool))

    def step(state, inp):
        qc, kc, vc, gc = inp
        cum = lax.cumsum(gc, axis=2)
        o_inter = jnp.einsum('bhik,bhkv->bhiv', qc * jnp.exp(cum), state)
        decay = jnp.exp(jnp.where(causal[:, :, None], cum[:, :, :, None, :] - cum[:, :, None, :, :], NEG))
        attn = jnp.einsum('bhik,bhjk,bhijk->bhij', qc, kc, decay)
        o_intra = jnp.einsum('bhij,bhjv->bhiv', attn, vc)
        last = cum[:, :, -1:, :]
        state = jnp.exp(last[:, :, 0, :])[..., None] * state + jnp.einsum('bhjk,bhjv->bhkv', kc * jnp.exp(last - cum), vc)
        return state, o_inter + o_intra

    state0 = jnp.zeros((b, GLA_HEADS, GLA_DK, GLA_DV), f32)
    _, o = lax.scan(step, state0, (q, k, v, g))
    o = o.transpose(1, 0, 3, 2, 4).reshape(b, s, GLA_HEADS, GLA_DV)
    o = rmsnorm(o, norm_g).astype(gr.dtype).reshape(b, s, GLA_HEADS * GLA_DV)
    return jax.nn.silu(gr) * o

def second_inputs(seed: int = 0) -> dict:
    key = jax.random.key(seed)
    ks = jax.random.split(key, 20)
    f32 = jnp.float32

    def nrm(k, shape, scale):
        return jax.random.normal(k, shape, f32) * scale

    def gain(k, shape):
        return 1.0 + 0.05 * jax.random.normal(k, shape, f32)

    return {
        'x': nrm(ks[0], (BATCH, SEQ, D_MODEL), 1.0),
        'positions': jnp.broadcast_to(jnp.arange(SEQ, dtype=jnp.int32)[None, :], (BATCH, SEQ)),
        'attn_norm_g': gain(ks[1], (DEPTH, D_MODEL)),
        'w_in': nrm(ks[2], (DEPTH, D_MODEL, IN_TOTAL), D_MODEL ** -0.5),
        'mla_q_norm_g': gain(ks[3], (DEPTH, MLA_Q_RANK)),
        'mla_w_q_up': nrm(ks[4], (DEPTH, MLA_Q_RANK, MLA_HEADS * (MLA_NOPE + MLA_ROPE)), MLA_Q_RANK ** -0.5),
        'mla_kv_norm_g': gain(ks[5], (DEPTH, MLA_KV_RANK)),
        'mla_w_kv_up': nrm(ks[6], (DEPTH, MLA_KV_RANK, MLA_HEADS * (MLA_NOPE + MLA_V)), MLA_KV_RANK ** -0.5),
        'conv_w': nrm(ks[7], (DEPTH, CONV_K, CONV_WIDTH), CONV_K ** -0.5),
        'gla_w_gate_up': nrm(ks[8], (DEPTH, GLA_GATE_RANK, GLA_HEADS * GLA_DK), GLA_GATE_RANK ** -0.5),
        'gla_b_gate': nrm(ks[9], (DEPTH, GLA_HEADS * GLA_DK), 0.1),
        'gla_norm_g': gain(ks[10], (DEPTH, GLA_DV)),
        'w_branch': nrm(ks[11], (DEPTH, N_BRANCH_2, BRANCH_WIDTH_2, D_MODEL), BRANCH_WIDTH_2 ** -0.5),
        'w_out': nrm(ks[12], (DEPTH, D_MODEL, D_MODEL), D_MODEL ** -0.5),
        'ffn_norm_g': gain(ks[13], (DEPTH, D_MODEL)),
        'w_ffn_gate': nrm(ks[14], (DEPTH, D_MODEL, D_FF_2), D_MODEL ** -0.5),
        'w_ffn_up': nrm(ks[15], (DEPTH, D_MODEL, D_FF_2), D_MODEL ** -0.5),
        'w_ffn_down': nrm(ks[16], (DEPTH, D_FF_2, D_MODEL), D_FF_2 ** -0.5),
        'final_norm_g': gain(ks[17], (D_MODEL,)),
    }

def second_block(x, positions, attn_norm_g, w_in, mla_q_norm_g, mla_w_q_up, mla_kv_norm_g, mla_w_kv_up,
              conv_w, gla_w_gate_up, gla_b_gate, gla_norm_g, w_branch, w_out, ffn_norm_g,
              w_ffn_gate, w_ffn_up, w_ffn_down, final_norm_g):
    b, s, d = x.shape
    split_points = [int(p) for p in np.cumsum(IN_SIZES)[:-1]]
    for l in range(DEPTH):
        h = rmsnorm(x, attn_norm_g[l])
        (cq, ckv, krope, cb, cc, cx, dq, dk, dv, iq, ik, iw,
         gq, gk, gv, glr, gr, gate_pre) = jnp.split(h @ w_in[l], split_points, axis=-1)

        o_mla = mla_branch(cq, ckv, krope, positions, mla_q_norm_g[l], mla_w_q_up[l],
                           mla_kv_norm_g[l], mla_w_kv_up[l])
        o_conv = shortconv_branch(cb, cc, cx, conv_w[l])
        o_dsa = dsa_branch(dq, dk, dv, iq, ik, iw)
        o_gla = gla_branch(gq, gk, gv, glr, gr, gla_w_gate_up[l], gla_b_gate[l], gla_norm_g[l])

        gates = jax.nn.sigmoid(gate_pre).reshape(b, s, N_BRANCH_2, d)
        branches = (o_mla, o_conv, o_dsa, o_gla)
        merged = gates[:, :, 0, :] * (branches[0] @ w_branch[l, 0])
        for n in range(1, N_BRANCH_2):
            merged = merged + gates[:, :, n, :] * (branches[n] @ w_branch[l, n])
        x = x + merged @ w_out[l]

        h2 = rmsnorm(x, ffn_norm_g[l])
        x = x + (jax.nn.silu(h2 @ w_ffn_gate[l]) * (h2 @ w_ffn_up[l])) @ w_ffn_down[l]
    return rmsnorm(x, final_norm_g)


def setup_inputs(seed=0):
    out = dict(first_inputs(seed))
    for name, value in second_inputs(seed + 1).items():
        if name != "x":
            out[name + "_2"] = value
    return out


def reference(
    x, meta, norm_mix_g, w_in, w_branch, w_out, hg_lb, da_lambda, da_subln_g, norm_ffn_g,
    w_ffn_in, ffn_conv_w, ffn_conv_b, w_ffn_out, norm_final_g, positions_2, attn_norm_g_2,
    w_in_2, mla_q_norm_g_2, mla_w_q_up_2, mla_kv_norm_g_2, mla_w_kv_up_2, conv_w_2,
    gla_w_gate_up_2, gla_b_gate_2, gla_norm_g_2, w_branch_2, w_out_2, ffn_norm_g_2,
    w_ffn_gate_2, w_ffn_up_2, w_ffn_down_2, final_norm_g_2,
):
    x = first_block(
        x, meta, norm_mix_g, w_in, w_branch, w_out, hg_lb, da_lambda, da_subln_g, norm_ffn_g,
        w_ffn_in, ffn_conv_w, ffn_conv_b, w_ffn_out, norm_final_g,
    )
    return second_block(
        x, positions_2, attn_norm_g_2, w_in_2, mla_q_norm_g_2, mla_w_q_up_2, mla_kv_norm_g_2,
        mla_w_kv_up_2, conv_w_2, gla_w_gate_up_2, gla_b_gate_2, gla_norm_g_2, w_branch_2,
        w_out_2, ffn_norm_g_2, w_ffn_gate_2, w_ffn_up_2, w_ffn_down_2, final_norm_g_2,
    )


_drawn_inputs = setup_inputs


def setup_inputs(seed=0):
    import zlib

    import numpy as np

    out = dict(_drawn_inputs(seed))
    spreads = {}
    factors = {'mla_q_norm_g_2': 6.956, 'mla_kv_norm_g_2': 3.991, 'gla_b_gate_2': 2.868}
    for name, (base, spread) in spreads.items():
        noise = np.random.default_rng([zlib.crc32(name.encode()), seed]).standard_normal(out[name].shape)
        drawn = base * np.exp(spread * noise) if base else spread * noise
        out[name] = __import__('jax').numpy.asarray(drawn.astype(out[name].dtype))
    for name, factor in factors.items():
        out[name] = (out[name] * factor).astype(out[name].dtype)
    return out
```

```python
from contextlib import ExitStack

import concourse.bass as bass
import numpy as np
from concourse import mybir

F32 = mybir.dt.float32
I32 = mybir.dt.int32
ALU = mybir.AluOpType
ACT = mybir.ActivationFunctionType
AXX = mybir.AxisListType.X

P = 128
DEPTH = 2
D_MODEL = 1024
KT = D_MODEL // P
N_META = 16
SEQ = 256
T1 = N_META + SEQ
T2 = SEQ
D_FF = 2816
FT = D_FF // P
EPS = 1e-6
NEG = -1e30
LB_FLOOR = 1e-30
THETA = 10000.0
SLAB = 32
RING = 3
RET_HEADS, HG_HEADS, DA_HEADS = 4, 8, 8
MLA_HEADS, MLA_QK, MLA_NOPE = 4, 96, 64
GLA_HEADS, GLA_DK = 4, 32
DSA_HEADS, IDX_HEADS, TOPK = 4, 8, 64
IN1 = dict(rq=0, rk=512, rv=1024, rg=2048, hq=3072, hf=4096, hi=5120, hg=6144, dq=7168, dk=8192, dv=9216, mg=10240)
IN2 = dict(cq=0, ckv=256, krope=384, cb=416, cc=672, cx=928, dq=1184, dk=1440, dv=1504, iq=1568, ik=1824, iw=1856,
           gq=1864, gk=1992, gv=2120, glr=2376, gr=2392, mg=2648)
LEVELS = [64, 32, 16, 8, 4, 2, 1]

TILES_HG = [("hq", h) for h in range(8)] + [("hf", h) for h in range(8)] + [("hi", h) for h in range(8)] \
    + [("hg", h) for h in range(8)]
TILES_RET = [("rq", h) for h in range(4)] + [("rk", h) for h in range(4)] + [("rv", h) for h in range(8)] \
    + [("rg", h) for h in range(8)]
TILES_DA = [("dq", h) for h in range(8)] + [("dk", h) for h in range(8)] + [("dv", h) for h in range(8)]
MERGE1 = [1, 0, 2]
MERGE2 = [1, 0, 3, 2]
BLOCKS1 = 13312 // P * KT + 3 * KT * KT + KT * KT + 2 * FT * KT + FT * KT
SLABS1 = -(-BLOCKS1 // (SLAB * RING)) * RING
HEAD2 = 7
BLOCKS2 = 4 * KT * (KT + 2) + KT * KT + 2 * FT * KT + FT * KT
SLABS2 = -(-(HEAD2 * SLAB + BLOCKS2) // (SLAB * RING)) * RING
WIDE2 = [0, 416, 928, None, 1440, 1864, 2376]

CONST = {}
_at = 0
for _name, _n in [("cosR", T1), ("sinR", T1), ("cosD", T1), ("sinD", T1), ("rotR", P), ("rotD", P), ("rotM", P),
                  ("retD", RET_HEADS * T1), ("lvl", 8 * P), ("causal", 3 * P), ("ident", P), ("ones", P),
                  ("ones64", P), ("restart", T1), ("invM", 1), ("eps", 1), ("one", 1)]:
    CONST[_name] = (_at, _n)
    _at += _n
NCONST = _at
PAR1 = {}
_at = 0
for _name, _n in [("gmix", KT), ("gffn", KT), ("cw", 3 * 2 * FT), ("cb", 2 * FT), ("sub", 1), ("nlam", 1), ("omlb", KT),
                  ("lbf", KT)]:
    PAR1[_name] = (_at, _n)
    _at += _n
NPAR1, NPAR1_IN = _at, PAR1["nlam"][0]
PAR2 = {}
_at = 0
for _name, _n in [("gatt", KT), ("gffn", KT), ("gq", 2), ("gkv", 1), ("cw", 6), ("bg", 1), ("ggla", 1)]:
    PAR2[_name] = (_at, _n)
    _at += _n
NPAR2 = _at


ROUND = 12582912.0
TWO_PI = [6.28125, 0.0019350051879882812, 3.0199157663446432e-07]
N_INPUTS = 9


def constants():
    c = np.zeros((P, NCONST), np.float32)

    def put(name, a):
        at, n = CONST[name]
        c[:a.shape[0], at:at + n] = a.reshape(a.shape[0], n)

    def angles(d, copies):
        inv = np.float32(THETA) ** (-np.arange(0, d, 2, dtype=np.float32) / np.float32(d))
        ang = (np.arange(T1, dtype=np.float32)[None, :] * inv.astype(np.float32)[:, None]).astype(np.float32)
        return np.tile(ang, (2 * copies, 1)).astype(np.float64)

    def rotation(d, starts):
        r = np.zeros((P, P))
        for s in starts:
            for i in range(d // 2):
                r[s + i + d // 2, s + i] = -1.0
                r[s + i, s + i + d // 2] = 1.0
        return r

    put("cosR", np.cos(angles(128, 1)))
    put("sinR", np.sin(angles(128, 1)))
    put("cosD", np.cos(angles(64, 2)))
    put("sinD", np.sin(angles(64, 2)))
    put("rotR", rotation(128, [0]))
    put("rotD", rotation(64, [0, 64]))
    put("rotM", rotation(32, [MLA_NOPE]))
    k, j = np.arange(P)[:, None], np.arange(T1)[None, :]
    dec = [np.where(j >= k, (1 - 2.0 ** (-5 - h)) ** np.maximum(j - k, 0), 0.0) * 128 ** -0.5 for h in range(RET_HEADS)]
    put("retD", np.stack(dec, 1))
    kk, qq = np.arange(P)[:, None], np.arange(P)[None, :]
    lv = [(kk // s % 2 == 0) & (qq // s == kk // s + 1) for s in LEVELS] + [kk == qq]
    put("lvl", np.stack(lv, 1).astype(np.float32))
    put("causal", np.where(np.arange(3 * P)[None, :] <= kk + 2 * P, 0.0, NEG))
    put("ident", np.eye(P))
    put("ones", np.ones((P, P)))
    put("ones64", (kk // 64 == qq // 64).astype(np.float32))
    put("restart", np.tile((np.arange(T1) % P != 0).astype(np.float32), (P, 1)))
    inv = np.zeros((P, 1), np.float32)
    inv[MLA_NOPE:MLA_QK, 0] = np.tile(np.float32(THETA) ** (-np.arange(16, dtype=np.float32) / np.float32(16)), 2)
    put("invM", inv)
    put("eps", np.full((P, 1), EPS))
    put("one", np.ones((P, 1)))
    return c


class Signal:

    def __init__(self, sem, known):
        self.sem, self.known, self.count = sem, known, 0

    def done(self, key=0, by=1):
        self.count += by
        self.known[key] = self.count
        return self.sem, by

    def upto(self, key=0):
        return self.sem, self.known.get(key, 1)


class Banks:

    def __init__(self, psum, full, free, known):
        self.psum, self.fulls, self.frees, self.known, self.n = psum, full, free, known, 0

    def take(self, pe, key):
        bank, use = self.n % 8, self.n // 8 + 1
        self.n += 1
        self.known[key] = (bank, use)
        if use > 1:
            pe.wait_ge(self.frees[bank], use - 1)
        return self.psum[:, bank, :]

    def full(self, key):
        bank, use = self.known.get(key, (0, 1))
        return self.fulls[bank], use

    def filled(self, key):
        return self.fulls[self.known[key][0]], 1

    def free(self, key):
        return self.frees[self.known.get(key, (0, 1))[0]], 1

    def of(self, key):
        return self.psum[:, self.known.get(key, (0, 1))[0], :]


def program(nc, x_meta, w1, par1, lb, lam, final1, w2, par2, positions, final2, consts, out, known):
    with ExitStack() as ctx:
        def sb(name, n, dt=F32):
            return ctx.enter_context(nc.sbuf_tensor(name, [P, n], dt))

        def sem(name):
            return ctx.enter_context(nc.semaphore(name))

        psum = ctx.enter_context(nc.psum_tensor("psum", [P, 8, 512], F32))
        x_sb = sb("x_sb", KT * T1)
        hn_sb = sb("hn_sb", KT * T1)
        ring = sb("ring", RING * SLAB * P)
        cst = sb("cst", NCONST)
        par1_sb = sb("par1_sb", DEPTH * NPAR1)
        cur = sb("cur", NPAR1)
        par2_sb = sb("par2_sb", DEPTH * NPAR2)
        fin_sb = sb("fin_sb", 2 * KT)
        small = sb("small", 96)
        tab_sb = sb("tab_sb", 2 * T2)
        pos_sb = sb("pos_sb", T2, I32)
        arena = sb("arena", 29912)

        def view(at, *shape):
            n = int(np.prod(shape))
            v = arena[:, at:at + n]
            if len(shape) == 2:
                v = v.rearrange("p (a b) -> p a b", b=shape[1])
            if len(shape) == 3:
                v = v.rearrange("p (a b c) -> p a b c", b=shape[1], c=shape[2])
            return v, at + n

        def const(name, shape=None):
            at, n = CONST[name]
            v = cst[:, at:at + n]
            return v if shape is None else v.rearrange("p (a b) -> p a b", b=shape)

        X1 = x_sb[:, :].rearrange("p (k t) -> p k t", t=T1)
        HN1 = hn_sb[:, :].rearrange("p (k t) -> p k t", t=T1)
        OUT2 = x_sb[:, 0:KT * T2].rearrange("p (k t) -> p k t", t=T2)
        HN2 = hn_sb[:, 0:KT * T2].rearrange("p (k t) -> p k t", t=T2)
        cosR, sinR, cosD, sinD = const("cosR"), const("sinR"), const("cosD"), const("sinD")
        rotR, rotD, rotM = const("rotR"), const("rotD"), const("rotM")
        ident, ones, ones64 = const("ident"), const("ones"), const("ones64")
        causal, restart, eps, one = const("causal"), const("restart"), const("eps"), const("one")
        retD, lvl = const("retD", T1), const("lvl", P)

        HQ, a = view(0, KT, T1)
        HK, a = view(a, KT, T1)
        HC, a = view(a, KT, T1)
        HG, a = view(a, KT, T1)
        RQ, a = view(a, 4, T1)
        RK, a = view(a, 4, T1)
        RG, a = view(a, KT, T1)
        DQ, a = view(a, KT, T1)
        DK, a = view(a, KT, T1)
        HV, a = view(a, 2, D_MODEL)
        RV, a = view(a, 2, D_MODEL)
        DV, a = view(a, 2, D_MODEL)
        V3, a = view(a, D_MODEL)
        Z, z_end = view(a, 9, T1)
        Y1, _ = view(a, KT, T1)
        a = z_end
        XS, a = view(a, 2, T1)
        SG, a = view(a, 2, T1)
        S0, a = view(a, T1)
        S1, a = view(a, P + N_META)
        S2, a = view(a, N_META)
        RS, a = view(a, T1)
        LT, _ = view(a, 8, P)
        SQ, a = view(a, 2, T1)
        TMP, a = view(a, 2, T1)
        e1_sb, a = view(a, KT)
        assert a <= 29912, a
        c0 = 2 * KT * T1
        SC = [view(c0, 2, P)[0], view(c0 + 256, 2, 2 * P)[0], view(c0 + 768, 2, T1)[0]]
        WA = [view(c0 + 1312, P)[0], view(c0 + 1440, 2 * P)[0], view(c0 + 1696, T1)[0]]
        FF, _ = view(0, FT, T1)
        CG, b = view(KT * T1 * 3, 2, T1)
        CV, b = view(b, 2, T1)
        VT = {"h": (HV, 0), "r": (RV, 32), "d": (DV, 64)}
        ROT = {"rq": (RQ, cosR, sinR, rotR), "rk": (RK, cosR, sinR, rotR),
               "dq": (DQ, cosD, sinD, rotD), "dk": (DK, cosD, sinD, rotD)}

        lb_sb, b = view(0, 2 * KT)
        lb_e, b = view(b, 2 * KT)
        lb_t, b = view(b, KT)
        lam_sb, b = view(b, DEPTH * 4 * 64)
        lam_t, b = view(b, DEPTH * 2 * 64)
        lam_e, b = view(b, DEPTH * 2)
        angs, b = view(b, 2 * T2)
        turns, b = view(b, T2)
        cosM, sinM = tab_sb[:, 0:T2], tab_sb[:, T2:2 * T2]

        X2, a = view(0, KT, T2)
        Y2, a = view(a, KT, T2)
        CQ, a = view(a, 2, T2)
        CKV, a = view(a, T2)
        KR, a = view(a, T2)
        QM, a = view(a, MLA_HEADS, T2)
        KM, a = view(a, MLA_HEADS, T2)
        VM, a = view(a, 2, MLA_HEADS * 64)
        OM, a = view(a, 2, T2)
        SB, a = view(a, 2, T2)
        SI, a = view(a, 2, T2)
        OC, a = view(a, 2, T2)
        QS, a = view(a, 2, T2)
        KS, a = view(a, T2)
        VS, a = view(a, 2, 64)
        OS, a = view(a, 2, T2)
        IQ, a = view(a, 2, T2)
        IK, a = view(a, T2)
        IW, a = view(a, 2, IDX_HEADS)
        REL, a = view(a, 2, 512)
        IS, a = view(a, 3 * P)
        BS, a = view(a, 3 * P)
        TOP, a = view(a, 8)
        GQ, a = view(a, T2)
        GK, a = view(a, T2)
        GC, a = view(a, T2)
        GE, a = view(a, T2)
        GV, a = view(a, 2, GLA_HEADS * 64)
        GL, a = view(a, T2)
        WG, a = view(a, P)
        GG, a = view(a, 2, T2)
        GO, a = view(a, 2, T2)
        Z2, a = view(a, 8, T2)
        SS, a = view(a, 2, 3 * P)
        LT2, _ = view(a, 8, P)
        SC2, a = view(a, 2, 3 * P)
        W2, a = view(a, 2, 3 * P)
        SQ2, a = view(a, 3, T2)
        SGM, a = view(a, 2, T2)
        TP2, a = view(a, 2, 2 * T2)
        FF2, a = view(a, FT, T2)
        assert a <= 29912, a

        def par(name, i=0):
            at = PAR1[name][0] + i
            return cur[:, at:at + 1]

        def parb(name, i=0):
            at = PAR2[name][0] + i
            return cur[:, at:at + 1]

        STAGED = [k for k in TILES_HG + TILES_RET + TILES_DA if k[0] in ("hi", "rv", "dv") or k[0] in ROT]
        s1_slot = {k: i % 2 for i, k in enumerate(STAGED)}

        slab_loaded = [sem(f"slab_loaded{i}") for i in range(RING)]
        slab_used = [sem(f"slab_used{i}") for i in range(RING)]
        bank_full = [sem(f"bank_full{i}") for i in range(8)]
        bank_free = [sem(f"bank_free{i}") for i in range(8)]
        inputs_in = sem("inputs_in")
        out_written = sem("out_written")
        layer_begin = sem("layer_begin")
        layer_end = sem("layer_end")
        pe_in, act_in, dve_in = sem("pe_in"), sem("act_in"), sem("dve_in")

        def signals(section, names):
            return {n: Signal(sem(section + "_" + n), known.setdefault((section, n), {})) for n in names.split()}

        def banks(section):
            return Banks(psum, bank_full, bank_free, known.setdefault((section, "banks"), {}))

        s0 = signals("start", "act dve")
        s1 = signals("one", "sq rs hn staged taken sig_f f_in lnf cum e1 sg gated zdiff zexp z att sqo normed "
                     "sco expd w tr y sigm conv ff x")
        s2 = signals("two", "sq rs hn evac cqn ckn krn qm km oc sg gated gz gez gl gcum zdiff zexp z att sqo normed "
                     "sc expd w tr o rel relu used y sigm sigf ff x srt small mlaw")
        sm = signals("middle", "sq rs x")
        se = signals("end", "sq rs x")
        b1, b2, bm, be = banks("one"), banks("two"), banks("middle"), banks("end")
        block = ctx.enter_context(nc.Block())

        @block.tensor
        def _(pe):
            stream = {"n": 0, "release": None, "layer": None, "first": 0, "per": 0}

            def slab_wait(k):
                pe.wait_ge(slab_loaded[k % RING], (stream["layer"] * stream["per"] + (stream["first"] + k // RING + 1)) * 16)

            def mm(out_, lhsT, rhs, first, last, done=None):
                i = nc.tensor.matmul(out_, lhsT=lhsT, rhs=rhs, start=first, stop=last)
                if done is not None:
                    i.then_inc(*done)
                elif stream["release"] is not None:
                    i.then_inc(slab_used[stream["release"]], 1)
                    stream["release"] = None

            def weight_block():
                n = stream["n"]
                k = n // SLAB
                if n % SLAB == 0:
                    if stream["release"] is not None:
                        pe.drain().then_inc(slab_used[stream["release"]], 1)
                        stream["release"] = None
                    slab_wait(k)
                at = (k % RING) * SLAB * P + (n % SLAB) * P
                stream["n"] = n + 1
                return ring[:, at:at + P]

            def through():
                if stream["n"] % SLAB == 0:
                    stream["release"] = (stream["n"] // SLAB - 1) % RING

            def product(b, key, rhs, tokens, begin=True, end=True, ready=None):
                ps = b.take(pe, key) if begin else b.of(key)
                for i, r in enumerate(rhs):
                    w = weight_block()
                    if ready is not None and ready[i] is not None:
                        pe.wait_ge(*ready[i])
                    final = end and i == len(rhs) - 1
                    mm(ps[:, 0:tokens], w, r, begin and i == 0, final, b.filled(key) if final else None)
                    through()

            def sum_squares(b, key, tiles, tokens, ready, mat=None):
                ps = b.take(pe, key)
                for i, r in enumerate(tiles):
                    pe.wait_ge(*ready[i])
                    final = i == len(tiles) - 1
                    mm(ps[:, 0:tokens], ones if mat is None else mat, r, i == 0, final, b.filled(key) if final else None)

            def scores(b, key, parts):
                ps = b.take(pe, key)
                for i, (rows, cols, lhsT, rhs) in enumerate(parts):
                    mm(ps[rows, cols], lhsT, rhs, True, True, b.filled(key) if i == len(parts) - 1 else None)

            def transposes(b, key, parts):
                ps = b.take(pe, key)
                for i, (rows, cols, src) in enumerate(parts):
                    t = nc.tensor.transpose(ps[rows, cols], src, ident[0:src.shape[0], 0:src.shape[0]])
                    if i == len(parts) - 1:
                        t.then_inc(*b.filled(key))

            def level_products(b, h, Zv, t, q, k):
                n = P if t < 2 else N_META
                levels = [0, 1, 2, 4, 5, 6, 7] if t < 2 else [4, 5, 6, 7]
                tok = slice(t * P, t * P + n)
                mats = [(Zv[:, z, tok], Zv[:, z, tok]) for z in levels] + [(k[:, tok], q[:, tok])]
                groups = [mats[:4], mats[4:]] if t < 2 else [mats]
                for g, group in enumerate(groups):
                    scores(b, ("lv", h, t, g), [(slice(0, n), slice(i * n, i * n + n), l, r) for i, (l, r) in enumerate(group)])

            def values_times_weights(b, key, V, base, cols, rows=slice(0, P), more=True):
                ps = b.take(pe, key) if more is True else b.of(key)
                mm(ps[rows, 0:T1], V[:, 0, cols], S0[:, :], True, False)
                mm(ps[rows, P:T1], V[:, 1, cols], S1[:, :], False, False)
                mm(ps[rows, 2 * P:T1], V3[base:base + N_META, cols], S2[base:base + N_META, :], False, True, b.filled(key))

            hn1 = [HN1[:, k, :] for k in range(KT)]
            hn2 = [HN2[:, k, :] for k in range(KT)]

            def projection(key):
                first = key == ("hq", 0)
                product(b1, key, hn1, T1, ready=[s1["hn"].upto(k) for k in range(KT)] if first else None)

            def turn(key):
                kind, h = key
                if kind in ROT:
                    pe.wait_ge(*s1["staged"].upto(key))
                    scores(b1, (kind, h, "turned"), [(slice(0, P), slice(0, T1), ROT[kind][3], XS[:, s1_slot[key], :])])
                elif kind in ("hi", "rv", "dv"):
                    pe.wait_ge(*s1["staged"].upto(key))
                    x = XS[:, s1_slot[key], :]
                    transposes(b1, (kind, h, "turned"),
                               [(slice(0, P), slice(0, P), x[:, 0:P]), (slice(0, P), slice(P, 2 * P), x[:, P:2 * P]),
                                (slice(0, N_META), slice(2 * P, 3 * P), x[:, 2 * P:T1])])

            def project_all(keys, before=None):
                for key in keys:
                    projection(key)
                    if before is not None:
                        turn(before)
                    before = key
                return before

            def merge_a(n, j):
                product(b1, ("mA", n, j), hn1, T1)

            def merge_b(n, j):
                src = {0: RG, 1: HG, 2: DQ}[n]
                step = [("h", k) if n == 1 else ("r", k // 2) if n == 0 else ("d", k) for k in range(KT)]
                product(b1, ("mB", n, j), [src[:, k, :] for k in range(KT)], T1,
                        ready=[s1["normed"].upto(step[k]) for k in range(KT)] if j == 0 else None)

            pe.wait_ge(inputs_in, 16 * N_INPUTS)
            with pe.Fori(0, DEPTH) as layer:
                pe.wait_ge(layer_begin, layer + 1)
                pe.sem_inc(pe_in)
                stream.update(n=0, release=None, layer=layer, first=0, per=SLABS1 // RING)
                sum_squares(b1, "ss_mix", hn1, T1, [s1["sq"].upto(("mix", k)) for k in range(KT)])
                last = project_all(TILES_HG)
                last = project_all(TILES_RET, last)
                da = list(TILES_DA)
                for h in range(HG_HEADS):
                    pe.wait_ge(*s1["z"].upto(h))
                    for t in range(3):
                        level_products(b1, h, Z, t, HQ[:, h, :], HK[:, h, :])
                    scores(b1, ("cross", h), [
                        (slice(0, P), slice(0, P), Z[:, 3, 0:P], Z[:, 3, P:2 * P]),
                        (slice(0, P), slice(P, P + N_META), Z[:, 8, 0:P], Z[:, 8, 2 * P:T1]),
                        (slice(0, P), slice(P + N_META, P + 2 * N_META), Z[:, 8, P:2 * P], Z[:, 8, 2 * P:T1])])
                    last = project_all([da.pop(0)], last)
                    pe.wait_ge(*s1["att"].upto(("h", h)))
                    values_times_weights(b1, ("o", "h", h), HV, 0, slice(h * P, h * P + P))
                    last = project_all([da.pop(0)], last)
                    sum_squares(b1, ("ss", "h", h), [SQ[:, 0, :]], T1, [s1["sqo"].upto(("h", h, 0))])
                    last = project_all([da.pop(0)], last)
                turn(last)
                pe.wait_ge(*s1["taken"].upto(("rk", 3)))
                for h in range(RET_HEADS):
                    scores(b1, ("rs", h, 0), [(slice(0, P), slice(0, T1), RK[:, h, 0:P], RQ[:, h, :])])
                    scores(b1, ("rs", h, 1), [
                        (slice(0, P), slice(0, P + N_META), RK[:, h, P:2 * P], RQ[:, h, P:T1]),
                        (slice(0, N_META), slice(P + N_META, P + 2 * N_META), RK[:, h, 2 * P:T1], RQ[:, h, 2 * P:T1])])
                    merge_a(1, 2 * h)
                    merge_b(1, 2 * h)
                    pe.wait_ge(*s1["att"].upto(("r", h)))
                    for e in range(2):
                        values_times_weights(b1, ("o", "r", 2 * h + e), RV, 32, slice((2 * h + e) * P, (2 * h + e + 1) * P))
                    merge_a(1, 2 * h + 1)
                    sum_squares(b1, ("ss", "r", h), [SQ[:, e, :] for e in range(2)], T1,
                                [s1["sqo"].upto(("r", h, e)) for e in range(2)])
                    merge_b(1, 2 * h + 1)

                def da_scores(h):
                    for m in range(2):
                        q, k = DQ[64 * m:64 * m + 64, h, :], DK[64 * m:64 * m + 64, h, :]
                        scores(b1, ("ds", h, m), [(slice(0, P), slice(0, P), q[:, 0:P], k[:, 0:P]),
                                                  (slice(0, P), slice(P, 3 * P), q[:, P:2 * P], k[:, 0:2 * P])])
                        scores(b1, ("ds", h, 2 + m), [(slice(0, N_META), slice(0, T1), q[:, 2 * P:T1], k)])

                pe.wait_ge(*s1["taken"].upto(("dk", 7)))
                da_scores(0)
                for h in range(DA_HEADS):
                    if h + 1 < DA_HEADS:
                        da_scores(h + 1)
                    merge_a(0, h)
                    if h > 0:
                        sum_squares(b1, ("ss", "d", h - 1), [SQ[:, 0, :]], T1, [s1["sqo"].upto(("d", h - 1, 0))])
                    pe.wait_ge(*s1["w"].upto(h))
                    transposes(b1, ("dt", h), [
                        (slice(0, P), slice(0, P), WA[0][:, :]), (slice(0, P), slice(P, 2 * P), WA[1][:, 0:P]),
                        (slice(0, P), slice(2 * P, T1), WA[2][0:N_META, 0:P]),
                        (slice(0, P), slice(T1, T1 + P), WA[1][:, P:2 * P]),
                        (slice(0, P), slice(T1 + P, T1 + P + N_META), WA[2][0:N_META, P:2 * P]),
                        (slice(0, N_META), slice(T1 + P + N_META, T1 + P + 2 * N_META), WA[2][0:N_META, 2 * P:T1])])
                    merge_b(0, h)
                    pe.wait_ge(*s1["tr"].upto(h))
                    values_times_weights(b1, ("o", "d", h), DV, 64, slice(h * P, h * P + P))
                merge_a(2, 0)
                sum_squares(b1, ("ss", "d", 7), [SQ[:, 0, :]], T1, [s1["sqo"].upto(("d", 7, 0))])
                merge_b(2, 0)
                for j in range(1, KT):
                    merge_a(2, j)
                    merge_b(2, j)
                for j in range(KT):
                    product(b1, ("wo", j), [Y1[:, k, :] for k in range(KT)], T1,
                            ready=[s1["y"].upto((2, k)) for k in range(KT)] if j == 0 else None)
                sum_squares(b1, "ss_ffn", hn1, T1, [s1["sq"].upto(("ffn", k)) for k in range(KT)])
                for j in range(FT):
                    for half in range(2):
                        product(b1, ("ff", j, half), hn1, T1,
                                ready=[s1["hn"].upto(("ffn", k)) for k in range(KT)] if j + half == 0 else None)
                for j in range(KT):
                    product(b1, ("down", j), [FF[:, k, :] for k in range(FT)], T1,
                            ready=[s1["ff"].upto(k) for k in range(FT)] if j == 0 else None)
                pe.drain().then_inc(slab_used[(SLABS1 - 1) % RING], 1)
                pe.drain().then_inc(layer_end, 1)

            sum_squares(bm, "ss", [HN1[:, k, N_META:T1] for k in range(KT)], T2, [sm["sq"].upto(k) for k in range(KT)])

            def wide(k, kt, c, n):
                at = (k % RING) * SLAB * P + kt * 512 + c
                return ring[:, at:at + n]

            def wide_done(k):
                stream["release"] = k % RING

            def wide_tile(key, k, c, m=P, ready=None):
                ps = b2.take(pe, key)
                for kt in range(KT):
                    if ready is not None:
                        pe.wait_ge(*ready[kt])
                    last_ = kt == KT - 1
                    mm(ps[0:m, 0:T2], wide(k, kt, c, m), hn2[kt], kt == 0, last_, b2.filled(key) if last_ else None)

            def token_major(key, k, parts):
                ps = b2.take(pe, key)
                at = 0
                for i, (c, n) in enumerate(parts):
                    for t in range(2):
                        for kt in range(KT):
                            end = kt == KT - 1
                            mm(ps[:, at:at + n], HN2[:, kt, t * P:(t + 1) * P], wide(k, kt, c, n), kt == 0, end,
                               b2.filled(key) if end and t == 1 and i == len(parts) - 1 else None)
                        at += n

            def merge2(n, j):
                src = {0: OM, 1: OC, 2: OS, 3: GG}[n]
                product(b2, ("mA", n, j), hn2, T2)
                ready = None
                if j == 0:
                    ready = {0: [s2["o"].upto(("m", p)) for p in range(2)], 1: [s2["oc"].upto()] * 2,
                             2: [s2["o"].upto(("s", p)) for p in range(2)], 3: [s2["normed"].upto(p) for p in range(2)]}[n]
                product(b2, ("mB", n, j), [src[:, k, :] for k in range(2)], T2, ready=ready)

            def attention_scores(kind, h):
                if kind == "m":
                    q, k = QM[0:MLA_QK, h, :], KM[0:MLA_QK, h, :]
                else:
                    r = slice(64 * (h % 2), 64 * (h % 2) + 64)
                    q, k = QS[r, h // 2, :], KS[r, :]
                scores(b2, (kind, "sc", h), [(slice(0, P), slice(0, P), q[:, 0:P], k[:, 0:P]),
                                             (slice(0, P), slice(P, 3 * P), q[:, P:T2], k)])

            def attention_turn(kind, h):
                pe.wait_ge(*s2["w"].upto((kind, h)))
                w = W2[:, h % 2, :]
                transposes(b2, (kind, "t", h), [(slice(0, P), slice(i * P, (i + 1) * P), w[:, i * P:(i + 1) * P])
                                                for i in range(3)])

            def values2(kind, h, V):
                key = (kind, "o", h if kind == "g" else h // 2)
                ps = b2.take(pe, key) if h % 2 == 0 or kind == "g" else b2.of(key)
                r = slice(64 * (h % 2), 64 * (h % 2) + 64)
                mm(ps[r, 0:T2], V[:, 0, h * 64:h * 64 + 64] if V is not VS else V[:, 0, :], SS[:, h % 2, 0:T2], True, False)
                mm(ps[r, P:T2], V[:, 1, h * 64:h * 64 + 64] if V is not VS else V[:, 1, :], SS[:, h % 2, T2:3 * P], False, True,
                   b2.filled(key) if h % 2 or kind == "g" else None)

            with pe.Fori(0, DEPTH) as layer:
                pe.wait_ge(layer_begin, layer + DEPTH + 2)
                pe.sem_inc(pe_in)
                stream.update(n=HEAD2 * SLAB, release=None, layer=layer, first=DEPTH * SLABS1 // RING, per=SLABS2 // RING)
                sum_squares(b2, "ss_att", hn2, T2, [s2["sq"].upto(("att", k)) for k in range(KT)])
                slab_wait(0)
                wide_tile("cq0", 0, 0, ready=[s2["hn"].upto(("att", k)) for k in range(KT)])
                wide_tile("cq1", 0, P)
                wide_tile("ckv", 0, IN2["ckv"])
                wide_tile("kr", 0, IN2["krope"] - MLA_NOPE, MLA_QK)
                wide_done(0)
                slab_wait(1)
                for i, key in enumerate(("cb0", "cb1", "cc0", "cc1")):
                    wide_tile(key, 1, i * P)
                sum_squares(b2, "ss_q", [SQ2[:, i, :] for i in range(2)], T2, [s2["evac"].upto(k) for k in ("cq0", "cq1")])
                sum_squares(b2, "ss_kv", [SQ2[:, 2, :]], T2, [s2["evac"].upto("ckv")])
                wide_done(1)
                slab_wait(2)
                for i, key in enumerate(("cx0", "cx1", "qs0", "qs1")):
                    wide_tile(key, 2, i * P)
                wide_done(2)
                slab_wait(3)
                sw = (3 % RING) * SLAB * P
                pe.wait_ge(*s2["cqn"].upto())
                for p in range(2):
                    ps = b2.take(pe, ("qu", p))
                    for h in (2 * p, 2 * p + 1):
                        for kt in range(2):
                            at = sw + kt * MLA_HEADS * MLA_QK + h * MLA_QK
                            done = None
                            if h % 2 and kt:
                                done = b2.filled(("qu", p))
                            mm(ps[0:MLA_QK, (h % 2) * T2:(h % 2 + 1) * T2], ring[:, at:at + MLA_QK], CQ[:, kt, :],
                               kt == 0, kt == 1, done)
                pe.wait_ge(*s2["ckn"].upto())
                kv = sw + 2 * MLA_HEADS * MLA_QK
                for p in range(2):
                    scores(b2, ("ku", p), [(slice(0, MLA_NOPE), slice((h % 2) * T2, (h % 2 + 1) * T2),
                                            ring[:, kv + h * P:kv + h * P + 64], CKV[:, :]) for h in (2 * p, 2 * p + 1)])
                vw = ring[:, kv:kv + MLA_HEADS * P].rearrange("p (h c) -> p h c", c=P)[:, :, 64:P]
                scores(b2, "vu", [(slice(0, P), slice(t * T2, (t + 1) * T2), CKV[:, t * P:(t + 1) * P], vw) for t in range(2)])
                pe.wait_ge(*s2["mlaw"].upto())
                wide_done(3)
                slab_wait(4)
                wide_tile("ks", 4, IN2["dk"] - WIDE2[4], 64)
                wide_tile("iq0", 4, IN2["iq"] - WIDE2[4])
                wide_tile("iq1", 4, IN2["iq"] - WIDE2[4] + P)
                wide_tile("ik", 4, IN2["ik"] - WIDE2[4], 32)
                pe.wait_ge(*s2["evac"].upto("kr"))
                scores(b2, "kturn", [(slice(0, MLA_QK), slice(0, T2), rotM[0:MLA_QK, 0:MLA_QK], KR[0:MLA_QK, :])])
                for p in range(2):
                    pe.wait_ge(*s2["qm"].upto(p))
                    scores(b2, ("qturn", p), [(slice(0, MLA_QK), slice(i * T2, (i + 1) * T2), rotM[0:MLA_QK, 0:MLA_QK],
                                               QM[0:MLA_QK, 2 * p + i, :]) for i in range(2)])
                token_major("vsw", 4, [(IN2["dv"] - WIDE2[4], 64), (IN2["iw"] - WIDE2[4], IDX_HEADS)])
                wide_done(4)
                slab_wait(5)
                wide_tile("gq", 5, 0)
                wide_tile("gk", 5, P)
                token_major("gv", 5, [(2 * P, 2 * P)])
                wide_done(5)
                slab_wait(6)
                wide_tile("glr", 6, 0, 16)
                wide_tile("gr0", 6, 16)
                wide_tile("gr1", 6, 16 + P)
                pe.wait_ge(*s2["evac"].upto("glr"))
                scores(b2, "gl", [(slice(0, P), slice(0, T2), WG[0:16, :], GL[0:16, :])])
                wide_done(6)
                pe.wait_ge(*s2["evac"].upto("ik"))
                for i in range(2):
                    kn = (i + 1) * P
                    for c in range(4):
                        r = slice(32 * c, 32 * c + 32)
                        scores(b2, ("ix", i, c), [(slice(0, P), slice(g * kn, (g + 1) * kn), IQ[r, g, i * P:(i + 1) * P],
                                                   IK[r, 0:kn]) for g in range(2)])
                pe.wait_ge(*s2["km"].upto())
                attention_scores("m", 0)
                for h in range(MLA_HEADS):
                    if h + 1 < MLA_HEADS:
                        attention_scores("m", h + 1)
                    merge2(1, 2 * h)
                    attention_turn("m", h)
                    merge2(1, 2 * h + 1)
                    pe.wait_ge(*s2["tr"].upto(("m", h)))
                    values2("m", h, VM)
                pe.wait_ge(*s2["z"].upto())
                for g in range(GLA_HEADS):
                    r = slice(32 * g, 32 * g + 32)
                    for t in range(2):
                        level_products(b2, g, Z2[r, :, :], t, GQ[r, :], GK[r, :])
                    scores(b2, ("cross", g), [(slice(0, P), slice(0, P), Z2[r, 3, 0:P], Z2[r, 3, P:T2])])
                    merge2(0, 2 * g)
                    pe.wait_ge(*s2["att"].upto(g))
                    values2("g", g, GV)
                    merge2(0, 2 * g + 1)
                    if g % 2:
                        p = g // 2
                        sum_squares(b2, ("ssg", p), [SQ2[:, p, :]], T2, [s2["sqo"].upto(p)], ones64)
                attention_scores("s", 0)
                for h in range(DSA_HEADS):
                    if h + 1 < DSA_HEADS:
                        attention_scores("s", h + 1)
                    merge2(3, 2 * h)
                    attention_turn("s", h)
                    merge2(3, 2 * h + 1)
                    pe.wait_ge(*s2["tr"].upto(("s", h)))
                    values2("s", h, VS)
                for j in range(KT):
                    merge2(2, j)
                for j in range(KT):
                    product(b2, ("wo", j), [Y2[:, k, :] for k in range(KT)], T2,
                            ready=[s2["y"].upto((2, k)) for k in range(KT)] if j == 0 else None)
                sum_squares(b2, "ss_ffn", hn2, T2, [s2["sq"].upto(("ffn", k)) for k in range(KT)])
                for j in range(FT):
                    for half in range(2):
                        product(b2, ("ff", j, half), hn2, T2,
                                ready=[s2["hn"].upto(("ffn", k)) for k in range(KT)] if j + half == 0 else None)
                for j in range(KT):
                    product(b2, ("down", j), [FF2[:, k, :] for k in range(FT)], T2,
                            ready=[s2["ff"].upto(k) for k in range(FT)] if j == 0 else None)
                pe.drain().then_inc(slab_used[(SLABS2 - 1) % RING], 1)
                pe.drain().then_inc(layer_end, 1)
            sum_squares(be, "ss", hn2, T2, [se["sq"].upto(k) for k in range(KT)])

        @block.scalar
        def _(act):
            def op(out_, in_, func, done=None, **kw):
                i = nc.scalar.activation(out_, in_, func, **kw)
                if done is not None:
                    i.then_inc(*done)
                return i

            def squares(s, tag, src, dst, ready=None):
                for k in range(KT):
                    if ready is not None:
                        act.wait_ge(*ready(k))
                    op(dst[:, k, :], src[:, k, :], ACT.Square, s["sq"].done((tag, k) if tag else k))

            def inverse_root(s, b, key, step, width, tokens, free=None):
                act.wait_ge(*b.full(key))
                if free is not None:
                    act.wait_ge(*free)
                op(RS[:, 0:tokens], b.of(key)[:, 0:tokens], ACT.Ln, b.free(key), scale=1.0 / width, bias=eps)
                nc.scalar.drain()
                op(RS[:, 0:tokens], RS[:, 0:tokens], ACT.Exp, s["rs"].done(step), scale=-0.5)

            def stage(key):
                kind, h = key
                act.wait_ge(*b1.full(key))
                ps = b1.of(key)[:, 0:T1]
                if kind == "hq":
                    op(HQ[:, h, :], ps, ACT.Copy, b1.free(key))
                elif kind == "hf":
                    op(HC[:, h, :], ps, ACT.Sigmoid)
                    op(HK[:, h, :], ps, ACT.Sigmoid, b1.free(key), scale=-1.0)
                    nc.scalar.drain().then_inc(*s1["sig_f"].done(h))
                elif kind in ("hg", "rg"):
                    if h >= 2 or kind == "rg":
                        act.wait_ge(*s1["gated"].upto((kind, h - 2) if h >= 2 else ("hg", 6 + h)))
                    op(SG[:, h % 2, :], ps, ACT.Sigmoid, s1["sg"].done(key))
                else:
                    i = STAGED.index(key)
                    if i >= 2:
                        act.wait_ge(*s1["taken"].upto(STAGED[i - 2]))
                    op(XS[:, s1_slot[key], :], ps, ACT.Copy, b1.free(key))
                    nc.scalar.drain().then_inc(*s1["staged"].done(key))

            def exp_levels(h):
                act.wait_ge(*s1["zdiff"].upto(h))
                op(Z[:, 0:4, 0:2 * P], Z[:, 0:4, 0:2 * P], ACT.Exp)
                op(Z[:, 4:8, :], Z[:, 4:8, :], ACT.Exp)
                op(Z[:, 8, P:T1], Z[:, 8, P:T1], ACT.Exp)
                nc.scalar.drain().then_inc(*s1["zexp"].done(h))

            def square_output(key, e):
                act.wait_ge(*b1.full(("o",) + key))
                op(SQ[:, e, :], b1.of(("o",) + key)[:, 0:T1], ACT.Square, s1["sqo"].done((key[0], key[1] // 2 if key[0] == "r" else key[1], e)))

            def merge_sigmoid(n, j):
                act.wait_ge(*b1.full(("mA", n, j)))
                seq = MERGE1.index(n) * KT + j
                if seq >= 2:
                    act.wait_ge(*s1["y"].upto((MERGE1[(seq - 2) // KT], (seq - 2) % KT)))
                op(SG[:, j % 2, :], b1.of(("mA", n, j))[:, 0:T1], ACT.Sigmoid, b1.free(("mA", n, j)))
                nc.scalar.drain().then_inc(*s1["sigm"].done((n, j)))

            def da_exp(h):
                for i, n in enumerate([P, P, N_META]):
                    act.wait_ge(*s1["sco"].upto((h, i)))
                    for m in range(2):
                        op(SC[i][0:n, m, :], SC[i][0:n, m, :], ACT.Exp, bias=small[0:n, 2 * i + m:2 * i + m + 1],
                           accum_out=small[0:n, 8 + 2 * i + m:9 + 2 * i + m])
                    nc.scalar.drain().then_inc(*s1["expd"].done((h, i)))

            def da_turned(h):
                act.wait_ge(*b1.full(("dt", h)))
                ps = b1.of(("dt", h))
                op(S0[:, :], ps[:, 0:T1], ACT.Copy)
                op(S1[:, :], ps[:, T1:T1 + P + N_META], ACT.Copy)
                op(S2[64:64 + N_META, :], ps[0:N_META, T1 + P + N_META:T1 + P + 2 * N_META], ACT.Copy, b1.free(("dt", h)))
                nc.scalar.drain().then_inc(*s1["tr"].done(h))

            act.wait_ge(inputs_in, 16 * N_INPUTS)
            act.wait_ge(*s0["dve"].upto("lb"))
            op(lb_e[:, :], lb_e[:, :], ACT.Exp)
            op(lam_e[:, :], lam_e[:, :], ACT.Exp)
            nc.scalar.drain().then_inc(*s0["act"].done("exp"))
            act.wait_ge(*s0["dve"].upto("ang"))
            op(angs[:, :], angs[:, :], ACT.Sin)
            nc.scalar.drain().then_inc(*s0["act"].done("sin"))
            with act.Fori(0, DEPTH) as layer:
                act.wait_ge(layer_begin, layer + 1)
                act.sem_inc(act_in)
                squares(s1, "mix", X1, HN1)
                inverse_root(s1, b1, "ss_mix", "mix", D_MODEL, T1)
                for key in TILES_HG:
                    stage(key)
                    if key == ("hi", 1):
                        act.wait_ge(*s1["f_in"].upto())
                        op(HC[:, :, :], HC[:, :, :], ACT.Ln, s1["lnf"].done())
                    if key == ("hi", 5):
                        act.wait_ge(*s1["cum"].upto())
                        op(e1_sb[:, :], HC[:, :, 2 * P - 1], ACT.Exp, s1["e1"].done())
                for key in TILES_RET:
                    stage(key)
                    if key == ("rk", 3):
                        exp_levels(0)
                da = list(TILES_DA)
                for h in range(HG_HEADS):
                    if h + 1 < HG_HEADS:
                        exp_levels(h + 1)
                    stage(da.pop(0))
                    square_output(("h", h), 0)
                    stage(da.pop(0))
                    inverse_root(s1, b1, ("ss", "h", h), ("h", h), P, T1,
                                 s1["normed"].upto(("h", h - 1)) if h else s1["hn"].upto(KT - 1))
                    stage(da.pop(0))
                for h in range(RET_HEADS):
                    merge_sigmoid(1, 2 * h)
                    square_output(("r", 2 * h), 0)
                    square_output(("r", 2 * h + 1), 1)
                    merge_sigmoid(1, 2 * h + 1)
                    inverse_root(s1, b1, ("ss", "r", h), ("r", h), 2 * P, T1, s1["normed"].upto(("r", h - 1) if h else ("h", 7)))
                da_exp(0)
                for h in range(DA_HEADS):
                    if h + 1 < DA_HEADS:
                        da_exp(h + 1)
                    if h > 0:
                        inverse_root(s1, b1, ("ss", "d", h - 1), ("d", h - 1), P, T1,
                                     s1["normed"].upto(("d", h - 2) if h > 1 else ("r", 3)))
                    merge_sigmoid(0, h)
                    da_turned(h)
                    square_output(("d", h), 0)
                merge_sigmoid(2, 0)
                inverse_root(s1, b1, ("ss", "d", 7), ("d", 7), P, T1, s1["normed"].upto(("d", 6)))
                for j in range(1, KT):
                    merge_sigmoid(2, j)
                squares(s1, "ffn", X1, HN1, ready=lambda k: s1["x"].upto(("wo", k)))
                inverse_root(s1, b1, "ss_ffn", "ffn", D_MODEL, T1, s1["normed"].upto(("d", 7)))
                for j in range(FT):
                    if j >= 2:
                        act.wait_ge(*s1["ff"].upto(j - 2))
                    for half, dst in enumerate((CG, CV)):
                        act.wait_ge(*b1.full(("ff", j, half)))
                        f = half * FT + j
                        op(dst[:, j % 2, :], b1.of(("ff", j, half))[:, 0:T1], ACT.Identity,
                           s1["conv"].done((j, half)), scale=par("cw", 2 * 2 * FT + f), bias=par("cb", f))
                    act.wait_ge(*s1["gated"].upto(("ff", j)))
                    op(SG[:, j % 2, :], CG[:, j % 2, :], ACT.Sigmoid, s1["sg"].done(("ff", j)))
                act.drain().then_inc(layer_end, 1)

            act.wait_ge(layer_begin, DEPTH + 1)
            for k in range(KT):
                op(HN1[:, k, N_META:T1], X1[:, k, N_META:T1], ACT.Square, sm["sq"].done(k))
            inverse_root(sm, bm, "ss", 0, D_MODEL, T2)

            def copy2(key, dst, rows=slice(0, P), cols=slice(0, T2), last=True, signal=True, func=ACT.Copy, **kw):
                act.wait_ge(*b2.full(key))
                op(dst, b2.of(key)[rows, cols], func, b2.free(key) if last else None, **kw)
                if signal:
                    nc.scalar.drain().then_inc(*s2["evac"].done(key))

            def attention_exp(kind, h):
                act.wait_ge(*s2["sc"].upto((kind, h)))
                for i, cols in enumerate((slice(0, P), slice(P, 3 * P))):
                    c = 32 + 8 * (h % 2) + i
                    op(SC2[:, h % 2, cols], SC2[:, h % 2, cols], ACT.Exp, bias=small[:, c:c + 1],
                       accum_out=small[:, c + 2:c + 3])
                nc.scalar.drain().then_inc(*s2["expd"].done((kind, h)))

            def attention_turned(kind, h):
                act.wait_ge(*b2.full((kind, "t", h)))
                if h >= 2:
                    act.wait_ge(*b2.full((kind, "o", h // 2 - 1)))
                op(SS[:, h % 2, :], b2.of((kind, "t", h))[:, 0:3 * P], ACT.Copy, b2.free((kind, "t", h)))
                nc.scalar.drain().then_inc(*s2["tr"].done((kind, h)))

            def attention_output(kind, p, dst):
                act.wait_ge(*b2.full((kind, "o", p)))
                op(dst[:, p, :], b2.of((kind, "o", p))[:, 0:T2], ACT.Copy, b2.free((kind, "o", p)))
                nc.scalar.drain().then_inc(*s2["o"].done((kind, p)))

            def merge_sigmoid2(n, j):
                act.wait_ge(*b2.full(("mA", n, j)))
                seq = MERGE2.index(n) * KT + j
                if seq >= 2:
                    act.wait_ge(*s2["y"].upto((MERGE2[(seq - 2) // KT], (seq - 2) % KT)))
                op(SGM[:, j % 2, :], b2.of(("mA", n, j))[:, 0:T2], ACT.Sigmoid, b2.free(("mA", n, j)))
                nc.scalar.drain().then_inc(*s2["sigm"].done((n, j)))

            with act.Fori(0, DEPTH) as layer:
                act.wait_ge(layer_begin, layer + DEPTH + 2)
                act.sem_inc(act_in)
                squares(s2, "att", X2, HN2)
                inverse_root(s2, b2, "ss_att", "att", D_MODEL, T2)
                for i, key in enumerate(("cq0", "cq1", "ckv")):
                    act.wait_ge(*b2.full(key))
                    op(SQ2[:, i, :], b2.of(key)[:, 0:T2], ACT.Square)
                    copy2(key, CQ[:, i, :] if i < 2 else CKV[:, :])
                copy2("kr", KR[MLA_NOPE:MLA_QK, :], rows=slice(MLA_NOPE, MLA_QK))
                for i in range(2):
                    copy2(f"cb{i}", SB[:, i, :])
                for i in range(2):
                    copy2(f"cc{i}", SI[:, i, :])
                inverse_root(s2, b2, "ss_q", "q", 2 * P, T2, s2["hn"].upto(("att", KT - 1)))
                inverse_root(s2, b2, "ss_kv", "kv", P, T2, s2["cqn"].upto())
                for i in range(2):
                    copy2(f"qs{i}", QS[:, i, :])
                for p in range(2):
                    act.wait_ge(*b2.full(("qu", p)))
                    op(QM[0:MLA_QK, 2 * p:2 * p + 2, :], b2.of(("qu", p))[0:MLA_QK, :].rearrange("p (h t) -> p h t", t=T2), ACT.Copy,
                       b2.free(("qu", p)))
                    nc.scalar.drain().then_inc(*s2["qm"].done(p))
                for p in range(2):
                    copy2(("ku", p), KM[0:MLA_NOPE, 2 * p:2 * p + 2, :].rearrange("p h t -> p (h t)"), rows=slice(0, MLA_NOPE),
                          cols=slice(0, 2 * T2))
                copy2("vu", VM[:, :, :].rearrange("p a b -> p (a b)"), cols=slice(0, 2 * T2))
                copy2("ks", KS[0:64, :], rows=slice(0, 64), last=False, signal=False)
                copy2("ks", KS[64:P, :], rows=slice(0, 64))
                copy2("iq0", IQ[:, 0, :])
                copy2("iq1", IQ[:, 1, :])
                for q in range(4):
                    copy2("ik", IK[32 * q:32 * q + 32, :], rows=slice(0, 32), last=q == 3, signal=q == 3)
                copy2("vsw", VS[:, :, :].rearrange("p a b -> p (a b)"), cols=slice(0, P), last=False, signal=False)
                copy2("vsw", IW[:, :, :].rearrange("p a b -> p (a b)"), cols=slice(P, P + 2 * IDX_HEADS), scale=IDX_HEADS ** -0.5)
                copy2("gq", GQ[:, :], scale=GLA_DK ** -0.5)
                copy2("gk", GK[:, :])
                copy2("gv", GV[:, :, :].rearrange("p a b -> p (a b)"), cols=slice(0, 2 * T2))
                copy2("glr", GL[0:16, :], rows=slice(0, 16))
                for i in range(2):
                    act.wait_ge(*b2.full(f"gr{i}"))
                    op(SGM[:, i, :], b2.of(f"gr{i}")[:, 0:T2], ACT.Sigmoid)
                    nc.scalar.drain().then_inc(*s2["sg"].done(i))
                for i in range(2):
                    for c in range(4):
                        seq = 4 * i + c
                        if seq >= 2:
                            act.wait_ge(*s2["used"].upto(seq - 2))
                        copy2(("ix", i, c), REL[:, seq % 2, 0:2 * (i + 1) * P], cols=slice(0, 2 * (i + 1) * P), signal=False,
                              func=ACT.Relu, scale=32 ** -0.5)
                        nc.scalar.drain().then_inc(*s2["relu"].done(seq))
                act.wait_ge(*s2["gz"].upto())
                op(GE[:, :], GE[:, :], ACT.Exp)
                nc.scalar.drain()
                op(GE[:, :], GE[:, :], ACT.Ln, bias=one)
                nc.scalar.drain().then_inc(*s2["gez"].done())
                attention_exp("m", 0)
                act.wait_ge(*s2["zdiff"].upto())
                op(Z2[:, :, :], Z2[:, :, :], ACT.Exp)
                nc.scalar.drain().then_inc(*s2["zexp"].done())
                for h in range(MLA_HEADS):
                    if h + 1 < MLA_HEADS:
                        attention_exp("m", h + 1)
                    merge_sigmoid2(1, 2 * h)
                    attention_turned("m", h)
                    merge_sigmoid2(1, 2 * h + 1)
                    if h % 2:
                        attention_output("m", h // 2, OM)
                for g in range(GLA_HEADS):
                    merge_sigmoid2(0, 2 * g)
                    r = slice(64 * (g % 2), 64 * (g % 2) + 64)
                    act.wait_ge(*b2.full(("g", "o", g)))
                    op(SQ2[r, g // 2, :], b2.of(("g", "o", g))[r, 0:T2], ACT.Square)
                    op(GO[r, g // 2, :], b2.of(("g", "o", g))[r, 0:T2], ACT.Copy, b2.free(("g", "o", g)))
                    if g % 2:
                        nc.scalar.drain().then_inc(*s2["sqo"].done(g // 2))
                    merge_sigmoid2(0, 2 * g + 1)
                    if g % 2:
                        inverse_root(s2, b2, ("ssg", g // 2), ("g", g // 2), 64, T2,
                                     s2["ckn"].upto() if g == 1 else s2["normed"].upto(0))
                attention_exp("s", 0)
                for h in range(DSA_HEADS):
                    if h + 1 < DSA_HEADS:
                        attention_exp("s", h + 1)
                    merge_sigmoid2(3, 2 * h)
                    attention_turned("s", h)
                    merge_sigmoid2(3, 2 * h + 1)
                    if h % 2:
                        attention_output("s", h // 2, OS)
                for j in range(KT):
                    merge_sigmoid2(2, j)
                squares(s2, "ffn", X2, HN2, ready=lambda k: s2["x"].upto(("wo", k)))
                inverse_root(s2, b2, "ss_ffn", "ffn", D_MODEL, T2, s2["normed"].upto(1))
                for j in range(FT):
                    act.wait_ge(*b2.full(("ff", j, 0)))
                    if j >= 2:
                        act.wait_ge(*s2["ff"].upto(j - 2))
                    op(SGM[:, j % 2, :], b2.of(("ff", j, 0))[:, 0:T2], ACT.Sigmoid, s2["sigf"].done(j))
                act.drain().then_inc(layer_end, 1)
            act.wait_ge(layer_begin, 2 * DEPTH + 2)
            for k in range(KT):
                op(HN2[:, k, :], X2[:, k, :], ACT.Square, se["sq"].done(k))
            inverse_root(se, be, "ss", 0, D_MODEL, T2)

        @block.vector
        def _(dve):
            V = nc.vector

            def fence(done=None):
                i = V.drain()
                if done is not None:
                    i.then_inc(*done)

            def norm(s, rs_step, src, gains, dst, tokens, step):
                dve.wait_ge(*s["rs"].upto(rs_step))
                for k in range(KT):
                    V.scalar_tensor_tensor(dst[:, k, :], src[:, k, :], gains(k), RS[:, 0:tokens], ALU.mult, ALU.mult)\
                        .then_inc(*step(k))

            def level_differences(C, zq, levels_at, tokens, scan_end):
                for s, z in levels_at:
                    n = 2 * P if s >= 16 else tokens
                    c = C[:, 0:n].rearrange("p (b t s) -> p b t s", t=2, s=s)
                    d = zq[:, z, 0:n].rearrange("p (b t s) -> p b t s", t=2, s=s)
                    ref = c[:, :, 0, s - 1:s].to_broadcast([P, n // (2 * s), s])
                    V.tensor_tensor(d[:, :, 0, :], ref, c[:, :, 0, :], ALU.subtract)
                    V.tensor_tensor(d[:, :, 1, :], c[:, :, 1, :], ref, ALU.subtract)

            def level_factors(zq, levels_at, tokens, q, k):
                for s, z in levels_at:
                    n = 2 * P if s >= 16 else tokens
                    d = zq[:, z, 0:n].rearrange("p (b t s) -> p b t s", t=2, s=s)
                    for t, m in ((0, k), (1, q)):
                        m = m[:, 0:n].rearrange("p (b t s) -> p b t s", t=2, s=s)[:, :, t, :]
                        V.tensor_tensor(d[:, :, t, :], d[:, :, t, :], m, ALU.mult)

            LV = [(64, 0), (32, 1), (16, 2), (8, 4), (4, 5), (2, 6), (1, 7)]

            def mask_levels(b, h, t, dst):
                if t < 2:
                    for g in range(2):
                        dve.wait_ge(*b.full(("lv", h, t, g)))
                        V.tensor_tensor(LT[:, 4 * g:4 * g + 4, :], b.of(("lv", h, t, g)).rearrange("p (a b) -> p a b", b=P),
                                        lvl[:, 4 * g:4 * g + 4, :], ALU.mult).then_inc(*b.free(("lv", h, t, g)))
                    V.drain()
                    V.tensor_reduce(dst, LT[:, :, :].rearrange("p a b -> p b a"), AXX, ALU.add)
                else:
                    n = N_META
                    dve.wait_ge(*b.full(("lv", h, t, 0)))
                    V.tensor_tensor(LT[0:n, 0:5, 0:n], b.of(("lv", h, t, 0))[0:n, 0:5 * n].rearrange("p (a b) -> p a b", b=n),
                                    lvl[0:n, 3:8, 0:n], ALU.mult).then_inc(*b.free(("lv", h, t, 0)))
                    V.drain()
                    V.tensor_reduce(dst, LT[0:n, 0:5, 0:n].rearrange("p a b -> p b a"), AXX, ALU.add)
                V.drain()

            def hg_differences(h):
                if h > 0:
                    dve.wait_ge(*b1.full(("cross", h - 1)))
                C = HC[:, h, :]
                level_differences(C, Z, LV, T1, None)
                V.tensor_scalar(Z[:, 3, 0:P], C[:, 0:P], C[:, P - 1:P], -1.0, ALU.subtract, ALU.mult)
                V.tensor_copy(Z[:, 3, P:2 * P], C[:, P:2 * P])
                V.tensor_scalar(Z[:, 8, P:2 * P], C[:, P:2 * P], C[:, 2 * P - 1:2 * P], -1.0, ALU.subtract, ALU.mult)
                V.tensor_copy(Z[:, 8, 2 * P:T1], C[:, 2 * P:T1])
                fence(s1["zdiff"].done(h))

            def hg_factors(h):
                dve.wait_ge(*s1["zexp"].upto(h))
                q, k = HQ[:, h, :], HK[:, h, :]
                level_factors(Z, LV, T1, q, k)
                V.tensor_tensor(Z[:, 3, 0:P], Z[:, 3, 0:P], k[:, 0:P], ALU.mult)
                V.tensor_tensor(Z[:, 3, P:2 * P], Z[:, 3, P:2 * P], q[:, P:2 * P], ALU.mult)
                V.tensor_tensor(Z[:, 8, P:2 * P], Z[:, 8, P:2 * P], k[:, P:2 * P], ALU.mult)
                V.tensor_tensor(Z[:, 8, 2 * P:T1], Z[:, 8, 2 * P:T1], q[:, 2 * P:T1], ALU.mult)
                V.drain()
                V.tensor_scalar(Z[:, 8, 0:P], Z[:, 3, 0:P], e1_sb[:, h:h + 1], None, ALU.mult)
                fence(s1["z"].done(h))

            def hg_weights(h):
                mask_levels(b1, h, 0, S0[:, 0:P])
                mask_levels(b1, h, 1, S1[:, 0:P])
                mask_levels(b1, h, 2, S2[0:N_META, :])
                dve.wait_ge(*b1.full(("cross", h)))
                ps = b1.of(("cross", h))
                V.tensor_copy(S0[:, P:T1], ps[:, 0:P + N_META])
                V.tensor_copy(S1[:, P:P + N_META], ps[:, P + N_META:P + 2 * N_META]).then_inc(*b1.free(("cross", h)))
                fence(s1["att"].done(("h", h)))

            def normalise(kind, h):
                dve.wait_ge(*s1["rs"].upto((kind, h)))
                tiles = [("r", 2 * h), ("r", 2 * h + 1)] if kind == "r" else [(kind, h)]
                for i, (kd, t) in enumerate(tiles):
                    o = b1.of(("o", kd, t))[:, 0:T1]
                    if kind == "d":
                        V.scalar_tensor_tensor(DQ[:, t, :], o, par("sub"), RS[:, :], ALU.mult, ALU.mult)\
                            .then_inc(*b1.free(("o", kd, t)))
                        continue
                    dst = HG if kind == "h" else RG
                    V.tensor_tensor(TMP[:, i, :], o, RS[:, :], ALU.mult).then_inc(*b1.free(("o", kd, t)))
                    V.drain()
                    V.tensor_tensor(dst[:, t, :], dst[:, t, :], TMP[:, i, :], ALU.mult)
                fence(s1["normed"].done((kind, h)))

            def settle(key):
                kind, h = key
                if kind in ROT:
                    dst, cos, sin, _ = ROT[kind]
                    dve.wait_ge(*s1["staged"].upto(key))
                    x = XS[:, s1_slot[key], :]
                    V.tensor_tensor(TMP[:, 0, :], x, cos, ALU.mult)
                    dve.wait_ge(*b1.full((kind, h, "turned")))
                    V.tensor_tensor(TMP[:, 1, :], b1.of((kind, h, "turned"))[:, 0:T1], sin, ALU.mult)\
                        .then_inc(*b1.free((kind, h, "turned")))
                    V.drain()
                    V.tensor_tensor(dst[:, h, :], TMP[:, 0, :], TMP[:, 1, :], ALU.add)
                    fence(s1["taken"].done(key))
                elif kind in ("hi", "rv", "dv"):
                    dst, base = VT[{"hi": "h", "rv": "r", "dv": "d"}[kind]]
                    dve.wait_ge(*b1.full((kind, h, "turned")))
                    ps = b1.of((kind, h, "turned"))
                    V.tensor_copy(dst[:, :, h * P:(h + 1) * P], ps[:, 0:2 * P].rearrange("p (a b) -> p a b", b=P))
                    V.tensor_copy(V3[base:base + N_META, h * P:(h + 1) * P], ps[0:N_META, 2 * P:3 * P])\
                        .then_inc(*b1.free((kind, h, "turned")))
                    fence(s1["taken"].done(key))
                elif kind in ("hg", "rg"):
                    dve.wait_ge(*s1["sg"].upto(key))
                    dst = HG if kind == "hg" else RG
                    V.tensor_tensor(dst[:, h, :], SG[:, h % 2, :], b1.of(key)[:, 0:T1], ALU.mult).then_inc(*b1.free(key))
                    fence(s1["gated"].done(key))
                elif kind == "hf":
                    dve.wait_ge(*s1["sig_f"].upto(h))
                    V.tensor_scalar(HK[:, h, :], HK[:, h, :], par("omlb", h), None, ALU.mult)
                    V.tensor_scalar(HC[:, h, :], HC[:, h, :], par("omlb", h), par("lbf", h), ALU.mult, ALU.add)
                    if h == HG_HEADS - 1:
                        fence(s1["f_in"].done())

            def merge(n, j):
                dve.wait_ge(*s1["sigm"].upto((n, j)))
                dve.wait_ge(*b1.full(("mB", n, j)))
                first = n == MERGE1[0]
                dst = Y1[:, j, :] if first else TMP[:, 0, :]
                V.tensor_tensor(dst, SG[:, j % 2, :], b1.of(("mB", n, j))[:, 0:T1], ALU.mult).then_inc(*b1.free(("mB", n, j)))
                V.drain()
                if not first:
                    V.tensor_tensor(Y1[:, j, :], Y1[:, j, :], TMP[:, 0, :], ALU.add)
                fence(s1["y"].done((n, j)))

            def retention_weights(h):
                dve.wait_ge(*b1.full(("rs", h, 0)))
                V.tensor_tensor(S0[:, :], b1.of(("rs", h, 0))[:, 0:T1], retD[:, h, :], ALU.mult).then_inc(*b1.free(("rs", h, 0)))
                dve.wait_ge(*b1.full(("rs", h, 1)))
                ps = b1.of(("rs", h, 1))
                V.tensor_tensor(S1[:, :], ps[:, 0:P + N_META], retD[:, h, 0:P + N_META], ALU.mult)
                V.tensor_tensor(S2[32:32 + N_META, :], ps[0:N_META, P + N_META:P + 2 * N_META], retD[0:N_META, h, 0:N_META],
                                ALU.mult).then_inc(*b1.free(("rs", h, 1)))
                fence(s1["att"].done(("r", h)))

            DA_TILES = [(P, P), (P, 2 * P), (N_META, T1)]

            def da_masked(h):
                for i, (n, kn) in enumerate(DA_TILES):
                    mask = causal[0:n, (2 - i) * P:(2 - i) * P + kn]
                    for m in range(2):
                        key = ("ds", h, m if i < 2 else 2 + m)
                        dve.wait_ge(*b1.full(key))
                        at = P if i == 1 else 0
                        ins = V.scalar_tensor_tensor(SC[i][0:n, m, :], b1.of(key)[0:n, at:at + kn], 64 ** -0.5, mask,
                                                     ALU.mult, ALU.add)
                        if i > 0:
                            ins.then_inc(*b1.free(key))
                    V.drain()
                    V.tensor_reduce(small[0:n, 2 * i:2 * i + 2], SC[i][0:n, :, :], AXX, ALU.max, negate=True)
                    fence(s1["sco"].done((h, i)))

            def da_combined(h):
                if h > 0:
                    dve.wait_ge(*b1.full(("dt", h - 1)))
                for i, (n, kn) in enumerate(DA_TILES):
                    dve.wait_ge(*s1["expd"].upto((h, i)))
                    r = small[0:n, 16 + 2 * i:18 + 2 * i]
                    V.reciprocal(r, small[0:n, 8 + 2 * i:10 + 2 * i])
                    V.drain()
                    V.tensor_scalar(r[:, 1:2], r[:, 1:2], par("nlam")[0:n, :], None, ALU.mult)
                    V.tensor_scalar(WA[i][0:n, :], SC[i][0:n, 0, :], r[:, 0:1], None, ALU.mult)
                    V.drain()
                    V.scalar_tensor_tensor(WA[i][0:n, :], SC[i][0:n, 1, :], r[:, 1:2], WA[i][0:n, :], ALU.mult, ALU.add)
                fence(s1["w"].done(h))

            def conv(j, half):
                key = ("ff", j, half)
                dst = (CG, CV)[half][:, j % 2, :]
                f = half * FT + j
                dve.wait_ge(*s1["conv"].upto((j, half)))
                ps = b1.of(key)
                V.scalar_tensor_tensor(dst[:, 1:T1], ps[:, 0:T1 - 1], par("cw", 2 * FT + f), dst[:, 1:T1], ALU.mult, ALU.add)
                V.drain()
                V.scalar_tensor_tensor(dst[:, 2:T1], ps[:, 0:T1 - 2], par("cw", f), dst[:, 2:T1], ALU.mult, ALU.add)\
                    .then_inc(*b1.free(key))

            def add_to_x(b, s, X, key, j, tokens):
                dve.wait_ge(*b.full(key))
                V.tensor_tensor(X[:, j, :], X[:, j, :], b.of(key)[:, 0:tokens], ALU.add).then_inc(*b.free(key))
                fence(s["x"].done(key))

            dve.wait_ge(inputs_in, 16 * N_INPUTS)
            lb2 = lb_sb[:, :].rearrange("p (l k) -> p l k", k=KT)
            lbe2 = lb_e[:, :].rearrange("p (l k) -> p l k", k=KT)
            V.tensor_tensor(lb_t[:, 0:KT], lb2[:, 0, :], lb2[:, 1, :], ALU.max)
            lam3 = lam_sb[:, :].rearrange("p (l a b d) -> p l a b d", l=DEPTH, a=2, b=2)
            V.tensor_tensor(lam_t[:, :].rearrange("p (l a d) -> p l a d", l=DEPTH, a=2), lam3[:, :, :, 0, :],
                            lam3[:, :, :, 1, :], ALU.mult)
            V.drain()
            V.tensor_reduce(lam_e[:, :], lam_t[:, :].rearrange("p (a d) -> p a d", d=64), AXX, ALU.add)
            for l in range(DEPTH):
                V.tensor_tensor(lbe2[:, l, :], lb2[:, l, :], lb_t[:, 0:KT], ALU.subtract)
            fence(s0["dve"].done("lb"))
            V.tensor_copy(angs[:, T2:2 * T2], pos_sb[:, :])
            V.drain()
            V.tensor_scalar(angs[:, 0:T2], angs[:, T2:2 * T2], const("invM"), None, ALU.mult)
            V.drain()
            V.tensor_scalar(turns[:, :], angs[:, 0:T2], float(np.float32(1 / (2 * np.pi))), ROUND, ALU.mult, ALU.add)
            V.drain()
            V.tensor_scalar(turns[:, :], turns[:, :], ROUND, None, ALU.subtract)
            for c in TWO_PI:
                V.drain()
                V.scalar_tensor_tensor(angs[:, 0:T2], turns[:, :], -c, angs[:, 0:T2], ALU.mult, ALU.add)
            V.drain()
            V.tensor_scalar(angs[:, 0:T2], angs[:, 0:T2], 3.1415925, -3.1415925, ALU.min, ALU.max)
            V.drain()
            V.tensor_scalar(angs[:, T2:2 * T2], angs[:, 0:T2], 0.5, None, ALU.mult)
            fence(s0["dve"].done("ang"))
            dve.wait_ge(*s0["act"].upto("exp"))
            V.tensor_tensor(lb_t[:, 0:KT], lbe2[:, 0, :], lbe2[:, 1, :], ALU.add)
            V.drain()
            V.reciprocal(lb_t[:, 0:KT], lb_t[:, 0:KT])
            V.drain()
            for l in range(DEPTH):
                V.tensor_tensor(lbe2[:, l, :], lbe2[:, l, :], lb_t[:, 0:KT], ALU.mult)
            V.drain()
            V.tensor_tensor(lb_t[:, 0:KT], lbe2[:, 0, :], lbe2[:, 1, :], ALU.add)
            V.drain()
            V.tensor_tensor(lb_t[:, 0:KT], lb_t[:, 0:KT], lbe2[:, 0, :], ALU.subtract)
            V.drain()
            p1 = par1_sb[:, :].rearrange("p (l n) -> p l n", n=NPAR1)
            om, lf = PAR1["omlb"][0], PAR1["lbf"][0]
            V.memset(p1[:, 0, om:om + KT], 1.0)
            V.memset(p1[:, 0, lf:lf + KT], LB_FLOOR)
            V.tensor_scalar(p1[:, 1, om:om + KT], lb_t[:, 0:KT], -1.0, 1.0, ALU.mult, ALU.add)
            V.tensor_scalar(p1[:, 1, lf:lf + KT], lb_t[:, 0:KT], LB_FLOOR, None, ALU.max)
            nl, sub = PAR1["nlam"][0], PAR1["sub"][0]
            for l in range(DEPTH):
                init = 0.8 - 0.6 * float(np.exp(-0.3 * l))
                V.tensor_tensor(p1[:, l, nl:nl + 1], lam_e[:, 2 * l + 1:2 * l + 2], lam_e[:, 2 * l:2 * l + 1], ALU.subtract)
                V.drain()
                V.tensor_scalar(p1[:, l, nl:nl + 1], p1[:, l, nl:nl + 1], init, None, ALU.subtract)
                V.tensor_scalar(p1[:, l, sub:sub + 1], p1[:, l, sub:sub + 1], 1.0 - init, None, ALU.mult)
            V.drain()
            dve.wait_ge(*s0["act"].upto("sin"))
            V.tensor_copy(sinM, angs[:, 0:T2])
            V.tensor_tensor(cosM, angs[:, T2:2 * T2], angs[:, T2:2 * T2], ALU.mult)
            V.drain()
            V.tensor_scalar(cosM, cosM, -2.0, 1.0, ALU.mult, ALU.add)
            V.drain()
            with dve.Fori(0, DEPTH) as layer:
                V.tensor_copy(cur[:, 0:NPAR1], par1_sb[:, bass.ds(layer * NPAR1, NPAR1)])
                fence((layer_begin, 1))
                norm(s1, "mix", X1, lambda k: par("gmix", k), HN1, T1, lambda k: s1["hn"].done(k))
                for key in TILES_HG:
                    settle(key)
                    if key == ("hi", 1):
                        dve.wait_ge(*s1["lnf"].upto())
                        for h in range(HG_HEADS):
                            V.tensor_tensor_scan(HC[:, h, :], restart[:, :], HC[:, h, :], 0.0, ALU.mult, ALU.add)
                        fence(s1["cum"].done())
                for key in TILES_RET:
                    settle(key)
                    if key == ("rq", 0):
                        hg_differences(0)
                    if key == ("rv", 0):
                        dve.wait_ge(*s1["e1"].upto())
                        hg_factors(0)
                da, before = list(TILES_DA), None

                def next_tile(before):
                    if before is not None:
                        settle(before)
                    return da.pop(0)

                for h in range(HG_HEADS):
                    hg_weights(h)
                    if h + 1 < HG_HEADS:
                        hg_differences(h + 1)
                    before = next_tile(before)
                    if h + 1 < HG_HEADS:
                        hg_factors(h + 1)
                    before = next_tile(before)
                    before = next_tile(before)
                    normalise("h", h)
                settle(before)
                for h in range(RET_HEADS):
                    retention_weights(h)
                    merge(1, 2 * h)
                    merge(1, 2 * h + 1)
                    normalise("r", h)
                da_masked(0)
                da_combined(0)
                for h in range(DA_HEADS):
                    if h + 1 < DA_HEADS:
                        da_masked(h + 1)
                    if h > 0:
                        normalise("d", h - 1)
                    if h + 1 < DA_HEADS:
                        da_combined(h + 1)
                    merge(0, h)
                normalise("d", 7)
                for j in range(KT):
                    merge(2, j)
                for j in range(KT):
                    add_to_x(b1, s1, X1, ("wo", j), j, T1)
                norm(s1, "ffn", X1, lambda k: par("gffn", k), HN1, T1, lambda k: s1["hn"].done(("ffn", k)))
                for j in range(FT):
                    conv(j, 0)
                    fence(s1["gated"].done(("ff", j)))
                    conv(j, 1)
                    V.drain()
                    dve.wait_ge(*s1["sg"].upto(("ff", j)))
                    V.tensor_tensor(CG[:, j % 2, :], CG[:, j % 2, :], SG[:, j % 2, :], ALU.mult)
                    V.drain()
                    V.tensor_tensor(FF[:, j, :], CG[:, j % 2, :], CV[:, j % 2, :], ALU.mult)
                    fence(s1["ff"].done(j))
                for j in range(KT):
                    add_to_x(b1, s1, X1, ("down", j), j, T1)
                dve.wait_ge(layer_end, 2 * layer + 2)
                dve.sem_inc(dve_in)
                for x in list(s1.values()):
                    dve.sem_clear(x.sem)
                for x in bank_full + bank_free:
                    dve.sem_clear(x)

            fence((layer_begin, 1))
            dve.wait_ge(*sm["rs"].upto(0))
            for k in range(KT):
                V.scalar_tensor_tensor(X2[:, k, :], X1[:, k, N_META:T1], fin_sb[:, k:k + 1], RS[:, 0:T2], ALU.mult, ALU.mult)
            V.drain()
            for x in bank_full + bank_free:
                dve.sem_clear(x)

            def attention_masked(kind, h):
                dve.wait_ge(*b2.full((kind, "sc", h)))
                ps, s = b2.of((kind, "sc", h)), SC2[:, h % 2, :]
                if kind == "m":
                    V.scalar_tensor_tensor(s[:, 0:P], ps[:, 0:P], MLA_QK ** -0.5, causal[:, 2 * P:3 * P], ALU.mult, ALU.add)
                    V.scalar_tensor_tensor(s[:, P:3 * P], ps[:, P:3 * P], MLA_QK ** -0.5, causal[:, P:3 * P], ALU.mult, ALU.add)\
                        .then_inc(*b2.free((kind, "sc", h)))
                else:
                    V.scalar_tensor_tensor(s, ps[:, 0:3 * P], 64 ** -0.5, BS[:, :], ALU.mult, ALU.add)\
                        .then_inc(*b2.free((kind, "sc", h)))
                V.drain()
                c = 32 + 8 * (h % 2)
                V.tensor_reduce(small[:, c:c + 1], s[:, 0:P], AXX, ALU.max, negate=True)
                V.tensor_reduce(small[:, c + 1:c + 2], s[:, P:3 * P], AXX, ALU.max, negate=True)
                fence(s2["sc"].done((kind, h)))

            def attention_combined(kind, h):
                dve.wait_ge(*s2["expd"].upto((kind, h)))
                c = 32 + 8 * (h % 2)
                V.reciprocal(small[:, c + 4:c + 6], small[:, c + 2:c + 4])
                V.drain()
                if h >= 2:
                    dve.wait_ge(*b2.full((kind, "t", h - 2)))
                for i, cols in enumerate((slice(0, P), slice(P, 3 * P))):
                    V.tensor_scalar(W2[:, h % 2, cols], SC2[:, h % 2, cols], small[:, c + 4 + i:c + 5 + i], None, ALU.mult)
                fence(s2["w"].done((kind, h)))

            def merge_two(n, j):
                dve.wait_ge(*s2["sigm"].upto((n, j)))
                dve.wait_ge(*b2.full(("mB", n, j)))
                first = n == MERGE2[0]
                dst = Y2[:, j, :] if first else TP2[:, 0, 0:T2]
                V.tensor_tensor(dst, SGM[:, j % 2, :], b2.of(("mB", n, j))[:, 0:T2], ALU.mult).then_inc(*b2.free(("mB", n, j)))
                V.drain()
                if not first:
                    V.tensor_tensor(Y2[:, j, :], Y2[:, j, :], TP2[:, 0, 0:T2], ALU.add)
                fence(s2["y"].done((n, j)))

            with dve.Fori(0, DEPTH) as layer:
                V.tensor_copy(cur[:, 0:NPAR2], par2_sb[:, bass.ds(layer * NPAR2, NPAR2)])
                V.memset(KR[0:MLA_NOPE, :], 0.0)
                fence((layer_begin, 1))
                norm(s2, "att", X2, lambda k: parb("gatt", k), HN2, T2, lambda k: s2["hn"].done(("att", k)))
                dve.wait_ge(*s2["rs"].upto("q"))
                dve.wait_ge(*s2["evac"].upto("cq1"))
                for i in range(2):
                    V.scalar_tensor_tensor(CQ[:, i, :], CQ[:, i, :], parb("gq", i), RS[:, 0:T2], ALU.mult, ALU.mult)
                fence(s2["cqn"].done())
                dve.wait_ge(*s2["rs"].upto("kv"))
                V.scalar_tensor_tensor(CKV[:, :], CKV[:, :], parb("gkv"), RS[:, 0:T2], ALU.mult, ALU.mult)
                fence(s2["ckn"].done())
                for i in range(2):
                    dve.wait_ge(*b2.full(f"cx{i}"))
                    dve.wait_ge(*s2["evac"].upto(f"cc{i}"))
                    V.tensor_tensor(SI[:, i, :], SI[:, i, :], b2.of(f"cx{i}")[:, 0:T2], ALU.mult).then_inc(*b2.free(f"cx{i}"))
                    V.drain()
                    V.tensor_scalar(OC[:, i, :], SI[:, i, :], parb("cw", 4 + i), None, ALU.mult)
                    V.drain()
                    V.scalar_tensor_tensor(OC[:, i, 1:T2], SI[:, i, 0:T2 - 1], parb("cw", 2 + i), OC[:, i, 1:T2], ALU.mult, ALU.add)
                    V.drain()
                    V.scalar_tensor_tensor(OC[:, i, 2:T2], SI[:, i, 0:T2 - 2], parb("cw", i), OC[:, i, 2:T2], ALU.mult, ALU.add)
                    V.drain()
                    V.tensor_tensor(OC[:, i, :], OC[:, i, :], SB[:, i, :], ALU.mult)
                fence(s2["oc"].done())
                dve.wait_ge(*b2.full(("qu", 0)))
                sw = (3 % RING) * SLAB * P + 2 * MLA_HEADS * MLA_QK + MLA_HEADS * P
                V.tensor_copy(WG[0:16, :], ring[0:16, sw:sw + P])
                fence(s2["mlaw"].done())
                cM, sM = cosM[MLA_NOPE:MLA_QK, :], sinM[MLA_NOPE:MLA_QK, :]
                dve.wait_ge(*s2["evac"].upto("kr"))
                r = slice(MLA_NOPE, MLA_QK)
                V.tensor_tensor(TP2[r, 0, 0:T2], KR[r, :], cM, ALU.mult)
                dve.wait_ge(*b2.full("kturn"))
                V.tensor_tensor(TP2[r, 1, 0:T2], b2.of("kturn")[r, 0:T2], sM, ALU.mult).then_inc(*b2.free("kturn"))
                V.drain()
                for h in range(MLA_HEADS):
                    V.tensor_tensor(KM[r, h, :], TP2[r, 0, 0:T2], TP2[r, 1, 0:T2], ALU.add)
                V.drain()
                for p in range(2):
                    dve.wait_ge(*b2.full(("qturn", p)))
                    ps = b2.of(("qturn", p))
                    for i in range(2):
                        q = QM[r, 2 * p + i, :]
                        V.tensor_tensor(TP2[r, i, 0:T2], q, cM, ALU.mult)
                        ins = V.tensor_tensor(TP2[r, i, T2:2 * T2], ps[r, i * T2:(i + 1) * T2], sM, ALU.mult)
                        if i:
                            ins.then_inc(*b2.free(("qturn", p)))
                        V.drain()
                        V.tensor_tensor(q, TP2[r, i, 0:T2], TP2[r, i, T2:2 * T2], ALU.add)
                    V.drain()
                dve.wait_ge(*s2["evac"].upto(("ku", 1)))
                fence(s2["km"].done())
                for i in range(2):
                    dve.wait_ge(*s2["sg"].upto(i))
                    V.tensor_tensor(GG[:, i, :], SGM[:, i, :], b2.of(f"gr{i}")[:, 0:T2], ALU.mult).then_inc(*b2.free(f"gr{i}"))
                fence(s2["gated"].done())
                dve.wait_ge(*b2.full("gl"))
                V.tensor_scalar(GC[:, :], b2.of("gl")[:, 0:T2], parb("bg"), None, ALU.add).then_inc(*b2.free("gl"))
                V.drain()
                for i in range(2):
                    kn = (i + 1) * P
                    dst = IS[:, i * P:i * P + kn]
                    for c in range(4):
                        seq = 4 * i + c
                        dve.wait_ge(*s2["relu"].upto(seq))
                        for g in range(2):
                            before = causal[:, (2 - i) * P:(2 - i) * P + kn] if c + g == 0 else dst
                            head = c + 4 * g
                            V.scalar_tensor_tensor(dst, REL[:, seq % 2, g * kn:(g + 1) * kn], IW[:, i, head:head + 1], before,
                                                   ALU.mult, ALU.add)
                            V.drain()
                        V.drain().then_inc(*s2["used"].done(seq))
                V.tensor_scalar(GE[:, :], GC[:, :], 0.0, None, ALU.max)
                V.drain()
                V.scalar_tensor_tensor(GE[:, :], GC[:, :], 0.0, GE[:, :], ALU.min, ALU.subtract)
                fence(s2["gz"].done())
                attention_masked("m", 0)
                V.tensor_scalar(GC[:, :], GC[:, :], 0.0, None, ALU.min)
                V.drain()
                dve.wait_ge(*s2["gez"].upto())
                V.tensor_tensor(GC[:, :], GC[:, :], GE[:, :], ALU.subtract)
                V.drain()
                V.tensor_scalar(GC[:, :], GC[:, :], 1.0 / 16.0, None, ALU.mult)
                V.drain()
                V.tensor_tensor_scan(GC[:, :], restart[:, 0:T2], GC[:, :], 0.0, ALU.mult, ALU.add)
                V.drain()
                level_differences(GC[:, :], Z2, LV, T2, None)
                V.tensor_scalar(Z2[:, 3, 0:P], GC[:, 0:P], GC[:, P - 1:P], -1.0, ALU.subtract, ALU.mult)
                V.tensor_copy(Z2[:, 3, P:T2], GC[:, P:T2])
                fence(s2["zdiff"].done())
                attention_combined("m", 0)
                dve.wait_ge(*s2["zexp"].upto())
                dve.wait_ge(*s2["evac"].upto("gk"))
                level_factors(Z2, LV, T2, GQ, GK)
                V.tensor_tensor(Z2[:, 3, 0:P], Z2[:, 3, 0:P], GK[:, 0:P], ALU.mult)
                V.tensor_tensor(Z2[:, 3, P:T2], Z2[:, 3, P:T2], GQ[:, P:T2], ALU.mult)
                fence(s2["z"].done())
                for h in range(MLA_HEADS):
                    if h + 1 < MLA_HEADS:
                        attention_masked("m", h + 1)
                    merge_two(1, 2 * h)
                    if h + 1 < MLA_HEADS:
                        attention_combined("m", h + 1)
                    merge_two(1, 2 * h + 1)
                for g in range(GLA_HEADS):
                    dve.wait_ge(*b2.full(("m", "o", 1) if g < 2 else ("g", "o", g - 2)))
                    for t, cols in ((0, slice(0, P)), (1, slice(T2, T2 + P))):
                        for gg in range(2):
                            dve.wait_ge(*b2.full(("lv", g, t, gg)))
                            V.tensor_tensor(LT2[:, 4 * gg:4 * gg + 4, :],
                                            b2.of(("lv", g, t, gg)).rearrange("p (a b) -> p a b", b=P),
                                            lvl[:, 4 * gg:4 * gg + 4, :], ALU.mult).then_inc(*b2.free(("lv", g, t, gg)))
                        V.drain()
                        V.tensor_reduce(SS[:, g % 2, cols], LT2[:, :, :].rearrange("p a b -> p b a"), AXX, ALU.add)
                        V.drain()
                    dve.wait_ge(*b2.full(("cross", g)))
                    V.tensor_copy(SS[:, g % 2, P:T2], b2.of(("cross", g))[:, 0:P]).then_inc(*b2.free(("cross", g)))
                    fence(s2["att"].done(g))
                    merge_two(0, 2 * g)
                    merge_two(0, 2 * g + 1)
                    if g % 2 == 0:
                        i = g // 2
                        kn = (i + 1) * P
                        row = IS[:, i * P:i * P + kn]
                        for _ in range(TOPK // 8):
                            V.max(TOP[:, :], row)
                            V.drain()
                            V.match_replace(row, TOP[:, :], row, -3e38)
                            V.drain()
                        V.tensor_scalar(row, row, -2e38, NEG, ALU.is_gt, ALU.mult)
                        V.drain()
                        V.tensor_tensor(BS[:, i * P:i * P + kn], row, causal[:, (2 - i) * P:(2 - i) * P + kn], ALU.add)
                        V.drain()
                    if g % 2:
                        p = g // 2
                        dve.wait_ge(*s2["rs"].upto(("g", p)))
                        V.scalar_tensor_tensor(TP2[:, 1, 0:T2], GO[:, p, :], parb("ggla"), RS[:, 0:T2], ALU.mult, ALU.mult)
                        V.drain()
                        V.tensor_tensor(GG[:, p, :], GG[:, p, :], TP2[:, 1, 0:T2], ALU.mult)
                        fence(s2["normed"].done(p))
                attention_masked("s", 0)
                attention_combined("s", 0)
                for h in range(DSA_HEADS):
                    if h + 1 < DSA_HEADS:
                        attention_masked("s", h + 1)
                    merge_two(3, 2 * h)
                    if h + 1 < DSA_HEADS:
                        attention_combined("s", h + 1)
                    merge_two(3, 2 * h + 1)
                for j in range(KT):
                    merge_two(2, j)
                for j in range(KT):
                    add_to_x(b2, s2, X2, ("wo", j), j, T2)
                norm(s2, "ffn", X2, lambda k: parb("gffn", k), HN2, T2, lambda k: s2["hn"].done(("ffn", k)))
                for j in range(FT):
                    dve.wait_ge(*s2["sigf"].upto(j))
                    V.tensor_tensor(TP2[:, 0, 0:T2], SGM[:, j % 2, :], b2.of(("ff", j, 0))[:, 0:T2], ALU.mult)\
                        .then_inc(*b2.free(("ff", j, 0)))
                    V.drain()
                    dve.wait_ge(*b2.full(("ff", j, 1)))
                    V.tensor_tensor(FF2[:, j, :], TP2[:, 0, 0:T2], b2.of(("ff", j, 1))[:, 0:T2], ALU.mult)\
                        .then_inc(*b2.free(("ff", j, 1)))
                    fence(s2["ff"].done(j))
                for j in range(KT):
                    add_to_x(b2, s2, X2, ("down", j), j, T2)
                dve.wait_ge(layer_end, 2 * layer + 2 * DEPTH + 2)
                dve.sem_inc(dve_in)
                for x in list(s2.values()):
                    dve.sem_clear(x.sem)
                for x in bank_full + bank_free:
                    dve.sem_clear(x)
            fence((layer_begin, 1))
            dve.wait_ge(*se["rs"].upto(0))
            for k in range(KT):
                V.scalar_tensor_tensor(OUT2[:, k, :], X2[:, k, :], fin_sb[:, KT + k:KT + k + 1], RS[:, 0:T2], ALU.mult, ALU.mult)
            fence(se["x"].done())

        @block.sync
        def _(sp):
            sp.dma_start(x_sb[:, :], x_meta).then_inc(inputs_in, 16)
            sp.dma_start(cst[:, :], consts).then_inc(inputs_in, 16)
            sp.dma_start(par1_sb[:, :].rearrange("p (l n) -> p l n", n=NPAR1)[:, :, 0:NPAR1_IN], par1).then_inc(inputs_in, 16)
            sp.dma_start(lb_sb, lb).then_inc(inputs_in, 16)
            sp.dma_start(lam_sb, lam.to_broadcast([P, DEPTH * 256])).then_inc(inputs_in, 16)
            sp.dma_start(fin_sb[:, 0:KT], final1).then_inc(inputs_in, 16)
            sp.dma_start(fin_sb[:, KT:2 * KT], final2).then_inc(inputs_in, 16)
            sp.dma_start(par2_sb[:, :], par2).then_inc(inputs_in, 16)
            sp.dma_start(pos_sb[:, :], positions.to_broadcast([P, T2])).then_inc(inputs_in, 16)
            for slot in range(RING):
                sp.sem_inc(slab_used[slot])
            rounds = DEPTH * SLABS1 // RING
            with sp.Fori(0, rounds) as r:
                for slot in range(RING):
                    sp.wait_ge(slab_used[slot], r + 1)
                    sp.dma_start(ring[:, slot * SLAB * P:(slot + 1) * SLAB * P],
                                 w1[bass.ds(r * RING + slot, 1), :, :].rearrange("a p n -> p (a n)")).then_inc(slab_loaded[slot], 16)
            with sp.Fori(0, DEPTH * SLABS2 // RING) as r:
                for slot in range(RING):
                    sp.wait_ge(slab_used[slot], r + rounds + 1)
                    sp.dma_start(ring[:, slot * SLAB * P:(slot + 1) * SLAB * P],
                                 w2[bass.ds(r * RING + slot, 1), :, :].rearrange("a p n -> p (a n)")).then_inc(slab_loaded[slot], 16)
            sp.wait_ge(*se["x"].upto())
            sp.dma_start(out, x_sb[:, 0:KT * T2]).then_inc(out_written, 16)
            sp.wait_ge(out_written, 16)


def feature_rows(a):
    a = a.reshape(a.shape[:-1] + (a.shape[-1] // P, P))
    return np.ascontiguousarray(np.moveaxis(a, -1, 0))


def packed(blocks, slabs):
    a = np.zeros((slabs * SLAB, P, P), np.float32)
    for i, b in enumerate(blocks):
        a[i] = b
    return a.reshape(slabs, SLAB, P, P).transpose(0, 2, 1, 3).reshape(slabs, P, SLAB * P)


def tile_blocks(w, column, rows=None):
    return [w[k * P:(k + 1) * P, column:column + P] for k in range(w.shape[0] // P)]


def weights1(w_in, w_branch, w_out, w_ffn_in, w_ffn_out):
    n = {"hq": "hq", "hf": "hf", "hi": "hi", "hg": "hg", "rq": "rq", "rk": "rk", "rv": "rv", "rg": "rg", "dq": "dq",
         "dk": "dk", "dv": "dv"}
    layers = []
    for l in range(DEPTH):
        b = []
        for kind, h in TILES_HG + TILES_RET + TILES_DA:
            b += tile_blocks(w_in[l], IN1[n[kind]] + h * P)
        for branch in MERGE1:
            for j in range(KT):
                b += tile_blocks(w_in[l], IN1["mg"] + branch * D_MODEL + j * P) + tile_blocks(w_branch[l, branch], j * P)
        for j in range(KT):
            b += tile_blocks(w_out[l], j * P)
        for j in range(FT):
            b += tile_blocks(w_ffn_in[l], j * P) + tile_blocks(w_ffn_in[l], D_FF + j * P)
        for j in range(KT):
            b += tile_blocks(w_ffn_out[l], j * P)
        layers.append(packed(b, SLABS1))
    return np.concatenate(layers)


def weights2(w_in, q_up, kv_up, gate_up, w_branch, w_out, w_gate, w_up, w_down):
    layers = []
    for l in range(DEPTH):
        head = np.zeros((HEAD2, P, SLAB * P), np.float32)
        for k, column in enumerate(WIDE2):
            if column is None:
                at = 2 * MLA_HEADS * MLA_QK
                head[k, :, 0:at] = q_up[l].reshape(2, P, at // 2).transpose(1, 0, 2).reshape(P, at)
                head[k, :, at:at + 512] = kv_up[l]
                head[k, 0:16, at + 512:at + 640] = gate_up[l]
            else:
                head[k] = w_in[l][:, column:column + 512].reshape(KT, P, 512).transpose(1, 0, 2).reshape(P, KT * 512)
        b = []
        for branch in MERGE2:
            for j in range(KT):
                b += tile_blocks(w_in[l], IN2["mg"] + branch * D_MODEL + j * P) + tile_blocks(w_branch[l, branch], j * P)
        for j in range(KT):
            b += tile_blocks(w_out[l], j * P)
        for j in range(FT):
            b += tile_blocks(w_gate[l], j * P) + tile_blocks(w_up[l], j * P)
        for j in range(KT):
            b += tile_blocks(w_down[l], j * P)
        layers.append(np.concatenate([head, packed(b, SLABS2 - HEAD2)]))
    return np.concatenate(layers)


def kernel(x, meta, norm_mix_g, w_in, w_branch, w_out, hg_lb, da_lambda, da_subln_g, norm_ffn_g, w_ffn_in, ffn_conv_w,
           ffn_conv_b, w_ffn_out, norm_final_g, positions_2, attn_norm_g_2, w_in_2, mla_q_norm_g_2, mla_w_q_up_2,
           mla_kv_norm_g_2, mla_w_kv_up_2, conv_w_2, gla_w_gate_up_2, gla_b_gate_2, gla_norm_g_2, w_branch_2, w_out_2,
           ffn_norm_g_2, w_ffn_gate_2, w_ffn_up_2, w_ffn_down_2, final_norm_g_2):
    import concourse.bacc as bacc
    from concourse.bass_utils import run_bass_kernel_spmd

    g = lambda a: np.asarray(a)
    x, meta = g(x), g(meta)
    arrays = {
        "x_meta": feature_rows(np.concatenate([meta, x[0]])).transpose(0, 2, 1).reshape(P, KT * T1),
        "w1": weights1(g(w_in), g(w_branch), g(w_out), g(w_ffn_in), g(w_ffn_out)),
        "par1": np.concatenate([feature_rows(g(a)).reshape(P, DEPTH, -1) for a in
                                (norm_mix_g, norm_ffn_g, ffn_conv_w, ffn_conv_b, da_subln_g)], 2),
        "lb": feature_rows(g(hg_lb)).reshape(P, DEPTH * KT),
        "lam": g(da_lambda).reshape(1, DEPTH * 256),
        "final1": feature_rows(g(norm_final_g)),
        "w2": weights2(g(w_in_2), g(mla_w_q_up_2), g(mla_w_kv_up_2), g(gla_w_gate_up_2), g(w_branch_2), g(w_out_2),
                       g(w_ffn_gate_2), g(w_ffn_up_2), g(w_ffn_down_2)),
        "par2": np.concatenate([feature_rows(g(a)).reshape(P, DEPTH, -1) for a in
                                (attn_norm_g_2, ffn_norm_g_2, mla_q_norm_g_2, mla_kv_norm_g_2, conv_w_2, gla_b_gate_2)]
                               + [feature_rows(np.concatenate([g(gla_norm_g_2)] * 2, -1)).reshape(P, DEPTH, -1)],
                               2).reshape(P, DEPTH * NPAR2),
        "positions": g(positions_2),
        "final2": feature_rows(g(final_norm_g_2)),
        "consts": constants(),
    }
    arrays = {n: np.ascontiguousarray(a) for n, a in arrays.items()}
    known = {}
    for _ in range(2):
        nc = bacc.Bacc("TRN2", target_bir_lowering=False, num_devices=1)
        args = [nc.dram_tensor(n, a.shape, mybir.dt.from_np(a.dtype), kind="ExternalInput").ap() for n, a in arrays.items()]
        out = nc.dram_tensor("out", (P, KT * T2), F32, kind="ExternalOutput").ap()
        program(nc, *args, out, known)
    r = run_bass_kernel_spmd(nc, [arrays], core_ids=[0])
    return r.results[0]["out"].reshape(P, KT, T2).transpose(2, 1, 0).reshape(1, T2, D_MODEL)
```

```python
from contextlib import ExitStack

import concourse.bass as bass
import numpy as np
from concourse import mybir

F32 = mybir.dt.float32
F32R = mybir.dt.float32r
I32 = mybir.dt.int32
ALU = mybir.AluOpType
ACT = mybir.ActivationFunctionType
AXX = mybir.AxisListType.X

P = 128
DEPTH = 2
D_MODEL = 1024
KT = D_MODEL // P
N_META = 16
SEQ = 256
T1 = N_META + SEQ
T2 = SEQ
D_FF = 2816
FT = D_FF // P
EPS = 1e-6
NEG = -1e30
LB_FLOOR = 1e-30
THETA = 10000.0
SLAB = 8
RING = 4
RET_HEADS, HG_HEADS, DA_HEADS = 4, 8, 8
MLA_HEADS, MLA_QK, MLA_NOPE = 4, 96, 64
GLA_HEADS, GLA_DK = 4, 32
DSA_HEADS, IDX_HEADS, TOPK = 4, 8, 64
IN1 = dict(rq=0, rk=512, rv=1024, rg=2048, hq=3072, hf=4096, hi=5120, hg=6144, dq=7168, dk=8192, dv=9216, mg=10240)
IN2 = dict(cq=0, ckv=256, krope=384, cb=416, cc=672, cx=928, dq=1184, dk=1440, dv=1504, iq=1568, ik=1824, iw=1856,
           gq=1864, gk=1992, gv=2120, glr=2376, gr=2392, mg=2648)
LEVELS = [64, 32, 16, 8, 4, 2, 1]

TILES_HG = [("hq", h) for h in range(8)] + [("hf", h) for h in range(8)] + [("hi", h) for h in range(8)] \
    + [("hg", h) for h in range(8)]
TILES_RET = [("rq", h) for h in range(4)] + [("rk", h) for h in range(4)] + [("rv", h) for h in range(8)]
TILES_DA = [("dq", h) for h in range(8)] + [("dk", h) for h in range(8)] + [("dv", h) for h in range(8)]
VALUES = ("hi", "rv", "dv")
TILES_FILL = []
for _h in range(8):
    TILES_FILL += [t for t in TILES_RET + TILES_DA if t[0] not in VALUES][3 * _h:3 * _h + 3]
    TILES_FILL += [t for t in TILES_RET + TILES_DA if t[0] in VALUES][2 * _h:2 * _h + 2]
TILES_RG = [("rg", h) for h in range(8)]
MERGE1 = [1, 0, 2]
MERGE2 = [1, 0, 3, 2]
BLOCKS1 = 13312 // P * KT + 3 * KT * KT + KT * KT + 2 * FT * KT + FT * KT
SLABS1 = -(-BLOCKS1 // (SLAB * RING)) * RING
BLOCKS2 = 207 + 4 * KT * (KT + 2) + KT * KT + 2 * FT * KT + FT * KT
SLABS2 = -(-BLOCKS2 // (SLAB * RING)) * RING

CONST = {}
_at = 0
for _name, _n in [("cosR", T1), ("sinR", T1), ("cosD", T1), ("sinD", T1), ("rotR", P), ("rotD", P), ("rotM", P),
                  ("retD", RET_HEADS * T1), ("lvl", 8 * P), ("causal", 3 * P), ("ident", P), ("ones", P),
                  ("ones64", P), ("restart", T1), ("invM", 1), ("eps", 1), ("one", 1)]:
    CONST[_name] = (_at, _n)
    _at += _n
NCONST = _at
PAR1 = {}
_at = 0
for _name, _n in [("gmix", KT), ("gffn", KT), ("cw", 3 * 2 * FT), ("cb", 2 * FT), ("sub", 1), ("nlam", 1), ("omlb", KT),
                  ("lbf", KT)]:
    PAR1[_name] = (_at, _n)
    _at += _n
NPAR1, NPAR1_IN = _at, PAR1["nlam"][0]
PAR2 = {}
_at = 0
for _name, _n in [("gatt", KT), ("gffn", KT), ("gq", 2), ("gkv", 1), ("cw", 6), ("bg", 1), ("ggla", 1)]:
    PAR2[_name] = (_at, _n)
    _at += _n
NPAR2 = _at


ROUND = 12582912.0
TWO_PI = [6.28125, 0.0019350051879882812, 3.0199157663446432e-07]
ARENA = 27736
N_INPUTS = 9


def constants():
    c = np.zeros((P, NCONST), np.float32)

    def put(name, a):
        at, n = CONST[name]
        c[:a.shape[0], at:at + n] = a.reshape(a.shape[0], n)

    def angles(d, copies):
        inv = np.float32(THETA) ** (-np.arange(0, d, 2, dtype=np.float32) / np.float32(d))
        ang = (np.arange(T1, dtype=np.float32)[None, :] * inv.astype(np.float32)[:, None]).astype(np.float32)
        return np.tile(ang, (2 * copies, 1)).astype(np.float64)

    def rotation(d, starts):
        r = np.zeros((P, P))
        for s in starts:
            for i in range(d // 2):
                r[s + i + d // 2, s + i] = -1.0
                r[s + i, s + i + d // 2] = 1.0
        return r

    put("cosR", np.cos(angles(128, 1)))
    put("sinR", np.sin(angles(128, 1)))
    put("cosD", np.cos(angles(64, 2)))
    put("sinD", np.sin(angles(64, 2)))
    put("rotR", rotation(128, [0]))
    put("rotD", rotation(64, [0, 64]))
    put("rotM", rotation(32, [MLA_NOPE]))
    k, j = np.arange(P)[:, None], np.arange(T1)[None, :]
    dec = [np.where(j >= k, (1 - 2.0 ** (-5 - h)) ** np.maximum(j - k, 0), 0.0) * 128 ** -0.5 for h in range(RET_HEADS)]
    put("retD", np.stack(dec, 1))
    kk, qq = np.arange(P)[:, None], np.arange(P)[None, :]
    lv = [(kk // s % 2 == 0) & (qq // s == kk // s + 1) for s in LEVELS] + [kk == qq]
    put("lvl", np.stack(lv, 1).astype(np.float32))
    put("causal", np.where(np.arange(3 * P)[None, :] <= kk + 2 * P, 0.0, NEG))
    put("ident", np.eye(P))
    put("ones", np.ones((P, P)))
    put("ones64", (kk // 64 == qq // 64).astype(np.float32))
    put("restart", np.tile((np.arange(T1) % P != 0).astype(np.float32), (P, 1)))
    inv = np.zeros((P, 1), np.float32)
    inv[MLA_NOPE:MLA_QK, 0] = np.tile(np.float32(THETA) ** (-np.arange(16, dtype=np.float32) / np.float32(16)), 2)
    put("invM", inv)
    put("eps", np.full((P, 1), EPS))
    put("one", np.ones((P, 1)))
    return c


class Signal:

    def __init__(self, sem, known):
        self.sem, self.known, self.count = sem, known, 0

    def done(self, key=0, by=1):
        self.count += by
        self.known[key] = self.count
        return self.sem, by

    def upto(self, key=0):
        return self.sem, self.known.get(key, 1)


class Banks:

    def __init__(self, psum, full, free, known):
        self.psum, self.fulls, self.frees, self.known, self.n = psum, full, free, known, 0

    def take(self, pe, key):
        bank, use = self.n % 8, self.n // 8 + 1
        self.n += 1
        self.known[key] = (bank, use)
        if use > 1:
            pe.wait_ge(self.frees[bank], use - 1)
        return self.psum[:, bank, :]

    def full(self, key):
        bank, use = self.known.get(key, (0, 1))
        return self.fulls[bank], use

    def filled(self, key):
        return self.fulls[self.known[key][0]], 1

    def free(self, key):
        return self.frees[self.known.get(key, (0, 1))[0]], 1

    def of(self, key):
        return self.psum[:, self.known.get(key, (0, 1))[0], :]


def program(nc, x_meta, w1, par1, lb, lam, final1, w2, par2, positions, final2, consts, out, known):
    with ExitStack() as ctx:
        def sb(name, n, dt=F32):
            return ctx.enter_context(nc.sbuf_tensor(name, [P, n], dt))

        def sem(name):
            return ctx.enter_context(nc.semaphore(name))

        psum = ctx.enter_context(nc.psum_tensor("psum", [P, 8, 512], F32))
        x_sb = sb("x_sb", KT * T1)
        def twin(name, n, dt):
            return nc.alloc_sbuf_tensor_at(name, [P, n], dt, offset=nc.sbuf_base - 4 * n)

        hn_hi = sb("hn_hi", KT * T1, F32R)
        hn_sq = twin("hn_sq", KT * T1, F32)
        hn_lo = sb("hn_lo", KT * T1, F32R)
        ring = sb("ring", RING * SLAB * P)
        ring_hi = sb("ring_hi", RING * SLAB * P, F32R)
        ring_lo = sb("ring_lo", RING * SLAB * P, F32R)
        cst = sb("cst", NCONST)
        par1_sb = sb("par1_sb", DEPTH * NPAR1)
        cur = sb("cur", NPAR1)
        par2_sb = sb("par2_sb", DEPTH * NPAR2)
        fin_sb = sb("fin_sb", 2 * KT)
        small = sb("small", 96)
        tab_sb = sb("tab_sb", 2 * T2)
        pos_sb = sb("pos_sb", T2, I32)
        oh_sb = sb("oh_sb", T1)
        arena = sb("arena", ARENA)
        arena_r = twin("arena_r", ARENA, F32R)

        def view(at, *shape):
            n = int(np.prod(shape))
            v = arena[:, at:at + n]
            if len(shape) == 2:
                v = v.rearrange("p (a b) -> p a b", b=shape[1])
            if len(shape) == 3:
                v = v.rearrange("p (a b c) -> p a b c", b=shape[1], c=shape[2])
            return v, at + n

        def split_view(at, *shape):
            n = int(np.prod(shape))
            v = arena_r[:, at:at + n]
            return v.rearrange("p (a b) -> p a b", b=shape[1]) if len(shape) == 2 else v

        def const(name, shape=None):
            at, n = CONST[name]
            v = cst[:, at:at + n]
            return v if shape is None else v.rearrange("p (a b) -> p a b", b=shape)

        X1 = x_sb[:, :].rearrange("p (k t) -> p k t", t=T1)
        H1, L1, Q1 = [t[:, :].rearrange("p (k t) -> p k t", t=T1) for t in (hn_hi, hn_lo, hn_sq)]
        H2, L2, Q2 = [t[:, 0:KT * T2].rearrange("p (k t) -> p k t", t=T2) for t in (hn_hi, hn_lo, hn_sq)]
        OUT2 = x_sb[:, 0:KT * T2].rearrange("p (k t) -> p k t", t=T2)
        cosR, sinR, cosD, sinD = const("cosR"), const("sinR"), const("cosD"), const("sinD")
        rotR, rotD, rotM = const("rotR"), const("rotD"), const("rotM")
        ident, ones, ones64 = const("ident"), const("ones"), const("ones64")
        causal, restart, eps, one = const("causal"), const("restart"), const("eps"), const("one")
        retD, lvl = const("retD", T1), const("lvl", P)

        HQ, a = view(0, KT, T1)
        HK, a = view(a, KT, T1)
        HC, a = view(a, KT, T1)
        HG, a = view(a, KT, T1)
        RQ, a = view(a, 4, T1)
        RK, a = view(a, 4, T1)
        DQ, a = view(a, KT, T1)
        DK, a = view(a, KT, T1)
        SIG2 = view(0, KT, T1)[0]
        RG = view(KT * T1, KT, T1)[0]
        BR = {0: (split_view(KT * T1, KT, T1), split_view(2 * KT * T1, KT, T1)),
              1: (split_view(3 * KT * T1, KT, T1), split_view(0, KT, T1)),
              2: (split_view(5 * KT * T1, KT, T1), split_view(4 * KT * T1, KT, T1))}
        HV, a = view(a, 2, D_MODEL)
        RV, a = view(a, 2, D_MODEL)
        DV, a = view(a, 2, D_MODEL)
        V3, a = view(a, D_MODEL)
        Z, z_end = view(a, 9, T1)
        Y1, _ = view(a, KT, T1)
        a = z_end
        XS, a = view(a, 2, T1)
        SG, a = view(a, 2, T1)
        S0, a = view(a, T1)
        S1, a = view(a, P + N_META)
        S2, a = view(a, N_META)
        RS, a = view(a, T1)
        LT, _ = view(a, 8, P)
        SQ, a = view(a, 2, T1)
        TMP, a = view(a, 2, T1)
        e1_sb, a = view(a, KT)
        YS = split_view(0, KT, T1), split_view(KT * T1, KT, T1)
        assert a <= ARENA, a
        c0 = 3 * KT * T1
        SC = [view(c0, 2, P)[0], view(c0 + 256, 2, 2 * P)[0], view(c0 + 768, 2, T1)[0]]
        WA = [view(c0 + 1312, P)[0], view(c0 + 1440, 2 * P)[0], view(c0 + 1696, T1)[0]]
        FF = split_view(0, FT, T1), split_view(4 * KT * T1, FT, T1)
        CG, b = view(FT * T1, 2, T1)
        CV, b = view(b, 2, T1)
        VT = {"h": (HV, 0), "r": (RV, 32), "d": (DV, 64)}
        ROT = {"rq": (RQ, cosR, sinR, rotR), "rk": (RK, cosR, sinR, rotR),
               "dq": (DQ, cosD, sinD, rotD), "dk": (DK, cosD, sinD, rotD)}

        lb_sb, b = view(0, 2 * KT)
        lb_e, b = view(b, 2 * KT)
        lb_t, b = view(b, KT)
        lam_sb, b = view(b, DEPTH * 4 * 64)
        lam_t, b = view(b, DEPTH * 2 * 64)
        lam_e, b = view(b, DEPTH * 2)
        angs, b = view(b, 2 * T2)
        turns, b = view(b, T2)
        cosM, sinM = tab_sb[:, 0:T2], tab_sb[:, T2:2 * T2]

        X2, a = view(0, KT, T2)
        SGM, a = view(a, 2, T2)
        TP2, a = view(a, 2, 2 * T2)
        FF2 = split_view(a, FT, T2), split_view(a + FT * T2, FT, T2)
        Y2S = split_view(a, KT, T2), split_view(a + KT * T2, KT, T2)

        def split_pair(a, *shape):
            n = int(np.prod(shape))
            return (split_view(a, *shape), split_view(a + n, *shape)), a + 2 * n

        QM, a = view(a, MLA_HEADS, T2)
        KM, a = view(a, MLA_HEADS, T2)
        GO = view(a, 2, T2)[0]
        CQ, a = view(a, 2, T2)
        CQS, a = split_pair(a, 2, T2)
        CKV, a = view(a, T2)
        CKS, a = split_pair(a, T2)
        KR, a = view(a, T2)
        VM, a = view(a, 2, MLA_HEADS * 64)
        Y2, a = view(a, KT, T2)
        OMS, a = split_pair(a, 2, T2)
        SB, a = view(a, 2, T2)
        SI, a = view(a, 2, T2)
        OC, a = view(a, 2, T2)
        OCS, a = split_pair(a, 2, T2)
        QS, a = view(a, 2, T2)
        KS, a = view(a, T2)
        VS, a = view(a, 2, 64)
        SQ2 = view(a, 3, T2)[0]
        OSS, a = split_pair(a, 2, T2)
        IQ, a = view(a, 2, T2)
        IK, a = view(a, T2)
        IW, a = view(a, 2, IDX_HEADS)
        REL, a = view(a, 2, 512)
        IS, a = view(a, 3 * P)
        BS, a = view(a, 3 * P)
        TOP, a = view(a, 8)
        GQ, a = view(a, T2)
        GK, a = view(a, T2)
        GC, a = view(a, T2)
        GE, a = view(a, T2)
        GV, a = view(a, 2, GLA_HEADS * 64)
        GL, a = view(a, T2)
        GLS, a = split_pair(a, T2)
        GG, a = view(a, 2, T2)
        GGS, a = split_pair(a, 2, T2)
        Z2, a = view(a, 8, T2)
        SS, a = view(a, 2, 3 * P)
        LT2, _ = view(a, 8, P)
        SC2, a = view(a, 2, 3 * P)
        W2, a = view(a, 2, 3 * P)
        assert a <= ARENA, a

        def par(name, i=0):
            at = PAR1[name][0] + i
            return cur[:, at:at + 1]

        def parb(name, i=0):
            at = PAR2[name][0] + i
            return cur[:, at:at + 1]

        STAGED = [k for k in TILES_HG + TILES_FILL if k[0] in VALUES or k[0] in ROT]
        s1_slot = {k: i % 2 for i, k in enumerate(STAGED)}

        slab_loaded = [sem(f"slab_loaded{i}") for i in range(RING)]
        slab_hi = [sem(f"slab_hi{i}") for i in range(RING)]
        slab_lo = [sem(f"slab_lo{i}") for i in range(RING)]
        slab_free = [sem(f"slab_free{i}") for i in range(RING)]
        slab_used = [sem(f"slab_used{i}") for i in range(RING)]
        bank_full = [sem(f"bank_full{i}") for i in range(8)]
        bank_free = [sem(f"bank_free{i}") for i in range(8)]
        inputs_in = sem("inputs_in")
        out_written = sem("out_written")
        layer_begin = sem("layer_begin")
        layer_end = sem("layer_end")
        pe_in, act_in, dve_in = sem("pe_in"), sem("act_in"), sem("dve_in")

        def signals(section, names):
            return {n: Signal(sem(section + "_" + n), known.setdefault((section, n), {})) for n in names.split()}

        def banks(section):
            return Banks(psum, bank_full, bank_free, known.setdefault((section, "banks"), {}))

        s0 = signals("start", "act dve")
        s1 = signals("one", "sq rs sqh hn hnlo yb staged taken valued sig_f f_in lnf cum e1 sg gated zdiff zexp z att sqo normed "
                     "sco expd w tr y sigm conv ff x")
        s2 = signals("two", "sq rs hn hnlo evac cqn ckn krn qm km oc sg gated gz gez gl gcum zdiff zexp z att sqo normed "
                     "sc expd w tr o relu used y sigm sigf ff x os gls yb")
        sm = signals("middle", "sq rs x")
        se = signals("end", "sq rs x")
        b1, b2, bm, be = banks("one"), banks("two"), banks("middle"), banks("end")
        block = ctx.enter_context(nc.Block())

        @block.tensor
        def _(pe):
            stream = {"n": 0, "release": None, "layer": None, "first": 0, "per": 0}

            def mm(out_, lhsT, rhs, first, last, done=None):
                i = nc.tensor.matmul(out_, lhsT=lhsT, rhs=rhs, start=first, stop=last)
                if done is not None:
                    i.then_inc(*done)
                elif stream["release"] is not None:
                    i.then_inc(slab_used[stream["release"]], 1)
                    stream["release"] = None

            def weight_block():
                n = stream["n"]
                k = n // SLAB
                if n % SLAB == 0:
                    pe.wait_ge(slab_lo[k % RING], stream["layer"] * stream["per"] + (stream["first"] + k // RING + 1))
                at = (k % RING) * SLAB * P + (n % SLAB) * P
                stream["n"] = n + 1
                return ring_hi[:, at:at + P], ring_lo[:, at:at + P]

            def through():
                if stream["n"] % SLAB == 0:
                    stream["release"] = (stream["n"] // SLAB - 1) % RING

            def product(b, key, rhs, tokens, ready=None, ready_lo=None):
                ps = b.take(pe, key)
                late = []
                count = len(rhs)
                for i, (hi, lo) in enumerate(rhs):
                    w_hi, w_lo = weight_block()
                    if ready is not None:
                        pe.wait_ge(*ready[i])
                    mm(ps[:, 0:tokens], w_hi, hi, i == 0, False)
                    final = ready_lo is None and i == count - 1
                    if ready_lo is None:
                        mm(ps[:, 0:tokens], w_hi, lo, False, False)
                    else:
                        late.append((w_hi, lo, stream["n"]))
                    mm(ps[:, 0:tokens], w_lo, hi, False, final, b.filled(key) if final else None)
                    if ready_lo is None:
                        through()
                for i, (w_hi, lo, n) in enumerate(late):
                    pe.wait_ge(*ready_lo[i])
                    final = i == count - 1
                    mm(ps[:, 0:tokens], w_hi, lo, False, final, b.filled(key) if final else None)
                    if n % SLAB == 0:
                        stream["release"] = (n // SLAB - 1) % RING
                b.known[("end", key)] = stream["n"]

            def finish_stream(slabs):
                used = (stream["n"] - 1) // SLAB
                pe.drain().then_inc(slab_used[used % RING], 1)
                stream["release"] = None
                for k in range(used + 1, slabs):
                    pe.wait_ge(slab_lo[k % RING], stream["layer"] * stream["per"] + (stream["first"] + k // RING + 1))
                    pe.sem_inc(slab_used[k % RING])

            def sum_squares(b, key, tiles, tokens, ready, mat=None):
                ps = b.take(pe, key)
                for i, r in enumerate(tiles):
                    pe.wait_ge(*ready[i])
                    final = i == len(tiles) - 1
                    mm(ps[:, 0:tokens], ones if mat is None else mat, r, i == 0, final, b.filled(key) if final else None)

            def scores(b, key, parts):
                ps = b.take(pe, key)
                for i, (rows, cols, lhsT, rhs) in enumerate(parts):
                    mm(ps[rows, cols], lhsT, rhs, True, True, b.filled(key) if i == len(parts) - 1 else None)

            def transposes(b, key, parts):
                ps = b.take(pe, key)
                for i, (rows, cols, src) in enumerate(parts):
                    t = nc.tensor.transpose(ps[rows, cols], src, ident[0:src.shape[0], 0:src.shape[0]])
                    if i == len(parts) - 1:
                        t.then_inc(*b.filled(key))

            def level_products(b, h, Zv, t, q, k):
                n = P if t < 2 else N_META
                levels = [0, 1, 2, 4, 5, 6, 7] if t < 2 else [4, 5, 6, 7]
                tok = slice(t * P, t * P + n)
                mats = [(Zv[:, z, tok], Zv[:, z, tok]) for z in levels] + [(k[:, tok], q[:, tok])]
                groups = [mats[:4], mats[4:]] if t < 2 else [mats]
                for g, group in enumerate(groups):
                    scores(b, ("lv", h, t, g), [(slice(0, n), slice(i * n, i * n + n), l, r) for i, (l, r) in enumerate(group)])

            def values_times_weights(b, key, V, base, cols, rows=slice(0, P), more=True):
                ps = b.take(pe, key) if more is True else b.of(key)
                mm(ps[rows, 0:T1], V[:, 0, cols], S0[:, :], True, False)
                mm(ps[rows, P:T1], V[:, 1, cols], S1[:, :], False, False)
                mm(ps[rows, 2 * P:T1], V3[base:base + N_META, cols], S2[base:base + N_META, :], False, True, b.filled(key))

            hn1 = [(H1[:, k, :], L1[:, k, :]) for k in range(KT)]
            sq1 = [Q1[:, k, :] for k in range(KT)]
            hn2 = [(H2[:, k, :], L2[:, k, :]) for k in range(KT)]
            sq2 = [Q2[:, k, :] for k in range(KT)]

            def projection(key):
                first = key == ("hq", 0)
                product(b1, key, hn1, T1, [s1["hn"].upto(k) for k in range(KT)] if first else None,
                        [s1["hnlo"].upto(k) for k in range(KT)] if first else None)

            def turn(key):
                kind, h = key
                if kind in ROT:
                    pe.wait_ge(*s1["staged"].upto(key))
                    scores(b1, (kind, h, "turned"), [(slice(0, P), slice(0, T1), ROT[kind][3], XS[:, s1_slot[key], :])])
                elif kind in VALUES:
                    pe.wait_ge(*s1["staged"].upto(key))
                    x = XS[:, s1_slot[key], :]
                    transposes(b1, (kind, h, "turned"),
                               [(slice(0, P), slice(0, P), x[:, 0:P]), (slice(0, P), slice(P, 2 * P), x[:, P:2 * P]),
                                (slice(0, N_META), slice(2 * P, 3 * P), x[:, 2 * P:T1])])

            def project_all(keys, before=None):
                for key in keys:
                    projection(key)
                    if before is not None:
                        turn(before)
                    before = key
                return before

            def merge_a(n, j):
                product(b1, ("mA", n, j), hn1, T1)

            def merge_b(n, j):
                step = [("h", k) if n == 1 else ("r", k // 2) if n == 0 else ("d", k) for k in range(KT)]
                product(b1, ("mB", n, j), [(BR[n][0][:, k, :], BR[n][1][:, k, :]) for k in range(KT)], T1,
                        ready=[s1["normed"].upto(step[k]) for k in range(KT)] if j == 0 else None)

            pe.wait_ge(inputs_in, 16 * N_INPUTS)
            with pe.Fori(0, DEPTH) as layer:
                pe.wait_ge(layer_begin, layer + 1)
                pe.sem_inc(pe_in)
                stream.update(n=0, release=None, layer=layer, first=0, per=SLABS1 // RING)
                sum_squares(b1, "ss_mix", sq1, T1, [s1["sq"].upto(("mix", k)) for k in range(KT)])
                last = project_all(TILES_HG)
                fill = list(TILES_FILL)
                for h in range(HG_HEADS):
                    pe.wait_ge(*s1["z"].upto(h))
                    for t in range(3):
                        level_products(b1, h, Z, t, HQ[:, h, :], HK[:, h, :])
                    scores(b1, ("cross", h), [
                        (slice(0, P), slice(0, P), Z[:, 3, 0:P], Z[:, 3, P:2 * P]),
                        (slice(0, P), slice(P, P + N_META), Z[:, 8, 0:P], Z[:, 8, 2 * P:T1]),
                        (slice(0, P), slice(P + N_META, P + 2 * N_META), Z[:, 8, P:2 * P], Z[:, 8, 2 * P:T1])])
                    for _ in range(3):
                        last = project_all([fill.pop(0)], last)
                    pe.wait_ge(*s1["att"].upto(("h", h)))
                    if h == 0:
                        pe.wait_ge(*s1["valued"].upto(("hi", 7)))
                    values_times_weights(b1, ("o", "h", h), HV, 0, slice(h * P, h * P + P))
                    for _ in range(2):
                        last = project_all([fill.pop(0)], last)
                    sum_squares(b1, ("ss", "h", h), [SQ[:, 0, :]], T1, [s1["sqh"].upto(h)])
                last = project_all(TILES_RG, last)
                pe.wait_ge(*s1["taken"].upto(TILES_FILL[-3]))
                pe.wait_ge(*s1["valued"].upto(TILES_FILL[-1]))
                for h in range(RET_HEADS):
                    scores(b1, ("rs", h, 0), [(slice(0, P), slice(0, T1), RK[:, h, 0:P], RQ[:, h, :])])
                    scores(b1, ("rs", h, 1), [
                        (slice(0, P), slice(0, P + N_META), RK[:, h, P:2 * P], RQ[:, h, P:T1]),
                        (slice(0, N_META), slice(P + N_META, P + 2 * N_META), RK[:, h, 2 * P:T1], RQ[:, h, 2 * P:T1])])
                    merge_a(1, 2 * h)
                    merge_b(1, 2 * h)
                    pe.wait_ge(*s1["att"].upto(("r", h)))
                    for e in range(2):
                        values_times_weights(b1, ("o", "r", 2 * h + e), RV, 32, slice((2 * h + e) * P, (2 * h + e + 1) * P))
                    merge_a(1, 2 * h + 1)
                    sum_squares(b1, ("ss", "r", h), [SQ[:, e, :] for e in range(2)], T1,
                                [s1["sqo"].upto(("r", h, e)) for e in range(2)])
                    merge_b(1, 2 * h + 1)

                def da_scores(h):
                    for m in range(2):
                        q, k = DQ[64 * m:64 * m + 64, h, :], DK[64 * m:64 * m + 64, h, :]
                        scores(b1, ("ds", h, m), [(slice(0, P), slice(0, P), q[:, 0:P], k[:, 0:P]),
                                                  (slice(0, P), slice(P, 3 * P), q[:, P:2 * P], k[:, 0:2 * P])])
                        scores(b1, ("ds", h, 2 + m), [(slice(0, N_META), slice(0, T1), q[:, 2 * P:T1], k)])

                da_scores(0)
                for h in range(DA_HEADS):
                    if h + 1 < DA_HEADS:
                        da_scores(h + 1)
                    merge_a(0, h)
                    if h > 0:
                        sum_squares(b1, ("ss", "d", h - 1), [SQ[:, 0, :]], T1, [s1["sqo"].upto(("d", h - 1, 0))])
                    pe.wait_ge(*s1["w"].upto(h))
                    transposes(b1, ("dt", h), [
                        (slice(0, P), slice(0, P), WA[0][:, :]), (slice(0, P), slice(P, 2 * P), WA[1][:, 0:P]),
                        (slice(0, P), slice(2 * P, T1), WA[2][0:N_META, 0:P]),
                        (slice(0, P), slice(T1, T1 + P), WA[1][:, P:2 * P]),
                        (slice(0, P), slice(T1 + P, T1 + P + N_META), WA[2][0:N_META, P:2 * P]),
                        (slice(0, N_META), slice(T1 + P + N_META, T1 + P + 2 * N_META), WA[2][0:N_META, 2 * P:T1])])
                    merge_b(0, h)
                    merge_a(2, h)
                    pe.wait_ge(*s1["tr"].upto(h))
                    values_times_weights(b1, ("o", "d", h), DV, 64, slice(h * P, h * P + P))
                sum_squares(b1, ("ss", "d", 7), [SQ[:, 0, :]], T1, [s1["sqo"].upto(("d", 7, 0))])
                for j in range(KT):
                    merge_b(2, j)
                for j in range(KT):
                    product(b1, ("wo", j), [(YS[0][:, k, :], YS[1][:, k, :]) for k in range(KT)], T1,
                            ready=[s1["yb"].upto(k) for k in range(KT)] if j == 0 else None)
                sum_squares(b1, "ss_ffn", sq1, T1, [s1["sq"].upto(("ffn", k)) for k in range(KT)])
                for j in range(FT):
                    for half in range(2):
                        product(b1, ("ff", j, half), hn1, T1,
                                ready=[s1["hn"].upto(("ffn", k)) for k in range(KT)] if j + half == 0 else None,
                                ready_lo=[s1["hnlo"].upto(("ffn", k)) for k in range(KT)] if j + half == 0 else None)
                for j in range(KT):
                    product(b1, ("down", j), [(FF[0][:, k, :], FF[1][:, k, :]) for k in range(FT)], T1,
                            ready=[s1["ff"].upto(k) for k in range(FT)] if j == 0 else None)
                finish_stream(SLABS1)
                pe.drain().then_inc(layer_end, 1)

            sum_squares(bm, "ss", [Q1[:, k, N_META:T1] for k in range(KT)], T2, [sm["sq"].upto(k) for k in range(KT)])

            def token_major(keys, n):
                ps = [b2.take(pe, key) for key in keys]
                blocks = max(1, n // P)
                for kt in range(KT):
                    w = [weight_block() for _ in range(blocks)]
                    for c in range(blocks):
                        w_hi, w_lo = w[c]
                        m = min(n, P)
                        for t in range(2):
                            tok = slice(t * P, (t + 1) * P)
                            end = kt == KT - 1
                            dst = ps[t][:, c * P:c * P + m]
                            mm(dst, H2[:, kt, tok], w_hi[:, 0:m], kt == 0 and c == 0, False)
                            mm(dst, L2[:, kt, tok], w_hi[:, 0:m], False, False)
                            mm(dst, H2[:, kt, tok], w_lo[:, 0:m], False, end and c == blocks - 1,
                               b2.filled(keys[t]) if end and c == blocks - 1 else None)
                    through()
                for key in keys:
                    b2.known[("end", key)] = stream["n"]

            def merge2(n, j):
                hi, lo = {0: OMS, 1: OCS, 2: OSS, 3: GGS}[n]
                product(b2, ("mA", n, j), hn2, T2)
                ready = None
                if j == 0:
                    ready = {0: [s2["os"].upto(("m", p)) for p in range(2)], 1: [s2["oc"].upto()] * 2,
                             2: [s2["os"].upto(("s", p)) for p in range(2)], 3: [s2["normed"].upto(p) for p in range(2)]}[n]
                product(b2, ("mB", n, j), [(hi[:, k, :], lo[:, k, :]) for k in range(2)], T2, ready=ready)

            def attention_scores(kind, h):
                if kind == "m":
                    q, k = QM[0:MLA_QK, h, :], KM[0:MLA_QK, h, :]
                else:
                    r = slice(64 * (h % 2), 64 * (h % 2) + 64)
                    q, k = QS[r, h // 2, :], KS[r, :]
                scores(b2, (kind, "sc", h), [(slice(0, P), slice(0, P), q[:, 0:P], k[:, 0:P]),
                                             (slice(0, P), slice(P, 3 * P), q[:, P:T2], k)])

            def attention_turn(kind, h):
                pe.wait_ge(*s2["w"].upto((kind, h)))
                w = W2[:, h % 2, :]
                transposes(b2, (kind, "t", h), [(slice(0, P), slice(i * P, (i + 1) * P), w[:, i * P:(i + 1) * P])
                                                for i in range(3)])

            def values2(kind, h, V):
                key = (kind, "o", h if kind == "g" else h // 2)
                ps = b2.take(pe, key) if h % 2 == 0 or kind == "g" else b2.of(key)
                r = slice(64 * (h % 2), 64 * (h % 2) + 64)
                mm(ps[r, 0:T2], V[:, 0, h * 64:h * 64 + 64] if V is not VS else V[:, 0, :], SS[:, h % 2, 0:T2], True, False)
                mm(ps[r, P:T2], V[:, 1, h * 64:h * 64 + 64] if V is not VS else V[:, 1, :], SS[:, h % 2, T2:3 * P], False, True,
                   b2.filled(key) if h % 2 or kind == "g" else None)

            def index_scores(i):
                if i == 0:
                    pe.wait_ge(*s2["evac"].upto("ik"))
                kn = (i + 1) * P
                for c in range(4):
                    r = slice(32 * c, 32 * c + 32)
                    scores(b2, ("ix", i, c), [(slice(0, P), slice(g * kn, (g + 1) * kn), IQ[r, g, i * P:(i + 1) * P],
                                               IK[r, 0:kn]) for g in range(2)])

            with pe.Fori(0, DEPTH) as layer:
                pe.wait_ge(layer_begin, layer + DEPTH + 2)
                pe.sem_inc(pe_in)
                stream.update(n=0, release=None, layer=layer, first=DEPTH * SLABS1 // RING, per=SLABS2 // RING)
                sum_squares(b2, "ss_att", sq2, T2, [s2["sq"].upto(("att", k)) for k in range(KT)])
                product(b2, "cq0", hn2, T2, [s2["hn"].upto(("att", k)) for k in range(KT)],
                        [s2["hnlo"].upto(("att", k)) for k in range(KT)])
                for key in ("cq1", "ckv", "kr", "cb0", "cb1", "cc0", "cc1"):
                    product(b2, key, hn2, T2)
                sum_squares(b2, "ss_q", [SQ2[:, i, :] for i in range(2)], T2, [s2["evac"].upto(k) for k in ("cq0", "cq1")])
                sum_squares(b2, "ss_kv", [SQ2[:, 2, :]], T2, [s2["evac"].upto("ckv")])
                for key in ("cx0", "cx1", "qs0", "qs1"):
                    product(b2, key, hn2, T2)
                pe.wait_ge(*s2["cqn"].upto())
                for h in range(MLA_HEADS):
                    product(b2, ("qu", h), [(CQS[0][:, k, :], CQS[1][:, k, :]) for k in range(2)], T2)
                pe.wait_ge(*s2["ckn"].upto())
                for h in range(MLA_HEADS):
                    product(b2, ("ku", h), [CKS], T2)
                vu = [b2.take(pe, ("vu", t)) for t in range(2)]
                for c in range(2):
                    w_hi, w_lo = weight_block()
                    for t in range(2):
                        tok = slice(t * P, (t + 1) * P)
                        dst = vu[t][:, c * P:(c + 1) * P]
                        mm(dst, CKS[0][:, tok], w_hi, c == 0, False)
                        mm(dst, CKS[1][:, tok], w_hi, False, False)
                        mm(dst, CKS[0][:, tok], w_lo, False, c == 1, b2.filled(("vu", t)) if c else None)
                    through()
                    b2.known[("end", ("vu", c))] = stream["n"]
                for key in ("ks", "iq0", "iq1", "ik"):
                    product(b2, key, hn2, T2)
                pe.wait_ge(*s2["evac"].upto("kr"))
                scores(b2, "kturn", [(slice(0, MLA_QK), slice(0, T2), rotM[0:MLA_QK, 0:MLA_QK], KR[0:MLA_QK, :])])
                for p in range(2):
                    pe.wait_ge(*s2["evac"].upto(("qu", 2 * p + 1)))
                    scores(b2, ("qturn", p), [(slice(0, MLA_QK), slice(i * T2, (i + 1) * T2), rotM[0:MLA_QK, 0:MLA_QK],
                                               QM[0:MLA_QK, 2 * p + i, :]) for i in range(2)])
                token_major([("vsw", 0), ("vsw", 1)], 64 + IDX_HEADS)
                index_scores(0)
                product(b2, "gq", hn2, T2)
                index_scores(1)
                pe.wait_ge(*s2["km"].upto())
                attention_scores("m", 0)
                product(b2, "gk", hn2, T2)
                token_major([("gv", 0), ("gv", 1)], 2 * P)
                product(b2, "glr", hn2, T2)
                product(b2, "gr0", hn2, T2)
                pe.wait_ge(*s2["gls"].upto())
                product(b2, "gl", [GLS], T2)
                product(b2, "gr1", hn2, T2)
                for h in range(MLA_HEADS):
                    if h + 1 < MLA_HEADS:
                        attention_scores("m", h + 1)
                    merge2(1, 2 * h)
                    attention_turn("m", h)
                    merge2(1, 2 * h + 1)
                    pe.wait_ge(*s2["tr"].upto(("m", h)))
                    values2("m", h, VM)
                pe.wait_ge(*s2["z"].upto())
                for g in range(GLA_HEADS):
                    r = slice(32 * g, 32 * g + 32)
                    for t in range(2):
                        level_products(b2, g, Z2[r, :, :], t, GQ[r, :], GK[r, :])
                    scores(b2, ("cross", g), [(slice(0, P), slice(0, P), Z2[r, 3, 0:P], Z2[r, 3, P:T2])])
                    merge2(0, 2 * g)
                    if g == GLA_HEADS - 1:
                        attention_scores("s", 0)
                    merge2(0, 2 * g + 1)
                    pe.wait_ge(*s2["att"].upto(g))
                    values2("g", g, GV)
                    if g % 2:
                        p = g // 2
                        sum_squares(b2, ("ssg", p), [SQ2[:, p, :]], T2, [s2["sqo"].upto(p)], ones64)
                for h in range(DSA_HEADS):
                    if h + 1 < DSA_HEADS:
                        attention_scores("s", h + 1)
                    merge2(3, 2 * h)
                    attention_turn("s", h)
                    merge2(3, 2 * h + 1)
                    pe.wait_ge(*s2["tr"].upto(("s", h)))
                    values2("s", h, VS)
                for j in range(KT):
                    merge2(2, j)
                for j in range(KT):
                    product(b2, ("wo", j), [(Y2S[0][:, k, :], Y2S[1][:, k, :]) for k in range(KT)], T2,
                            ready=[s2["yb"].upto(k) for k in range(KT)] if j == 0 else None)
                sum_squares(b2, "ss_ffn", sq2, T2, [s2["sq"].upto(("ffn", k)) for k in range(KT)])
                for j in range(FT):
                    for half in range(2):
                        product(b2, ("ff", j, half), hn2, T2,
                                ready=[s2["hn"].upto(("ffn", k)) for k in range(KT)] if j + half == 0 else None,
                                ready_lo=[s2["hnlo"].upto(("ffn", k)) for k in range(KT)] if j + half == 0 else None)
                for j in range(KT):
                    product(b2, ("down", j), [(FF2[0][:, k, :], FF2[1][:, k, :]) for k in range(FT)], T2,
                            ready=[s2["ff"].upto(k) for k in range(FT)] if j == 0 else None)
                finish_stream(SLABS2)
                pe.drain().then_inc(layer_end, 1)
            sum_squares(be, "ss", sq2, T2, [se["sq"].upto(k) for k in range(KT)])

        @block.scalar
        def _(act):
            def op(out_, in_, func, done=None, **kw):
                i = nc.scalar.activation(out_, in_, func, **kw)
                if done is not None:
                    i.then_inc(*done)
                return i

            feeder = {"fed": 0, "slabs": 0, "layer": None, "first": 0}

            def feed_slab():
                k = feeder["fed"]
                feeder["fed"] = k + 1
                slot = slice((k % RING) * SLAB * P, (k % RING + 1) * SLAB * P)
                turn = feeder["layer"] * (feeder["slabs"] // RING) + (feeder["first"] + k // RING + 1)
                act.wait_ge(slab_used[k % RING], turn)
                act.wait_ge(slab_loaded[k % RING], turn * 16)
                nc.scalar.activation(ring_hi[:, slot], ring[:, slot], ACT.Copy).then_inc(slab_hi[k % RING], 1)

            def feed(b, key):
                target = (b.known.get(("end", key), 1) - 1) // SLAB + 3
                while feeder["fed"] <= min(target, feeder["slabs"] - 1):
                    feed_slab()

            def begin_stream(layer, slabs, first):
                feeder.update(fed=0, slabs=slabs, layer=layer, first=first)
                for _ in range(RING):
                    feed_slab()

            def finish_stream():
                while feeder["fed"] < feeder["slabs"]:
                    feed_slab()

            def squares(s, tag, src, dst, ready=None, after=None):
                for k in range(KT):
                    if ready is not None:
                        feed(*after(k))
                        act.wait_ge(*ready(k))
                    op(dst[:, k, :], src[:, k, :], ACT.Square, s["sq"].done((tag, k) if tag else k))

            def log_exp_table():
                nc.scalar.preload_act_table_set("natural_log_exp_and_others")

            def inverse_root(s, b, key, width, tokens, free=None, table=True):
                if table:
                    log_exp_table()
                act.wait_ge(*b.full(key))
                if free is not None:
                    act.wait_ge(*free)
                op(RS[:, 0:tokens], b.of(key)[:, 0:tokens], ACT.Ln, b.free(key), scale=1.0 / width, bias=eps)
                nc.scalar.drain()
                op(RS[:, 0:tokens], RS[:, 0:tokens], ACT.Exp, s["rs"].done(key), scale=-0.5)

            def stage(key):
                kind, h = key
                act.wait_ge(*b1.full(key))
                ps = b1.of(key)[:, 0:T1]
                if kind == "hq":
                    op(HQ[:, h, :], ps, ACT.Copy, b1.free(key))
                elif kind == "hf":
                    op(HC[:, h, :], ps, ACT.Sigmoid)
                    op(HK[:, h, :], ps, ACT.Sigmoid, b1.free(key), scale=-1.0)
                    nc.scalar.drain().then_inc(*s1["sig_f"].done(h))
                elif kind in ("hg", "rg"):
                    if h >= 2 or kind == "rg":
                        act.wait_ge(*s1["gated"].upto((kind, h - 2) if h >= 2 else ("hg", 6 + h)))
                    op(SG[:, h % 2, :], ps, ACT.Sigmoid, s1["sg"].done(key))
                else:
                    i = STAGED.index(key)
                    if i >= 2:
                        two = STAGED[i - 2]
                        act.wait_ge(*(b1.full(two + ("turned",)) if two[0] in VALUES else s1["taken"].upto(two)))
                    op(XS[:, s1_slot[key], :], ps, ACT.Copy, b1.free(key))
                    nc.scalar.drain().then_inc(*s1["staged"].done(key))
                feed(b1, key)

            def token_major_values(key):
                kind, h = key
                dst, base = VT[{"hi": "h", "rv": "r", "dv": "d"}[kind]]
                act.wait_ge(*b1.full((kind, h, "turned")))
                ps = b1.of((kind, h, "turned"))
                op(dst[:, :, h * P:(h + 1) * P], ps[:, 0:2 * P].rearrange("p (a b) -> p a b", b=P), ACT.Copy)
                op(V3[base:base + N_META, h * P:(h + 1) * P], ps[0:N_META, 2 * P:3 * P], ACT.Copy,
                   b1.free((kind, h, "turned")))
                nc.scalar.drain().then_inc(*s1["valued"].done(key))

            def stage_all(keys, before):
                for key in keys:
                    stage(key)
                    if before is not None and before[0] in VALUES:
                        token_major_values(before)
                    before = key
                return before

            def exp_levels(h):
                act.wait_ge(*s1["zdiff"].upto(h))
                op(Z[:, 0:4, 0:2 * P], Z[:, 0:4, 0:2 * P], ACT.Exp)
                op(Z[:, 4:8, :], Z[:, 4:8, :], ACT.Exp)
                op(Z[:, 8, P:T1], Z[:, 8, P:T1], ACT.Exp)
                nc.scalar.drain().then_inc(*s1["zexp"].done(h))

            def square_output(key, e):
                kind, h = key[0], key[1] // (2 if key[0] == "r" else 1)
                last = (kind, h - 1) if h else {"r": ("h", 7), "d": ("r", 3)}.get(kind)
                if last is not None:
                    act.wait_ge(*b1.full(("ss",) + last))
                act.wait_ge(*b1.full(("o",) + key))
                op(SQ[:, e, :], b1.of(("o",) + key)[:, 0:T1], ACT.Square, s1["sqo"].done((kind, h, e)))
                before = {("r", 0): None, ("d", 0): ("r", 3), ("d", 1): ("r", 3)}.get((kind, h), (kind, h - (2 if kind == "d" else 1)))
                act.wait_ge(*(s1["normed"].upto(before) if before else s1["taken"].upto(TILES_FILL[-3])))
                op(XS[:, key[1] % 2, :], b1.of(("o",) + key)[:, 0:T1], ACT.Copy, b1.free(("o",) + key))

            def merge_sigmoid(n, j):
                act.wait_ge(*b1.full(("mA", n, j)))
                seq = MERGE1.index(n) * KT + j
                if n == 2:
                    pass
                elif seq >= 2:
                    act.wait_ge(*s1["y"].upto((MERGE1[(seq - 2) // KT], (seq - 2) % KT)))
                else:
                    act.wait_ge(*s1["gated"].upto(("rg", 6 + seq)))
                op(SG[:, j % 2, :] if n != 2 else SIG2[:, j, :], b1.of(("mA", n, j))[:, 0:T1], ACT.Sigmoid, b1.free(("mA", n, j)))
                nc.scalar.drain().then_inc(*s1["sigm"].done((n, j)))
                feed(b1, ("mA", n, j))

            def da_exp(h):
                for i, n in enumerate([P, P, N_META]):
                    act.wait_ge(*s1["sco"].upto((h, i)))
                    for m in range(2):
                        op(SC[i][0:n, m, :], SC[i][0:n, m, :], ACT.Exp, bias=small[0:n, 2 * i + m:2 * i + m + 1],
                           accum_out=small[0:n, 8 + 2 * i + m:9 + 2 * i + m])
                    nc.scalar.drain().then_inc(*s1["expd"].done((h, i)))

            def da_turned(h):
                act.wait_ge(*b1.full(("dt", h)))
                ps = b1.of(("dt", h))
                op(S0[:, :], ps[:, 0:T1], ACT.Copy)
                op(S1[:, :], ps[:, T1:T1 + P + N_META], ACT.Copy)
                op(S2[64:64 + N_META, :], ps[0:N_META, T1 + P + N_META:T1 + P + 2 * N_META], ACT.Copy, b1.free(("dt", h)))
                nc.scalar.drain().then_inc(*s1["tr"].done(h))

            act.wait_ge(inputs_in, 16 * N_INPUTS)
            act.wait_ge(*s0["dve"].upto("lb"))
            op(lb_e[:, :], lb_e[:, :], ACT.Exp)
            op(lam_e[:, :], lam_e[:, :], ACT.Exp)
            nc.scalar.drain().then_inc(*s0["act"].done("exp"))
            act.wait_ge(*s0["dve"].upto("ang"))
            op(angs[:, :], angs[:, :], ACT.Sin)
            nc.scalar.drain().then_inc(*s0["act"].done("sin"))
            for slot in range(RING):
                act.sem_inc(slab_used[slot])
            with act.Fori(0, DEPTH) as layer:
                begin_stream(layer, SLABS1, 0)
                act.wait_ge(layer_begin, layer + 1)
                act.sem_inc(act_in)
                squares(s1, "mix", X1, Q1)
                inverse_root(s1, b1, "ss_mix", D_MODEL, T1)
                before = None
                for key in TILES_HG:
                    before = stage_all([key], before)
                    if key == ("hi", 1):
                        act.wait_ge(*s1["f_in"].upto())
                        log_exp_table()
                        op(HC[:, :, :], HC[:, :, :], ACT.Ln, s1["lnf"].done())
                    if key == ("hi", 5):
                        act.wait_ge(*s1["cum"].upto())
                        op(e1_sb[:, :], HC[:, :, 2 * P - 1], ACT.Exp, s1["e1"].done())
                    if key == ("hi", 7):
                        exp_levels(0)
                fill = list(TILES_FILL)
                for h in range(HG_HEADS):
                    for i in range(5):
                        if i == 2 and h + 1 < HG_HEADS:
                            exp_levels(h + 1)
                        if i == 0 and h == 0:
                            log_exp_table()
                        before = stage_all([fill.pop(0)], before)
                    inverse_root(s1, b1, ("ss", "h", h), P, T1,
                                 s1["normed"].upto(("h", h - 1)) if h else s1["hn"].upto(KT - 1), table=False)
                stage_all(TILES_RG, before)
                for h in range(RET_HEADS):
                    merge_sigmoid(1, 2 * h)
                    square_output(("r", 2 * h), 0)
                    square_output(("r", 2 * h + 1), 1)
                    merge_sigmoid(1, 2 * h + 1)
                    inverse_root(s1, b1, ("ss", "r", h), 2 * P, T1, s1["normed"].upto(("r", h - 1) if h else ("h", 7)))
                da_exp(0)
                for h in range(DA_HEADS):
                    if h > 0:
                        log_exp_table()
                    if h + 1 < DA_HEADS:
                        da_exp(h + 1)
                    if h > 0:
                        inverse_root(s1, b1, ("ss", "d", h - 1), P, T1,
                                     s1["normed"].upto(("d", h - 2) if h > 1 else ("r", 3)), table=False)
                    merge_sigmoid(0, h)
                    da_turned(h)
                    merge_sigmoid(2, h)
                    square_output(("d", h), 0)
                inverse_root(s1, b1, ("ss", "d", 7), P, T1, s1["normed"].upto(("d", 6)))
                for j in range(KT):
                    feed(b1, ("mB", 2, j))
                squares(s1, "ffn", X1, Q1, lambda k: s1["x"].upto(("wo", k)), lambda k: (b1, ("wo", k)))
                inverse_root(s1, b1, "ss_ffn", D_MODEL, T1, s1["normed"].upto(("d", 7)))
                for j in range(FT):
                    if j >= 2:
                        act.wait_ge(*s1["ff"].upto(j - 2))
                    for half, dst in enumerate((CG, CV)):
                        act.wait_ge(*b1.full(("ff", j, half)))
                        f = half * FT + j
                        op(dst[:, j % 2, :], b1.of(("ff", j, half))[:, 0:T1], ACT.Identity,
                           s1["conv"].done((j, half)), scale=par("cw", 2 * 2 * FT + f), bias=par("cb", f))
                        feed(b1, ("ff", j, half))
                    act.wait_ge(*s1["gated"].upto(("ff", j)))
                    op(SG[:, j % 2, :], CG[:, j % 2, :], ACT.Sigmoid, s1["sg"].done(("ff", j)))
                for j in range(KT):
                    feed(b1, ("down", j))
                finish_stream()
                act.drain().then_inc(layer_end, 1)

            act.wait_ge(layer_begin, DEPTH + 1)
            for k in range(KT):
                op(Q1[:, k, N_META:T1], X1[:, k, N_META:T1], ACT.Square, sm["sq"].done(k))
            inverse_root(sm, bm, "ss", D_MODEL, T2)

            def copy2(key, dst, rows=slice(0, P), cols=slice(0, T2), last=True, signal=True, func=ACT.Copy, **kw):
                act.wait_ge(*b2.full(key))
                op(dst, b2.of(key)[rows, cols], func, b2.free(key) if last else None, **kw)
                if signal:
                    nc.scalar.drain().then_inc(*s2["evac"].done(key))
                feed(b2, key)

            def attention_exp(kind, h):
                act.wait_ge(*s2["sc"].upto((kind, h)))
                for i, cols in enumerate((slice(0, P), slice(P, 3 * P))):
                    c = 32 + 8 * (h % 2) + i
                    op(SC2[:, h % 2, cols], SC2[:, h % 2, cols], ACT.Exp, bias=small[:, c:c + 1],
                       accum_out=small[:, c + 2:c + 3])
                nc.scalar.drain().then_inc(*s2["expd"].done((kind, h)))

            def attention_turned(kind, h):
                act.wait_ge(*b2.full((kind, "t", h)))
                if h >= 2:
                    act.wait_ge(*b2.full((kind, "o", h // 2 - 1)))
                op(SS[:, h % 2, :], b2.of((kind, "t", h))[:, 0:3 * P], ACT.Copy, b2.free((kind, "t", h)))
                nc.scalar.drain().then_inc(*s2["tr"].done((kind, h)))

            def merge_sigmoid2(n, j):
                act.wait_ge(*b2.full(("mA", n, j)))
                seq = MERGE2.index(n) * KT + j
                if seq >= 2:
                    act.wait_ge(*s2["y"].upto((MERGE2[(seq - 2) // KT], (seq - 2) % KT)))
                op(SGM[:, j % 2, :], b2.of(("mA", n, j))[:, 0:T2], ACT.Sigmoid, b2.free(("mA", n, j)))
                nc.scalar.drain().then_inc(*s2["sigm"].done((n, j)))
                feed(b2, ("mA", n, j))

            def index_relu(i):
                for c in range(4):
                    seq = 4 * i + c
                    if seq >= 2:
                        act.wait_ge(*s2["used"].upto(seq - 2))
                    copy2(("ix", i, c), REL[:, seq % 2, 0:2 * (i + 1) * P], cols=slice(0, 2 * (i + 1) * P), signal=False,
                          func=ACT.Relu, scale=32 ** -0.5)
                    nc.scalar.drain().then_inc(*s2["relu"].done(seq))

            with act.Fori(0, DEPTH) as layer:
                begin_stream(layer, SLABS2, DEPTH * SLABS1 // RING)
                act.wait_ge(layer_begin, layer + DEPTH + 2)
                act.sem_inc(act_in)
                squares(s2, "att", X2, Q2)
                inverse_root(s2, b2, "ss_att", D_MODEL, T2)
                for i, key in enumerate(("cq0", "cq1", "ckv")):
                    act.wait_ge(*b2.full(key))
                    op(SQ2[:, i, :], b2.of(key)[:, 0:T2], ACT.Square)
                    copy2(key, CQ[:, i, :] if i < 2 else CKV[:, :])
                copy2("kr", KR[MLA_NOPE:MLA_QK, :], rows=slice(MLA_NOPE, MLA_QK))
                for i in range(2):
                    copy2(f"cb{i}", SB[:, i, :])
                for i in range(2):
                    copy2(f"cc{i}", SI[:, i, :])
                inverse_root(s2, b2, "ss_q", 2 * P, T2, s2["hn"].upto(("att", KT - 1)))
                inverse_root(s2, b2, "ss_kv", P, T2, s2["cqn"].upto(), table=False)
                for i in range(2):
                    copy2(f"qs{i}", QS[:, i, :])
                for h in range(MLA_HEADS):
                    copy2(("qu", h), QM[0:MLA_QK, h, :], rows=slice(0, MLA_QK))
                for h in range(MLA_HEADS):
                    copy2(("ku", h), KM[0:MLA_NOPE, h, :], rows=slice(0, MLA_NOPE))
                for t in range(2):
                    copy2(("vu", t), VM[:, t, :])
                copy2("ks", KS[0:64, :], rows=slice(0, 64), last=False, signal=False)
                copy2("ks", KS[64:P, :], rows=slice(0, 64))
                copy2("iq0", IQ[:, 0, :])
                copy2("iq1", IQ[:, 1, :])
                for q in range(4):
                    copy2("ik", IK[32 * q:32 * q + 32, :], rows=slice(0, 32), last=q == 3, signal=q == 3)
                for t in range(2):
                    copy2(("vsw", t), VS[:, t, :], cols=slice(0, 64), last=False, signal=False)
                    copy2(("vsw", t), IW[:, t, :], cols=slice(64, 64 + IDX_HEADS), scale=IDX_HEADS ** -0.5)
                index_relu(0)
                copy2("gq", GQ[:, :], scale=GLA_DK ** -0.5)
                index_relu(1)
                attention_exp("m", 0)
                copy2("gk", GK[:, :])
                for t in range(2):
                    copy2(("gv", t), GV[:, t, :])
                copy2("glr", GL[0:16, :], rows=slice(0, 16))
                for i in range(2):
                    act.wait_ge(*b2.full(f"gr{i}"))
                    op(SGM[:, i, :], b2.of(f"gr{i}")[:, 0:T2], ACT.Sigmoid)
                    nc.scalar.drain().then_inc(*s2["sg"].done(i))
                    feed(b2, f"gr{i}")
                log_exp_table()
                act.wait_ge(*s2["gz"].upto())
                op(GE[:, :], GE[:, :], ACT.Exp)
                nc.scalar.drain()
                op(GE[:, :], GE[:, :], ACT.Ln, bias=one)
                nc.scalar.drain().then_inc(*s2["gez"].done())
                for h in range(MLA_HEADS):
                    if h + 1 < MLA_HEADS:
                        attention_exp("m", h + 1)
                    merge_sigmoid2(1, 2 * h)
                    attention_turned("m", h)
                    merge_sigmoid2(1, 2 * h + 1)
                    if h == 0:
                        act.wait_ge(*s2["zdiff"].upto())
                        op(Z2[:, :, :], Z2[:, :, :], ACT.Exp)
                        nc.scalar.drain().then_inc(*s2["zexp"].done())
                for g in range(GLA_HEADS):
                    merge_sigmoid2(0, 2 * g)
                    merge_sigmoid2(0, 2 * g + 1)
                    r = slice(64 * (g % 2), 64 * (g % 2) + 64)
                    act.wait_ge(*b2.full(("g", "o", g)))
                    op(SQ2[r, g // 2, :], b2.of(("g", "o", g))[r, 0:T2], ACT.Square)
                    op(GO[r, g // 2, :], b2.of(("g", "o", g))[r, 0:T2], ACT.Copy, b2.free(("g", "o", g)))
                    if g % 2:
                        nc.scalar.drain().then_inc(*s2["sqo"].done(g // 2))
                    if g % 2:
                        inverse_root(s2, b2, ("ssg", g // 2), 64, T2,
                                     s2["ckn"].upto() if g == 1 else s2["normed"].upto(0))
                attention_exp("s", 0)
                for h in range(DSA_HEADS):
                    if h + 1 < DSA_HEADS:
                        attention_exp("s", h + 1)
                    merge_sigmoid2(3, 2 * h)
                    attention_turned("s", h)
                    merge_sigmoid2(3, 2 * h + 1)
                for j in range(KT):
                    merge_sigmoid2(2, j)
                squares(s2, "ffn", X2, Q2, lambda k: s2["x"].upto(("wo", k)), lambda k: (b2, ("wo", k)))
                inverse_root(s2, b2, "ss_ffn", D_MODEL, T2, s2["normed"].upto(1))
                for j in range(FT):
                    act.wait_ge(*b2.full(("ff", j, 0)))
                    if j >= 2:
                        act.wait_ge(*s2["ff"].upto(j - 2))
                    op(SGM[:, j % 2, :], b2.of(("ff", j, 0))[:, 0:T2], ACT.Sigmoid, s2["sigf"].done(j))
                    feed(b2, ("ff", j, 0))
                    feed(b2, ("ff", j, 1))
                for j in range(KT):
                    feed(b2, ("down", j))
                finish_stream()
                act.drain().then_inc(layer_end, 1)
            act.wait_ge(layer_begin, 2 * DEPTH + 2)
            for k in range(KT):
                op(Q2[:, k, :], X2[:, k, :], ACT.Square, se["sq"].done(k))
            inverse_root(se, be, "ss", D_MODEL, T2)

        @block.vector
        def _(dve):
            V = nc.vector

            def fence(done=None):
                i = V.drain()
                if done is not None:
                    i.then_inc(*done)

            def split(src, hi, lo):
                V.tensor_copy(hi, src)
                V.drain()
                return V.tensor_tensor(lo, src, hi.bitcast(F32), ALU.subtract)

            def norm(s, sums, src, gains, dst, tokens, tmp, tag):
                dve.wait_ge(*s["rs"].upto(sums))
                for k in range(KT):
                    V.scalar_tensor_tensor(dst[0][:, k, :], src[:, k, :], gains(k), RS[:, 0:tokens], ALU.mult, ALU.mult)\
                        .then_inc(*s["hn"].done(tag(k)))
                for k in range(KT):
                    t = tmp[:, k % 2, 0:tokens]
                    V.scalar_tensor_tensor(t, src[:, k, :], gains(k), RS[:, 0:tokens], ALU.mult, ALU.mult)
                    V.drain()
                    V.tensor_tensor(dst[1][:, k, :], t, dst[0][:, k, :].bitcast(F32), ALU.subtract)\
                        .then_inc(*s["hnlo"].done(tag(k)))

            def level_differences(C, zq, levels_at, tokens, scan_end):
                for s, z in levels_at:
                    n = 2 * P if s >= 16 else tokens
                    c = C[:, 0:n].rearrange("p (b t s) -> p b t s", t=2, s=s)
                    d = zq[:, z, 0:n].rearrange("p (b t s) -> p b t s", t=2, s=s)
                    ref = c[:, :, 0, s - 1:s].to_broadcast([P, n // (2 * s), s])
                    V.tensor_tensor(d[:, :, 0, :], ref, c[:, :, 0, :], ALU.subtract)
                    V.tensor_tensor(d[:, :, 1, :], c[:, :, 1, :], ref, ALU.subtract)

            def level_factors(zq, levels_at, tokens, q, k):
                for s, z in levels_at:
                    n = 2 * P if s >= 16 else tokens
                    d = zq[:, z, 0:n].rearrange("p (b t s) -> p b t s", t=2, s=s)
                    for t, m in ((0, k), (1, q)):
                        m = m[:, 0:n].rearrange("p (b t s) -> p b t s", t=2, s=s)[:, :, t, :]
                        V.tensor_tensor(d[:, :, t, :], d[:, :, t, :], m, ALU.mult)

            LV = [(64, 0), (32, 1), (16, 2), (8, 4), (4, 5), (2, 6), (1, 7)]

            def mask_levels(b, h, t, dst):
                if t < 2:
                    for g in range(2):
                        dve.wait_ge(*b.full(("lv", h, t, g)))
                        V.tensor_tensor(LT[:, 4 * g:4 * g + 4, :], b.of(("lv", h, t, g)).rearrange("p (a b) -> p a b", b=P),
                                        lvl[:, 4 * g:4 * g + 4, :], ALU.mult).then_inc(*b.free(("lv", h, t, g)))
                    V.drain()
                    V.tensor_reduce(dst, LT[:, :, :].rearrange("p a b -> p b a"), AXX, ALU.add)
                else:
                    n = N_META
                    dve.wait_ge(*b.full(("lv", h, t, 0)))
                    V.tensor_tensor(LT[0:n, 0:5, 0:n], b.of(("lv", h, t, 0))[0:n, 0:5 * n].rearrange("p (a b) -> p a b", b=n),
                                    lvl[0:n, 3:8, 0:n], ALU.mult).then_inc(*b.free(("lv", h, t, 0)))
                    V.drain()
                    V.tensor_reduce(dst, LT[0:n, 0:5, 0:n].rearrange("p a b -> p b a"), AXX, ALU.add)
                V.drain()

            def square_output(h):
                dve.wait_ge(*b1.full(("o", "h", h)))
                if h > 0:
                    dve.wait_ge(*b1.full(("ss", "h", h - 1)))
                o = b1.of(("o", "h", h))[:, 0:T1]
                V.tensor_copy(oh_sb[:, :], o)
                V.drain().then_inc(*b1.free(("o", "h", h)))
                V.tensor_tensor(SQ[:, 0, :], oh_sb[:, :], oh_sb[:, :], ALU.mult)
                fence(s1["sqh"].done(h))

            def hg_differences(h):
                if h > 0:
                    dve.wait_ge(*b1.full(("cross", h - 1)))
                C = HC[:, h, :]
                level_differences(C, Z, LV, T1, None)
                V.tensor_scalar(Z[:, 3, 0:P], C[:, 0:P], C[:, P - 1:P], -1.0, ALU.subtract, ALU.mult)
                V.tensor_copy(Z[:, 3, P:2 * P], C[:, P:2 * P])
                V.tensor_scalar(Z[:, 8, P:2 * P], C[:, P:2 * P], C[:, 2 * P - 1:2 * P], -1.0, ALU.subtract, ALU.mult)
                V.tensor_copy(Z[:, 8, 2 * P:T1], C[:, 2 * P:T1])
                fence(s1["zdiff"].done(h))

            def hg_factors(h):
                dve.wait_ge(*s1["zexp"].upto(h))
                q, k = HQ[:, h, :], HK[:, h, :]
                level_factors(Z, LV, T1, q, k)
                V.tensor_tensor(Z[:, 3, 0:P], Z[:, 3, 0:P], k[:, 0:P], ALU.mult)
                V.tensor_tensor(Z[:, 3, P:2 * P], Z[:, 3, P:2 * P], q[:, P:2 * P], ALU.mult)
                V.tensor_tensor(Z[:, 8, P:2 * P], Z[:, 8, P:2 * P], k[:, P:2 * P], ALU.mult)
                V.tensor_tensor(Z[:, 8, 2 * P:T1], Z[:, 8, 2 * P:T1], q[:, 2 * P:T1], ALU.mult)
                V.drain()
                V.tensor_scalar(Z[:, 8, 0:P], Z[:, 3, 0:P], e1_sb[:, h:h + 1], None, ALU.mult)
                fence(s1["z"].done(h))

            def hg_weights(h):
                mask_levels(b1, h, 0, S0[:, 0:P])
                mask_levels(b1, h, 1, S1[:, 0:P])
                mask_levels(b1, h, 2, S2[0:N_META, :])
                dve.wait_ge(*b1.full(("cross", h)))
                ps = b1.of(("cross", h))
                V.tensor_copy(S0[:, P:T1], ps[:, 0:P + N_META])
                V.tensor_copy(S1[:, P:P + N_META], ps[:, P + N_META:P + 2 * N_META]).then_inc(*b1.free(("cross", h)))
                fence(s1["att"].done(("h", h)))

            def normalise(kind, h):
                dve.wait_ge(*s1["rs"].upto(("ss", kind, h)))
                tiles = [("r", 2 * h), ("r", 2 * h + 1)] if kind == "r" else [(kind, h)]
                for i, (kd, t) in enumerate(tiles):
                    o = oh_sb[:, :] if kd == "h" else XS[:, t % 2, :]
                    hi, lo = BR["rhd".index(kd)]
                    if kind == "d":
                        V.scalar_tensor_tensor(TMP[:, i, :], o, par("sub"), RS[:, :], ALU.mult, ALU.mult)
                    else:
                        V.tensor_tensor(TMP[:, i, :], o, RS[:, :], ALU.mult)
                        V.drain()
                        V.tensor_tensor(TMP[:, i, :], (HG if kind == "h" else RG)[:, t, :], TMP[:, i, :], ALU.mult)
                    V.drain()
                    split(TMP[:, i, :], hi[:, t, :], lo[:, t, :])
                fence(s1["normed"].done((kind, h)))

            def settle(key):
                kind, h = key
                if kind in ROT:
                    dst, cos, sin, _ = ROT[kind]
                    dve.wait_ge(*s1["staged"].upto(key))
                    x = XS[:, s1_slot[key], :]
                    V.tensor_tensor(TMP[:, 0, :], x, cos, ALU.mult)
                    dve.wait_ge(*b1.full((kind, h, "turned")))
                    V.tensor_tensor(TMP[:, 1, :], b1.of((kind, h, "turned"))[:, 0:T1], sin, ALU.mult)\
                        .then_inc(*b1.free((kind, h, "turned")))
                    V.drain()
                    V.tensor_tensor(dst[:, h, :], TMP[:, 0, :], TMP[:, 1, :], ALU.add)
                    fence(s1["taken"].done(key))
                elif kind in ("hg", "rg"):
                    dve.wait_ge(*s1["sg"].upto(key))
                    dst = HG if kind == "hg" else RG
                    V.tensor_tensor(dst[:, h, :], SG[:, h % 2, :], b1.of(key)[:, 0:T1], ALU.mult).then_inc(*b1.free(key))
                    fence(s1["gated"].done(key))
                elif kind == "hf":
                    dve.wait_ge(*s1["sig_f"].upto(h))
                    V.tensor_scalar(HK[:, h, :], HK[:, h, :], par("omlb", h), None, ALU.mult)
                    V.tensor_scalar(HC[:, h, :], HC[:, h, :], par("omlb", h), par("lbf", h), ALU.mult, ALU.add)
                    if h == HG_HEADS - 1:
                        fence(s1["f_in"].done())

            def merge(n, j):
                dve.wait_ge(*s1["sigm"].upto((n, j)))
                dve.wait_ge(*b1.full(("mB", n, j)))
                first = n == MERGE1[0]
                dst = Y1[:, j, :] if first else TMP[:, 0, :]
                V.tensor_tensor(dst, SG[:, j % 2, :] if n != 2 else SIG2[:, j, :], b1.of(("mB", n, j))[:, 0:T1], ALU.mult).then_inc(*b1.free(("mB", n, j)))
                V.drain()
                if not first:
                    V.tensor_tensor(Y1[:, j, :], Y1[:, j, :], TMP[:, 0, :], ALU.add)
                fence(s1["y"].done((n, j)))
                if n == MERGE1[-1]:
                    split(Y1[:, j, :], YS[0][:, j, :], YS[1][:, j, :]).then_inc(*s1["yb"].done(j))

            def retention_weights(h):
                dve.wait_ge(*b1.full(("rs", h, 0)))
                V.tensor_tensor(S0[:, :], b1.of(("rs", h, 0))[:, 0:T1], retD[:, h, :], ALU.mult).then_inc(*b1.free(("rs", h, 0)))
                dve.wait_ge(*b1.full(("rs", h, 1)))
                ps = b1.of(("rs", h, 1))
                V.tensor_tensor(S1[:, :], ps[:, 0:P + N_META], retD[:, h, 0:P + N_META], ALU.mult)
                V.tensor_tensor(S2[32:32 + N_META, :], ps[0:N_META, P + N_META:P + 2 * N_META], retD[0:N_META, h, 0:N_META],
                                ALU.mult).then_inc(*b1.free(("rs", h, 1)))
                fence(s1["att"].done(("r", h)))

            DA_TILES = [(P, P), (P, 2 * P), (N_META, T1)]

            def da_masked(h):
                for i, (n, kn) in enumerate(DA_TILES):
                    mask = causal[0:n, (2 - i) * P:(2 - i) * P + kn]
                    for m in range(2):
                        key = ("ds", h, m if i < 2 else 2 + m)
                        dve.wait_ge(*b1.full(key))
                        at = P if i == 1 else 0
                        ins = V.scalar_tensor_tensor(SC[i][0:n, m, :], b1.of(key)[0:n, at:at + kn], 64 ** -0.5, mask,
                                                     ALU.mult, ALU.add)
                        if i > 0:
                            ins.then_inc(*b1.free(key))
                    V.drain()
                    V.tensor_reduce(small[0:n, 2 * i:2 * i + 2], SC[i][0:n, :, :], AXX, ALU.max, negate=True)
                    fence(s1["sco"].done((h, i)))

            def da_combined(h):
                if h > 0:
                    dve.wait_ge(*b1.full(("dt", h - 1)))
                for i, (n, kn) in enumerate(DA_TILES):
                    dve.wait_ge(*s1["expd"].upto((h, i)))
                    r = small[0:n, 16 + 2 * i:18 + 2 * i]
                    V.reciprocal(r, small[0:n, 8 + 2 * i:10 + 2 * i])
                    V.drain()
                    V.tensor_scalar(r[:, 1:2], r[:, 1:2], par("nlam")[0:n, :], None, ALU.mult)
                    V.tensor_scalar(WA[i][0:n, :], SC[i][0:n, 0, :], r[:, 0:1], None, ALU.mult)
                    V.drain()
                    V.scalar_tensor_tensor(WA[i][0:n, :], SC[i][0:n, 1, :], r[:, 1:2], WA[i][0:n, :], ALU.mult, ALU.add)
                fence(s1["w"].done(h))

            def conv(j, half):
                key = ("ff", j, half)
                dst = (CG, CV)[half][:, j % 2, :]
                f = half * FT + j
                dve.wait_ge(*s1["conv"].upto((j, half)))
                ps = b1.of(key)
                V.scalar_tensor_tensor(dst[:, 1:T1], ps[:, 0:T1 - 1], par("cw", 2 * FT + f), dst[:, 1:T1], ALU.mult, ALU.add)
                V.drain()
                V.scalar_tensor_tensor(dst[:, 2:T1], ps[:, 0:T1 - 2], par("cw", f), dst[:, 2:T1], ALU.mult, ALU.add)\
                    .then_inc(*b1.free(key))

            def add_to_x(b, s, X, key, j, tokens):
                dve.wait_ge(*b.full(key))
                V.tensor_tensor(X[:, j, :], X[:, j, :], b.of(key)[:, 0:tokens], ALU.add).then_inc(*b.free(key))
                fence(s["x"].done(key))

            dve.wait_ge(inputs_in, 16 * N_INPUTS)
            lb2 = lb_sb[:, :].rearrange("p (l k) -> p l k", k=KT)
            lbe2 = lb_e[:, :].rearrange("p (l k) -> p l k", k=KT)
            V.tensor_tensor(lb_t[:, 0:KT], lb2[:, 0, :], lb2[:, 1, :], ALU.max)
            lam3 = lam_sb[:, :].rearrange("p (l a b d) -> p l a b d", l=DEPTH, a=2, b=2)
            V.tensor_tensor(lam_t[:, :].rearrange("p (l a d) -> p l a d", l=DEPTH, a=2), lam3[:, :, :, 0, :],
                            lam3[:, :, :, 1, :], ALU.mult)
            V.drain()
            V.tensor_reduce(lam_e[:, :], lam_t[:, :].rearrange("p (a d) -> p a d", d=64), AXX, ALU.add)
            for l in range(DEPTH):
                V.tensor_tensor(lbe2[:, l, :], lb2[:, l, :], lb_t[:, 0:KT], ALU.subtract)
            fence(s0["dve"].done("lb"))
            V.tensor_copy(angs[:, T2:2 * T2], pos_sb[:, :])
            V.drain()
            V.tensor_scalar(angs[:, 0:T2], angs[:, T2:2 * T2], const("invM"), None, ALU.mult)
            V.drain()
            V.tensor_scalar(turns[:, :], angs[:, 0:T2], float(np.float32(1 / (2 * np.pi))), ROUND, ALU.mult, ALU.add)
            V.drain()
            V.tensor_scalar(turns[:, :], turns[:, :], ROUND, None, ALU.subtract)
            for c in TWO_PI:
                V.drain()
                V.scalar_tensor_tensor(angs[:, 0:T2], turns[:, :], -c, angs[:, 0:T2], ALU.mult, ALU.add)
            V.drain()
            V.tensor_scalar(angs[:, 0:T2], angs[:, 0:T2], 3.1415925, -3.1415925, ALU.min, ALU.max)
            V.drain()
            V.tensor_scalar(angs[:, T2:2 * T2], angs[:, 0:T2], 0.5, None, ALU.mult)
            fence(s0["dve"].done("ang"))
            dve.wait_ge(*s0["act"].upto("exp"))
            V.tensor_tensor(lb_t[:, 0:KT], lbe2[:, 0, :], lbe2[:, 1, :], ALU.add)
            V.drain()
            V.reciprocal(lb_t[:, 0:KT], lb_t[:, 0:KT])
            V.drain()
            for l in range(DEPTH):
                V.tensor_tensor(lbe2[:, l, :], lbe2[:, l, :], lb_t[:, 0:KT], ALU.mult)
            V.drain()
            V.tensor_tensor(lb_t[:, 0:KT], lbe2[:, 0, :], lbe2[:, 1, :], ALU.add)
            V.drain()
            V.tensor_tensor(lb_t[:, 0:KT], lb_t[:, 0:KT], lbe2[:, 0, :], ALU.subtract)
            V.drain()
            p1 = par1_sb[:, :].rearrange("p (l n) -> p l n", n=NPAR1)
            om, lf = PAR1["omlb"][0], PAR1["lbf"][0]
            V.memset(p1[:, 0, om:om + KT], 1.0)
            V.memset(p1[:, 0, lf:lf + KT], LB_FLOOR)
            V.tensor_scalar(p1[:, 1, om:om + KT], lb_t[:, 0:KT], -1.0, 1.0, ALU.mult, ALU.add)
            V.tensor_scalar(p1[:, 1, lf:lf + KT], lb_t[:, 0:KT], LB_FLOOR, None, ALU.max)
            nl, sub = PAR1["nlam"][0], PAR1["sub"][0]
            for l in range(DEPTH):
                init = 0.8 - 0.6 * float(np.exp(-0.3 * l))
                V.tensor_tensor(p1[:, l, nl:nl + 1], lam_e[:, 2 * l + 1:2 * l + 2], lam_e[:, 2 * l:2 * l + 1], ALU.subtract)
                V.drain()
                V.tensor_scalar(p1[:, l, nl:nl + 1], p1[:, l, nl:nl + 1], init, None, ALU.subtract)
                V.tensor_scalar(p1[:, l, sub:sub + 1], p1[:, l, sub:sub + 1], 1.0 - init, None, ALU.mult)
            V.drain()
            dve.wait_ge(*s0["act"].upto("sin"))
            V.tensor_copy(sinM, angs[:, 0:T2])
            V.tensor_tensor(cosM, angs[:, T2:2 * T2], angs[:, T2:2 * T2], ALU.mult)
            V.drain()
            V.tensor_scalar(cosM, cosM, -2.0, 1.0, ALU.mult, ALU.add)
            V.drain()
            with dve.Fori(0, DEPTH) as layer:
                V.tensor_copy(cur[:, 0:NPAR1], par1_sb[:, bass.ds(layer * NPAR1, NPAR1)])
                fence((layer_begin, 1))
                norm(s1, "ss_mix", X1, lambda k: par("gmix", k), (H1, L1), T1, TMP, lambda k: k)
                for key in TILES_HG:
                    settle(key)
                    if key == ("hi", 1):
                        dve.wait_ge(*s1["lnf"].upto())
                        for h in range(HG_HEADS):
                            V.tensor_tensor_scan(HC[:, h, :], restart[:, :], HC[:, h, :], 0.0, ALU.mult, ALU.add)
                        fence(s1["cum"].done())
                    if key == ("hi", 5):
                        hg_differences(0)
                    if key == ("hg", 0):
                        dve.wait_ge(*s1["e1"].upto())
                        hg_factors(0)
                fill, before = list(TILES_FILL), None
                for h in range(HG_HEADS):
                    hg_weights(h)
                    if h + 1 < HG_HEADS:
                        hg_differences(h + 1)
                    for i in range(5):
                        if before is not None:
                            settle(before)
                        before = fill.pop(0)
                        if i == 0 and h > 0:
                            normalise("h", h - 1)
                        if i == 1 and h + 1 < HG_HEADS:
                            hg_factors(h + 1)
                        if i == 2:
                            square_output(h)
                settle(before)
                normalise("h", HG_HEADS - 1)
                for key in TILES_RG:
                    settle(key)
                for h in range(RET_HEADS):
                    retention_weights(h)
                    merge(1, 2 * h)
                    merge(1, 2 * h + 1)
                    normalise("r", h)
                da_masked(0)
                da_combined(0)
                for h in range(DA_HEADS):
                    if h + 1 < DA_HEADS:
                        da_masked(h + 1)
                    if h > 0:
                        normalise("d", h - 1)
                    if h + 1 < DA_HEADS:
                        da_combined(h + 1)
                    merge(0, h)
                normalise("d", 7)
                for j in range(KT):
                    merge(2, j)
                for j in range(KT):
                    add_to_x(b1, s1, X1, ("wo", j), j, T1)
                norm(s1, "ss_ffn", X1, lambda k: par("gffn", k), (H1, L1), T1, TMP, lambda k: ("ffn", k))
                for j in range(FT):
                    conv(j, 0)
                    fence(s1["gated"].done(("ff", j)))
                    conv(j, 1)
                    V.drain()
                    dve.wait_ge(*s1["sg"].upto(("ff", j)))
                    V.tensor_tensor(CG[:, j % 2, :], CG[:, j % 2, :], SG[:, j % 2, :], ALU.mult)
                    V.drain()
                    V.tensor_tensor(CG[:, j % 2, :], CG[:, j % 2, :], CV[:, j % 2, :], ALU.mult)
                    V.drain()
                    split(CG[:, j % 2, :], FF[0][:, j, :], FF[1][:, j, :])
                    fence(s1["ff"].done(j))
                for j in range(KT):
                    add_to_x(b1, s1, X1, ("down", j), j, T1)
                dve.wait_ge(layer_end, 2 * layer + 2)
                dve.sem_inc(dve_in)
                for x in list(s1.values()):
                    dve.sem_clear(x.sem)
                for x in bank_full + bank_free:
                    dve.sem_clear(x)

            fence((layer_begin, 1))
            dve.wait_ge(*sm["rs"].upto("ss"))
            for k in range(KT):
                V.scalar_tensor_tensor(X2[:, k, :], X1[:, k, N_META:T1], fin_sb[:, k:k + 1], RS[:, 0:T2], ALU.mult, ALU.mult)
            V.drain()
            for x in bank_full + bank_free:
                dve.sem_clear(x)

            def attention_masked(kind, h):
                dve.wait_ge(*b2.full((kind, "sc", h)))
                ps, s = b2.of((kind, "sc", h)), SC2[:, h % 2, :]
                if kind == "m":
                    V.scalar_tensor_tensor(s[:, 0:P], ps[:, 0:P], MLA_QK ** -0.5, causal[:, 2 * P:3 * P], ALU.mult, ALU.add)
                    V.scalar_tensor_tensor(s[:, P:3 * P], ps[:, P:3 * P], MLA_QK ** -0.5, causal[:, P:3 * P], ALU.mult, ALU.add)\
                        .then_inc(*b2.free((kind, "sc", h)))
                else:
                    V.scalar_tensor_tensor(s, ps[:, 0:3 * P], 64 ** -0.5, BS[:, :], ALU.mult, ALU.add)\
                        .then_inc(*b2.free((kind, "sc", h)))
                V.drain()
                c = 32 + 8 * (h % 2)
                V.tensor_reduce(small[:, c:c + 1], s[:, 0:P], AXX, ALU.max, negate=True)
                V.tensor_reduce(small[:, c + 1:c + 2], s[:, P:3 * P], AXX, ALU.max, negate=True)
                fence(s2["sc"].done((kind, h)))

            def attention_combined(kind, h):
                dve.wait_ge(*s2["expd"].upto((kind, h)))
                c = 32 + 8 * (h % 2)
                V.reciprocal(small[:, c + 4:c + 6], small[:, c + 2:c + 4])
                V.drain()
                if h >= 2:
                    dve.wait_ge(*b2.full((kind, "t", h - 2)))
                for i, cols in enumerate((slice(0, P), slice(P, 3 * P))):
                    V.tensor_scalar(W2[:, h % 2, cols], SC2[:, h % 2, cols], small[:, c + 4 + i:c + 5 + i], None, ALU.mult)
                fence(s2["w"].done((kind, h)))

            def merge_two(n, j):
                dve.wait_ge(*s2["sigm"].upto((n, j)))
                dve.wait_ge(*b2.full(("mB", n, j)))
                first = n == MERGE2[0]
                dst = Y2[:, j, :] if first else TP2[:, 0, 0:T2]
                V.tensor_tensor(dst, SGM[:, j % 2, :], b2.of(("mB", n, j))[:, 0:T2], ALU.mult).then_inc(*b2.free(("mB", n, j)))
                V.drain()
                if not first:
                    V.tensor_tensor(Y2[:, j, :], Y2[:, j, :], TP2[:, 0, 0:T2], ALU.add)
                fence(s2["y"].done((n, j)))
                if n == MERGE2[-1]:
                    split(Y2[:, j, :], Y2S[0][:, j, :], Y2S[1][:, j, :]).then_inc(*s2["yb"].done(j))

            def attention_output(kind, p, dst):
                dve.wait_ge(*b2.full((kind, "o", p)))
                o = b2.of((kind, "o", p))[:, 0:T2]
                split(o, dst[0][:, p, :], dst[1][:, p, :]).then_inc(*b2.free((kind, "o", p)))
                fence(s2["os"].done((kind, p)))

            def best_keys(i):
                kn = (i + 1) * P
                row = IS[:, i * P:i * P + kn]
                for _ in range(TOPK // 8):
                    V.max(TOP[:, :], row)
                    V.drain()
                    V.match_replace(row, TOP[:, :], row, -3e38)
                    V.drain()
                V.tensor_scalar(row, row, -2e38, NEG, ALU.is_gt, ALU.mult)
                V.drain()
                V.tensor_tensor(BS[:, i * P:i * P + kn], row, causal[:, (2 - i) * P:(2 - i) * P + kn], ALU.add)
                V.drain()

            with dve.Fori(0, DEPTH) as layer:
                V.tensor_copy(cur[:, 0:NPAR2], par2_sb[:, bass.ds(layer * NPAR2, NPAR2)])
                V.memset(KR[0:MLA_NOPE, :], 0.0)
                fence((layer_begin, 1))
                norm(s2, "ss_att", X2, lambda k: parb("gatt", k), (H2, L2), T2, TP2, lambda k: ("att", k))
                dve.wait_ge(*s2["rs"].upto("ss_q"))
                dve.wait_ge(*s2["evac"].upto("cq1"))
                for i in range(2):
                    V.scalar_tensor_tensor(CQ[:, i, :], CQ[:, i, :], parb("gq", i), RS[:, 0:T2], ALU.mult, ALU.mult)
                V.drain()
                split(CQ[:, :, :], CQS[0][:, :, :], CQS[1][:, :, :])
                fence(s2["cqn"].done())
                dve.wait_ge(*s2["rs"].upto("ss_kv"))
                V.scalar_tensor_tensor(CKV[:, :], CKV[:, :], parb("gkv"), RS[:, 0:T2], ALU.mult, ALU.mult)
                V.drain()
                split(CKV[:, :], CKS[0], CKS[1])
                fence(s2["ckn"].done())
                for i in range(2):
                    dve.wait_ge(*b2.full(f"cx{i}"))
                    dve.wait_ge(*s2["evac"].upto(f"cc{i}"))
                    V.tensor_tensor(SI[:, i, :], SI[:, i, :], b2.of(f"cx{i}")[:, 0:T2], ALU.mult).then_inc(*b2.free(f"cx{i}"))
                    V.drain()
                    V.tensor_scalar(OC[:, i, :], SI[:, i, :], parb("cw", 4 + i), None, ALU.mult)
                    V.drain()
                    V.scalar_tensor_tensor(OC[:, i, 1:T2], SI[:, i, 0:T2 - 1], parb("cw", 2 + i), OC[:, i, 1:T2], ALU.mult, ALU.add)
                    V.drain()
                    V.scalar_tensor_tensor(OC[:, i, 2:T2], SI[:, i, 0:T2 - 2], parb("cw", i), OC[:, i, 2:T2], ALU.mult, ALU.add)
                    V.drain()
                    V.tensor_tensor(OC[:, i, :], OC[:, i, :], SB[:, i, :], ALU.mult)
                    V.drain()
                    split(OC[:, i, :], OCS[0][:, i, :], OCS[1][:, i, :])
                fence(s2["oc"].done())
                cM, sM = cosM[MLA_NOPE:MLA_QK, :], sinM[MLA_NOPE:MLA_QK, :]
                dve.wait_ge(*s2["evac"].upto("kr"))
                r = slice(MLA_NOPE, MLA_QK)
                V.tensor_tensor(TP2[r, 0, 0:T2], KR[r, :], cM, ALU.mult)
                dve.wait_ge(*b2.full("kturn"))
                V.tensor_tensor(TP2[r, 1, 0:T2], b2.of("kturn")[r, 0:T2], sM, ALU.mult).then_inc(*b2.free("kturn"))
                V.drain()
                for h in range(MLA_HEADS):
                    V.tensor_tensor(KM[r, h, :], TP2[r, 0, 0:T2], TP2[r, 1, 0:T2], ALU.add)
                V.drain()
                for p in range(2):
                    dve.wait_ge(*b2.full(("qturn", p)))
                    ps = b2.of(("qturn", p))
                    for i in range(2):
                        q = QM[r, 2 * p + i, :]
                        V.tensor_tensor(TP2[r, i, 0:T2], q, cM, ALU.mult)
                        ins = V.tensor_tensor(TP2[r, i, T2:2 * T2], ps[r, i * T2:(i + 1) * T2], sM, ALU.mult)
                        if i:
                            ins.then_inc(*b2.free(("qturn", p)))
                        V.drain()
                        V.tensor_tensor(q, TP2[r, i, 0:T2], TP2[r, i, T2:2 * T2], ALU.add)
                    V.drain()
                dve.wait_ge(*s2["evac"].upto(("ku", 3)))
                fence(s2["km"].done())
                def gla_gate(i):
                    dve.wait_ge(*s2["sg"].upto(i))
                    V.tensor_tensor(GG[:, i, :], SGM[:, i, :], b2.of(f"gr{i}")[:, 0:T2], ALU.mult).then_inc(*b2.free(f"gr{i}"))

                for i in range(2):
                    kn = (i + 1) * P
                    dst = IS[:, i * P:i * P + kn]
                    for c in range(4):
                        seq = 4 * i + c
                        dve.wait_ge(*s2["relu"].upto(seq))
                        for g in range(2):
                            before = causal[:, (2 - i) * P:(2 - i) * P + kn] if c + g == 0 else dst
                            head = c + 4 * g
                            V.scalar_tensor_tensor(dst, REL[:, seq % 2, g * kn:(g + 1) * kn], IW[:, i, head:head + 1], before,
                                                   ALU.mult, ALU.add)
                            V.drain()
                        V.drain().then_inc(*s2["used"].done(seq))
                attention_masked("m", 0)
                best_keys(0)
                attention_combined("m", 0)
                best_keys(1)
                dve.wait_ge(*s2["evac"].upto("glr"))
                split(GL[:, :], GLS[0], GLS[1])
                fence(s2["gls"].done())
                gla_gate(0)
                dve.wait_ge(*b2.full("gl"))
                V.tensor_scalar(GC[:, :], b2.of("gl")[:, 0:T2], parb("bg"), None, ALU.add).then_inc(*b2.free("gl"))
                gla_gate(1)
                fence(s2["gated"].done())
                V.tensor_scalar(GE[:, :], GC[:, :], 0.0, None, ALU.max)
                V.drain()
                V.scalar_tensor_tensor(GE[:, :], GC[:, :], 0.0, GE[:, :], ALU.min, ALU.subtract)
                fence(s2["gz"].done())
                for h in range(MLA_HEADS):
                    if h + 1 < MLA_HEADS:
                        attention_masked("m", h + 1)
                    merge_two(1, 2 * h)
                    if h + 1 < MLA_HEADS:
                        attention_combined("m", h + 1)
                    merge_two(1, 2 * h + 1)
                    if h % 2:
                        attention_output("m", h // 2, OMS)
                    if h == 0:
                        V.tensor_scalar(GC[:, :], GC[:, :], 0.0, None, ALU.min)
                        V.drain()
                        dve.wait_ge(*s2["gez"].upto())
                        V.tensor_tensor(GC[:, :], GC[:, :], GE[:, :], ALU.subtract)
                        V.drain()
                        V.tensor_scalar(GC[:, :], GC[:, :], 1.0 / 16.0, None, ALU.mult)
                        V.drain()
                        V.tensor_tensor_scan(GC[:, :], restart[:, 0:T2], GC[:, :], 0.0, ALU.mult, ALU.add)
                        V.drain()
                        level_differences(GC[:, :], Z2, LV, T2, None)
                        V.tensor_scalar(Z2[:, 3, 0:P], GC[:, 0:P], GC[:, P - 1:P], -1.0, ALU.subtract, ALU.mult)
                        V.tensor_copy(Z2[:, 3, P:T2], GC[:, P:T2])
                        fence(s2["zdiff"].done())
                    if h == 1:
                        dve.wait_ge(*s2["zexp"].upto())
                        dve.wait_ge(*s2["evac"].upto("gk"))
                        level_factors(Z2, LV, T2, GQ, GK)
                        V.tensor_tensor(Z2[:, 3, 0:P], Z2[:, 3, 0:P], GK[:, 0:P], ALU.mult)
                        V.tensor_tensor(Z2[:, 3, P:T2], Z2[:, 3, P:T2], GQ[:, P:T2], ALU.mult)
                        fence(s2["z"].done())
                for g in range(GLA_HEADS):
                    dve.wait_ge(*b2.full(("m", "o", 1) if g < 2 else ("g", "o", g - 2)))
                    for t, cols in ((0, slice(0, P)), (1, slice(T2, T2 + P))):
                        for gg in range(2):
                            dve.wait_ge(*b2.full(("lv", g, t, gg)))
                            V.tensor_tensor(LT2[:, 4 * gg:4 * gg + 4, :],
                                            b2.of(("lv", g, t, gg)).rearrange("p (a b) -> p a b", b=P),
                                            lvl[:, 4 * gg:4 * gg + 4, :], ALU.mult).then_inc(*b2.free(("lv", g, t, gg)))
                        V.drain()
                        V.tensor_reduce(SS[:, g % 2, cols], LT2[:, :, :].rearrange("p a b -> p b a"), AXX, ALU.add)
                        V.drain()
                    dve.wait_ge(*b2.full(("cross", g)))
                    V.tensor_copy(SS[:, g % 2, P:T2], b2.of(("cross", g))[:, 0:P]).then_inc(*b2.free(("cross", g)))
                    fence(s2["att"].done(g))
                    if g == GLA_HEADS - 1:
                        attention_masked("s", 0)
                    merge_two(0, 2 * g)
                    merge_two(0, 2 * g + 1)
                    if g % 2:
                        p = g // 2
                        dve.wait_ge(*s2["rs"].upto(("ssg", p)))
                        V.scalar_tensor_tensor(TP2[:, 1, 0:T2], GO[:, p, :], parb("ggla"), RS[:, 0:T2], ALU.mult, ALU.mult)
                        V.drain()
                        V.tensor_tensor(GG[:, p, :], GG[:, p, :], TP2[:, 1, 0:T2], ALU.mult)
                        V.drain()
                        split(GG[:, p, :], GGS[0][:, p, :], GGS[1][:, p, :])
                        fence(s2["normed"].done(p))
                attention_combined("s", 0)
                for h in range(DSA_HEADS):
                    if h + 1 < DSA_HEADS:
                        attention_masked("s", h + 1)
                    merge_two(3, 2 * h)
                    if h + 1 < DSA_HEADS:
                        attention_combined("s", h + 1)
                    merge_two(3, 2 * h + 1)
                    if h % 2:
                        attention_output("s", h // 2, OSS)
                for j in range(KT):
                    merge_two(2, j)
                for j in range(KT):
                    add_to_x(b2, s2, X2, ("wo", j), j, T2)
                norm(s2, "ss_ffn", X2, lambda k: parb("gffn", k), (H2, L2), T2, TP2, lambda k: ("ffn", k))
                for j in range(FT):
                    dve.wait_ge(*s2["sigf"].upto(j))
                    V.tensor_tensor(TP2[:, 0, 0:T2], SGM[:, j % 2, :], b2.of(("ff", j, 0))[:, 0:T2], ALU.mult)\
                        .then_inc(*b2.free(("ff", j, 0)))
                    V.drain()
                    dve.wait_ge(*b2.full(("ff", j, 1)))
                    V.tensor_tensor(TP2[:, 1, 0:T2], TP2[:, 0, 0:T2], b2.of(("ff", j, 1))[:, 0:T2], ALU.mult)\
                        .then_inc(*b2.free(("ff", j, 1)))
                    V.drain()
                    split(TP2[:, 1, 0:T2], FF2[0][:, j, :], FF2[1][:, j, :])
                    fence(s2["ff"].done(j))
                for j in range(KT):
                    add_to_x(b2, s2, X2, ("down", j), j, T2)
                dve.wait_ge(layer_end, 2 * layer + 2 * DEPTH + 2)
                dve.sem_inc(dve_in)
                for x in list(s2.values()):
                    dve.sem_clear(x.sem)
                for x in bank_full + bank_free:
                    dve.sem_clear(x)
            fence((layer_begin, 1))
            dve.wait_ge(*se["rs"].upto("ss"))
            for k in range(KT):
                V.scalar_tensor_tensor(OUT2[:, k, :], X2[:, k, :], fin_sb[:, KT + k:KT + k + 1], RS[:, 0:T2], ALU.mult, ALU.mult)
            fence(se["x"].done())

        @block.gpsimd
        def _(pool):
            with pool.Fori(0, DEPTH * (SLABS1 + SLABS2) // RING) as r:
                for slot in range(RING):
                    at = slice(slot * SLAB * P, (slot + 1) * SLAB * P)
                    pool.wait_ge(slab_hi[slot], r + 1)
                    nc.gpsimd.tensor_tensor(ring_lo[:, at], ring[:, at], ring_hi[:, at].bitcast(F32), ALU.subtract)\
                        .then_inc(slab_lo[slot], 1)
                    nc.gpsimd.drain().then_inc(slab_free[slot], 1)

        @block.sync
        def _(sp):
            sp.dma_start(x_sb[:, :], x_meta).then_inc(inputs_in, 16)
            sp.dma_start(cst[:, :], consts).then_inc(inputs_in, 16)
            sp.dma_start(par1_sb[:, :].rearrange("p (l n) -> p l n", n=NPAR1)[:, :, 0:NPAR1_IN], par1).then_inc(inputs_in, 16)
            sp.dma_start(lb_sb, lb).then_inc(inputs_in, 16)
            sp.dma_start(lam_sb, lam.to_broadcast([P, DEPTH * 256])).then_inc(inputs_in, 16)
            sp.dma_start(fin_sb[:, 0:KT], final1).then_inc(inputs_in, 16)
            sp.dma_start(fin_sb[:, KT:2 * KT], final2).then_inc(inputs_in, 16)
            sp.dma_start(par2_sb[:, :], par2).then_inc(inputs_in, 16)
            sp.dma_start(pos_sb[:, :], positions.to_broadcast([P, T2])).then_inc(inputs_in, 16)
            for slot in range(RING):
                sp.sem_inc(slab_free[slot])
            for w, slabs, rounds in ((w1, SLABS1, 0), (w2, SLABS2, DEPTH * SLABS1 // RING)):
                with sp.Fori(0, DEPTH * slabs // RING) as r:
                    for slot in range(RING):
                        sp.wait_ge(slab_free[slot], r + (rounds + 1))
                        sp.dma_start(ring[:, slot * SLAB * P:(slot + 1) * SLAB * P],
                                     w[bass.ds(r * RING + slot, 1), :, :].rearrange("a p n -> p (a n)"))\
                            .then_inc(slab_loaded[slot], 16)
            sp.wait_ge(*se["x"].upto())
            sp.dma_start(out, x_sb[:, 0:KT * T2]).then_inc(out_written, 16)
            sp.wait_ge(out_written, 16)


def feature_rows(a):
    a = a.reshape(a.shape[:-1] + (a.shape[-1] // P, P))
    return np.ascontiguousarray(np.moveaxis(a, -1, 0))


def packed(blocks, slabs):
    a = np.zeros((slabs * SLAB, P, P), np.float32)
    for i, b in enumerate(blocks):
        a[i] = b
    return a.reshape(slabs, SLAB, P, P).transpose(0, 2, 1, 3).reshape(slabs, P, SLAB * P)


def tile_blocks(w, column, rows=None):
    return [w[k * P:(k + 1) * P, column:column + P] for k in range(w.shape[0] // P)]


def weights1(w_in, w_branch, w_out, w_ffn_in, w_ffn_out):
    layers = []
    for l in range(DEPTH):
        b = []
        for kind, h in TILES_HG + TILES_FILL + TILES_RG:
            b += tile_blocks(w_in[l], IN1[kind] + h * P)
        for branch in MERGE1:
            for j in range(KT):
                if branch != 2:
                    b += tile_blocks(w_in[l], IN1["mg"] + branch * D_MODEL + j * P)
                b += tile_blocks(w_branch[l, branch], j * P)
                if branch == 0:
                    b += tile_blocks(w_in[l], IN1["mg"] + 2 * D_MODEL + j * P)
        for j in range(KT):
            b += tile_blocks(w_out[l], j * P)
        for j in range(FT):
            b += tile_blocks(w_ffn_in[l], j * P) + tile_blocks(w_ffn_in[l], D_FF + j * P)
        for j in range(KT):
            b += tile_blocks(w_ffn_out[l], j * P)
        layers.append(packed(b, SLABS1))
    return np.concatenate(layers)


def weights2(w_in, q_up, kv_up, gate_up, w_branch, w_out, w_gate, w_up, w_down):
    layers = []
    for l in range(DEPTH):
        wide = np.concatenate([w_in[l], np.zeros((D_MODEL, P), np.float32)], 1)

        def columns(name, n=1, back=0):
            return [x for i in range(n) for x in tile_blocks(wide, IN2[name] - back + i * P)]

        b = columns("cq", 2) + columns("ckv") + columns("krope", 1, MLA_NOPE) + columns("cb", 2) + columns("cc", 2)
        b += columns("cx", 2) + columns("dq", 2)
        heads = np.zeros((2 * P, MLA_HEADS, P), np.float32)
        heads[:, :, 0:MLA_QK] = q_up[l].reshape(2 * P, MLA_HEADS, MLA_QK)
        for h in range(MLA_HEADS):
            b += [heads[0:P, h], heads[P:2 * P, h]]
        for h in range(MLA_HEADS):
            b.append(kv_up[l][:, h * P:(h + 1) * P])
        values = kv_up[l].reshape(P, MLA_HEADS, 2, 64)[:, :, 1].reshape(P, 2, P)
        b += [values[:, 0], values[:, 1]]
        b += columns("dk") + columns("iq", 2) + columns("ik")
        both = np.zeros((D_MODEL, P), np.float32)
        both[:, 0:64] = w_in[l][:, IN2["dv"]:IN2["dv"] + 64]
        both[:, 64:64 + IDX_HEADS] = w_in[l][:, IN2["iw"]:IN2["iw"] + IDX_HEADS]
        b += tile_blocks(both, 0) + columns("gq") + columns("gk")
        for k0, k1 in zip(columns("gv"), tile_blocks(wide, IN2["gv"] + P)):
            b += [k0, k1]
        up = np.zeros((P, P), np.float32)
        up[0:16] = gate_up[l]
        b += columns("glr") + columns("gr") + [up] + tile_blocks(wide, IN2["gr"] + P)
        assert len(b) == 207
        for branch in MERGE2:
            for j in range(KT):
                b += tile_blocks(w_in[l], IN2["mg"] + branch * D_MODEL + j * P) + tile_blocks(w_branch[l, branch], j * P)
        for j in range(KT):
            b += tile_blocks(w_out[l], j * P)
        for j in range(FT):
            b += tile_blocks(w_gate[l], j * P) + tile_blocks(w_up[l], j * P)
        for j in range(KT):
            b += tile_blocks(w_down[l], j * P)
        layers.append(packed(b, SLABS2))
    return np.concatenate(layers)


def kernel(x, meta, norm_mix_g, w_in, w_branch, w_out, hg_lb, da_lambda, da_subln_g, norm_ffn_g, w_ffn_in, ffn_conv_w,
           ffn_conv_b, w_ffn_out, norm_final_g, positions_2, attn_norm_g_2, w_in_2, mla_q_norm_g_2, mla_w_q_up_2,
           mla_kv_norm_g_2, mla_w_kv_up_2, conv_w_2, gla_w_gate_up_2, gla_b_gate_2, gla_norm_g_2, w_branch_2, w_out_2,
           ffn_norm_g_2, w_ffn_gate_2, w_ffn_up_2, w_ffn_down_2, final_norm_g_2):
    import concourse.bacc as bacc
    from concourse.bass_utils import run_bass_kernel_spmd

    g = lambda a: np.asarray(a)
    x, meta = g(x), g(meta)
    arrays = {
        "x_meta": feature_rows(np.concatenate([meta, x[0]])).transpose(0, 2, 1).reshape(P, KT * T1),
        "w1": weights1(g(w_in), g(w_branch), g(w_out), g(w_ffn_in), g(w_ffn_out)),
        "par1": np.concatenate([feature_rows(g(a)).reshape(P, DEPTH, -1) for a in
                                (norm_mix_g, norm_ffn_g, ffn_conv_w, ffn_conv_b, da_subln_g)], 2),
        "lb": feature_rows(g(hg_lb)).reshape(P, DEPTH * KT),
        "lam": g(da_lambda).reshape(1, DEPTH * 256),
        "final1": feature_rows(g(norm_final_g)),
        "w2": weights2(g(w_in_2), g(mla_w_q_up_2), g(mla_w_kv_up_2), g(gla_w_gate_up_2), g(w_branch_2), g(w_out_2),
                       g(w_ffn_gate_2), g(w_ffn_up_2), g(w_ffn_down_2)),
        "par2": np.concatenate([feature_rows(g(a)).reshape(P, DEPTH, -1) for a in
                                (attn_norm_g_2, ffn_norm_g_2, mla_q_norm_g_2, mla_kv_norm_g_2, conv_w_2, gla_b_gate_2)]
                               + [feature_rows(np.concatenate([g(gla_norm_g_2)] * 2, -1)).reshape(P, DEPTH, -1)],
                               2).reshape(P, DEPTH * NPAR2),
        "positions": g(positions_2),
        "final2": feature_rows(g(final_norm_g_2)),
        "consts": constants(),
    }
    arrays = {n: np.ascontiguousarray(a) for n, a in arrays.items()}
    known = {}
    for _ in range(2):
        nc = bacc.Bacc("TRN2", target_bir_lowering=False, num_devices=1)
        args = [nc.dram_tensor(n, a.shape, mybir.dt.from_np(a.dtype), kind="ExternalInput").ap() for n, a in arrays.items()]
        out = nc.dram_tensor("out", (P, KT * T2), F32, kind="ExternalOutput").ap()
        program(nc, *args, out, known)
    r = run_bass_kernel_spmd(nc, [arrays], core_ids=[0])
    return r.results[0]["out"].reshape(P, KT, T2).transpose(2, 1, 0).reshape(1, T2, D_MODEL)
```
